# Optimizing a Trainium2 kernel written in Bass

```python
import jax
import jax.numpy as jnp
from jax import lax
import numpy as np
import math
import jax, jax.numpy as jnp

D_MODEL = 1024
BATCH = 1
SEQ = 256
DEPTH = 2

GRID_W = 64
CTX_LEN = 256
CHUNK = 64
GLA_HEADS = 4
GLA_DK = 64
GLA_DV = 128
GLA_GATE_RANK = 16
GLA_GATE_TAU = 16.0
ATT_Q_HEADS = 8
ATT_KV_HEADS = 2
ATT_HEAD_DIM = 64
ATT_GROUP = ATT_Q_HEADS // ATT_KV_HEADS
ROPE_AXIS_DIM = ATT_HEAD_DIM // 2
ROPE_THETA = 10000.0
Q_BLOCK = 128
HGRN_HEADS = 8
HGRN_DF = 128
HGRN_DV = D_MODEL // HGRN_HEADS
D_FF = ((8 * D_MODEL + 3 * 256 - 1) // (3 * 256)) * 256

EVEN_SIZES = (GLA_HEADS * GLA_DK, GLA_HEADS * GLA_DK, GLA_HEADS * GLA_DV, GLA_HEADS * GLA_DV, 2 * GLA_GATE_RANK,
              ATT_Q_HEADS * ATT_HEAD_DIM, ATT_KV_HEADS * ATT_HEAD_DIM, ATT_KV_HEADS * ATT_HEAD_DIM)
ODD_SIZES = (HGRN_HEADS * HGRN_DF,) * 3 + (HGRN_HEADS * HGRN_DV,) * 2
EVEN_MIX = GLA_HEADS * GLA_DV + ATT_Q_HEADS * ATT_HEAD_DIM
ODD_MIX = HGRN_HEADS * HGRN_DV


def _rms(x, gain, eps=1e-6):
    xf = x.astype(jnp.float32)
    y = xf * lax.rsqrt(jnp.mean(xf * xf, axis=-1, keepdims=True) + eps)
    return (y * gain.astype(jnp.float32)).astype(x.dtype)

def _modulate(h, shift, scale):
    return h * (1 + scale) + shift

def _split(a, sizes):
    return jnp.split(a, np.cumsum(sizes)[:-1].tolist(), axis=-1)

def _heads(a, n_heads):
    B, N, _ = a.shape
    return a.reshape(B, N, n_heads, -1).transpose(0, 2, 1, 3)

def _merge(a):
    B, H, N, d = a.shape
    return a.transpose(0, 2, 1, 3).reshape(B, N, H * d)

def _gated_readout(o, og, gain):
    return _merge(_rms(o, gain) * jax.nn.silu(og))

def _swiglu(h, w_gate, w_up, w_down):
    return (jax.nn.silu(h @ w_gate) * (h @ w_up)) @ w_down

def _chunk_gla(q, k, v, g, s0):
    B, H, T, K = q.shape
    V = v.shape[-1]
    n = T // CHUNK

    def blocks(a):
        return jnp.moveaxis(a.astype(jnp.float32).reshape(B, H, n, CHUNK, a.shape[-1]), 2, 0)

    tri = jnp.tril(jnp.ones((CHUNK, CHUNK), dtype=bool))[:, :, None]

    def step(s, blk):
        qc, kc, vc, gc = blk
        G = jnp.cumsum(gc, axis=2)
        decay = jnp.exp(jnp.where(tri, G[:, :, :, None, :] - G[:, :, None, :, :], -jnp.inf))
        scores = jnp.einsum('bhik,bhjk,bhijk->bhij', qc, kc, decay)
        o = jnp.einsum('bhij,bhjv->bhiv', scores, vc) + jnp.einsum('bhik,bhkv->bhiv', qc * jnp.exp(G), s)
        G_last = G[:, :, -1:, :]
        s = s * jnp.exp(G_last)[:, :, 0, :, None] + jnp.einsum('bhjk,bhjv->bhkv', kc * jnp.exp(G_last - G), vc)
        return s, o

    s, o = lax.scan(step, s0, (blocks(q), blocks(k), blocks(v), blocks(g)))
    return jnp.moveaxis(o, 0, 2).reshape(B, H, T, V).astype(v.dtype), s

def _directional_scan(q, k, v, g, n_ctx, reverse):
    def seg(a, sl):
        a = a[:, :, sl]
        return jnp.flip(a, 2) if reverse else a
    c_sl, t_sl = slice(0, n_ctx), slice(n_ctx, None)
    B, H, _, K = q.shape
    s0 = jnp.zeros((B, H, K, v.shape[-1]), jnp.float32)
    o_ctx, s_ctx = _chunk_gla(seg(q, c_sl), seg(k, c_sl), seg(v, c_sl), seg(g, c_sl), s0)
    o_lat, _ = _chunk_gla(seg(q, t_sl), seg(k, t_sl), seg(v, t_sl), seg(g, t_sl), s_ctx)
    if reverse:
        o_ctx, o_lat = jnp.flip(o_ctx, 2), jnp.flip(o_lat, 2)
    return o_ctx, o_lat

def _axial_rope_tables(n_tokens):
    rows_n = n_tokens // GRID_W
    row = jnp.repeat(jnp.arange(rows_n), GRID_W).astype(jnp.float32)
    col = jnp.tile(jnp.arange(GRID_W), rows_n).astype(jnp.float32)
    inv = ROPE_THETA ** (-jnp.arange(0, ROPE_AXIS_DIM, 2, dtype=jnp.float32) / ROPE_AXIS_DIM)
    ang = jnp.concatenate([row[:, None] * inv, col[:, None] * inv], axis=-1)
    return jnp.cos(ang), jnp.sin(ang)

def _rope(x, cos, sin):
    xf = x.astype(jnp.float32).reshape(x.shape[:-1] + (-1, 2))
    x0, x1 = xf[..., 0], xf[..., 1]
    out = jnp.stack([x0 * cos - x1 * sin, x0 * sin + x1 * cos], axis=-1)
    return out.reshape(x.shape).astype(x.dtype)

def _softmax_attend(q, k, v):
    s = jnp.einsum('bhgqd,bhkd->bhgqk', q, k, preferred_element_type=jnp.float32) * (ATT_HEAD_DIM ** -0.5)
    p = jax.nn.softmax(s, axis=-1).astype(v.dtype)
    return jnp.einsum('bhgqk,bhkd->bhgqd', p, v)

def _even_mixer(h_ctx, h_lat, w_in, gla_w_gate, gla_b_gate, gla_out_norm, att_q_norm, att_k_norm, cos, sin, ctx_out):
    B, n_ctx, _ = h_ctx.shape
    h = jnp.concatenate([h_ctx, h_lat], axis=1)
    N = h.shape[1]
    T = N - n_ctx
    gq, gk, gv, gog, gz, aq, ak, av = _split(h @ w_in, EVEN_SIZES)

    q = _heads(gq, GLA_HEADS) * (GLA_DK ** -0.5)
    k = _heads(gk, GLA_HEADS)
    v = _heads(gv, GLA_HEADS)
    og = _heads(gog, GLA_HEADS)
    dirs = []
    for d, z in enumerate(jnp.split(gz, 2, axis=-1)):
        logit = (z @ gla_w_gate[d] + gla_b_gate[d]).astype(jnp.float32)
        g = _heads(jax.nn.log_sigmoid(logit) / GLA_GATE_TAU, GLA_HEADS)
        dirs.append(_directional_scan(q, k, v, g, n_ctx, reverse=(d == 1)))
    a_lat = _gated_readout(dirs[0][1] + dirs[1][1], og[:, :, n_ctx:], gla_out_norm)

    qa = _rms(aq.reshape(B, N, ATT_KV_HEADS, ATT_GROUP, ATT_HEAD_DIM), att_q_norm).transpose(0, 2, 3, 1, 4)
    ka = _rms(ak.reshape(B, N, ATT_KV_HEADS, ATT_HEAD_DIM), att_k_norm).transpose(0, 2, 1, 3)
    va = av.reshape(B, N, ATT_KV_HEADS, ATT_HEAD_DIM).transpose(0, 2, 1, 3)
    q_lat = _rope(qa[:, :, :, n_ctx:], cos, sin)
    k_all = jnp.concatenate([ka[:, :, :n_ctx], _rope(ka[:, :, n_ctx:], cos, sin)], axis=2)
    q_blocks = jnp.moveaxis(q_lat.reshape(B, ATT_KV_HEADS, ATT_GROUP, T // Q_BLOCK, Q_BLOCK, ATT_HEAD_DIM), 3, 0)
    o_blocks = lax.map(lambda qb: _softmax_attend(qb, k_all, va), q_blocks)
    b_lat = jnp.moveaxis(o_blocks, 0, 3).reshape(B, ATT_KV_HEADS, ATT_GROUP, T, ATT_HEAD_DIM)
    b_lat = b_lat.transpose(0, 3, 1, 2, 4).reshape(B, T, ATT_Q_HEADS * ATT_HEAD_DIM)
    o_lat = jnp.concatenate([a_lat, b_lat], axis=-1)
    if not ctx_out:
        return None, o_lat
    a_ctx = _gated_readout(dirs[0][0] + dirs[1][0], og[:, :, :n_ctx], gla_out_norm)
    b_ctx = _softmax_attend(qa[:, :, :, :n_ctx], ka[:, :, :n_ctx], va[:, :, :n_ctx])
    b_ctx = b_ctx.transpose(0, 3, 1, 2, 4).reshape(B, n_ctx, ATT_Q_HEADS * ATT_HEAD_DIM)
    return jnp.concatenate([a_ctx, b_ctx], axis=-1), o_lat

def _odd_mixer(h_ctx, h_lat, w_in, lower_bounds, layer, out_norm, ctx_out):
    n_ctx = h_ctx.shape[1]
    h = jnp.concatenate([h_ctx, h_lat], axis=1)
    fq, f_fwd, f_bwd, fi, fog = _split(h @ w_in, ODD_SIZES)
    q = _heads(jax.nn.silu(fq), HGRN_HEADS)
    i = _heads(fi, HGRN_HEADS)
    og = _heads(fog, HGRN_HEADS)
    lbs = jnp.cumsum(jax.nn.softmax(lower_bounds.astype(jnp.float32), axis=1), axis=1)
    lb = (lbs[:, layer] - lbs[:, 0]).reshape(2, HGRN_HEADS, 1, HGRN_DF)
    dirs = []
    for d, f in enumerate((f_fwd, f_bwd)):
        log_f = jnp.logaddexp(jnp.log(lb[d]), jnp.log1p(-lb[d]) + jax.nn.log_sigmoid(_heads(f, HGRN_HEADS).astype(jnp.float32)))
        k = -jnp.expm1(log_f)
        dirs.append(_directional_scan(q, k, i, log_f, n_ctx, reverse=(d == 1)))
    o_lat = _gated_readout(dirs[0][1] + dirs[1][1], og[:, :, n_ctx:], out_norm)
    if not ctx_out:
        return None, o_lat
    return _gated_readout(dirs[0][0] + dirs[1][0], og[:, :, :n_ctx], out_norm), o_lat

def first_inputs(seed: int = 0) -> dict:
    key = jax.random.key(seed)
    ks = iter(jax.random.split(key, 32))
    n_even, n_odd = (DEPTH + 1) // 2, DEPTH // 2
    D = D_MODEL

    def nrm(shape, scale):
        return scale * jax.random.normal(next(ks), shape, jnp.float32)

    def gain(shape):
        return 1.0 + nrm(shape, 0.02)

    return {
        'x': nrm((BATCH, SEQ, D), 1.0),
        'c': nrm((BATCH, D), 1.0),
        'ctx': nrm((BATCH, CTX_LEN, D), 1.0),
        'c_ctx': nrm((D,), 1.0),
        'mod_w': nrm((DEPTH, D, 6 * D), D ** -0.5),
        'mod_b': nrm((DEPTH, 6 * D), 0.02),
        'norm_pre_mix': gain((DEPTH, D)),
        'norm_post_mix': gain((DEPTH, D)),
        'norm_pre_ffn': gain((DEPTH, D)),
        'norm_post_ffn': gain((DEPTH, D)),
        'even_w_in': nrm((n_even, D, sum(EVEN_SIZES)), D ** -0.5),
        'gla_w_gate': nrm((n_even, 2, GLA_GATE_RANK, GLA_HEADS * GLA_DK), GLA_GATE_RANK ** -0.5),
        'gla_b_gate': nrm((n_even, 2, GLA_HEADS * GLA_DK), 0.02),
        'gla_out_norm': gain((n_even, GLA_DV)),
        'att_q_norm': gain((n_even, ATT_HEAD_DIM)),
        'att_k_norm': gain((n_even, ATT_HEAD_DIM)),
        'even_w_out': nrm((n_even, EVEN_MIX, D), EVEN_MIX ** -0.5),
        'odd_w_in': nrm((n_odd, D, sum(ODD_SIZES)), D ** -0.5),
        'hgrn_lower_bounds': nrm((2, DEPTH, HGRN_HEADS * HGRN_DF), 0.1),
        'hgrn_out_norm': gain((n_odd, HGRN_DV)),
        'odd_w_out': nrm((n_odd, ODD_MIX, D), ODD_MIX ** -0.5),
        'ffn_w_gate': nrm((DEPTH, D, D_FF), D ** -0.5),
        'ffn_w_up': nrm((DEPTH, D, D_FF), D ** -0.5),
        'ffn_w_down': nrm((DEPTH, D_FF, D), D_FF ** -0.5),
    }

def first_block(x, c, ctx, c_ctx, mod_w, mod_b, norm_pre_mix, norm_post_mix, norm_pre_ffn, norm_post_ffn,
              even_w_in, gla_w_gate, gla_b_gate, gla_out_norm, att_q_norm, att_k_norm, even_w_out,
              odd_w_in, hgrn_lower_bounds, hgrn_out_norm, odd_w_out, ffn_w_gate, ffn_w_up, ffn_w_down):
    cos, sin = _axial_rope_tables(x.shape[1])
    sc = jax.nn.silu(c)
    scc = jax.nn.silu(c_ctx)
    x_ctx, x_lat = ctx, x
    for l in range(DEPTH):
        last = l == DEPTH - 1
        j = l // 2
        m_lat = jnp.split((sc @ mod_w[l] + mod_b[l])[:, None, :], 6, axis=-1)
        m_ctx = jnp.split((scc @ mod_w[l] + mod_b[l])[None, None, :], 6, axis=-1)
        h_ctx = _modulate(_rms(x_ctx, norm_pre_mix[l]), m_ctx[0], m_ctx[1])
        h_lat = _modulate(_rms(x_lat, norm_pre_mix[l]), m_lat[0], m_lat[1])
        if l % 2 == 0:
            o_ctx, o_lat = _even_mixer(h_ctx, h_lat, even_w_in[j], gla_w_gate[j], gla_b_gate[j], gla_out_norm[j],
                                       att_q_norm[j], att_k_norm[j], cos, sin, not last)
            w_out = even_w_out[j]
        else:
            o_ctx, o_lat = _odd_mixer(h_ctx, h_lat, odd_w_in[j], hgrn_lower_bounds, l, hgrn_out_norm[j], not last)
            w_out = odd_w_out[j]
        x_lat = x_lat + m_lat[2] * _rms(o_lat @ w_out, norm_post_mix[l])
        h_lat = _modulate(_rms(x_lat, norm_pre_ffn[l]), m_lat[3], m_lat[4])
        x_lat = x_lat + m_lat[5] * _rms(_swiglu(h_lat, ffn_w_gate[l], ffn_w_up[l], ffn_w_down[l]), norm_post_ffn[l])
        if not last:
            x_ctx = x_ctx + m_ctx[2] * _rms(o_ctx @ w_out, norm_post_mix[l])
            h_ctx = _modulate(_rms(x_ctx, norm_pre_ffn[l]), m_ctx[3], m_ctx[4])
            x_ctx = x_ctx + m_ctx[5] * _rms(_swiglu(h_ctx, ffn_w_gate[l], ffn_w_up[l], ffn_w_down[l]), norm_post_ffn[l])
    return x_lat


N_EVEN = (DEPTH + 1) // 2
N_ODD = DEPTH // 2
EPS = 1e-6
ADA_CHUNKS = 6

H_A = 8
Q_LORA = 256
KV_LORA = 128
NOPE_DIM = 64
ROPE_DIM = 32
QK_DIM = NOPE_DIM + ROPE_DIM
V_DIM = 64
ROPE_BASE = 10000.0

H_R = 8
DK_R = 64
DV_R = 64
RET_CHUNK = 128
RET_W = H_R * DK_R

MLA_IN = Q_LORA + KV_LORA + ROPE_DIM
IN_WIDTH = MLA_IN + 4 * RET_W
MIX_W = H_A * V_DIM + H_R * DV_R

S5_GROUP = 16
S5_GROUPS = D_MODEL // S5_GROUP
S5_STATE = 64
S5_CHUNK = 128
DT_MIN = 1e-3
DT_MAX = 1e-1

D_FF_2 = 4 * D_MODEL


def rmsnorm(x, g):
    xf = x.astype(jnp.float32)
    y = xf * lax.rsqrt(jnp.mean(xf * xf, axis=-1, keepdims=True) + EPS)
    return (y * g.astype(jnp.float32)).astype(x.dtype)

def head_norm(o):
    mu = jnp.mean(o, axis=-1, keepdims=True)
    var = jnp.mean(jnp.square(o - mu), axis=-1, keepdims=True)
    return (o - mu) * lax.rsqrt(var + EPS)

def modulate(h, shift, scale):
    return h * (1 + scale) + shift

def apply_rotary(x, ang):
    half = x.shape[-1] // 2
    cos = jnp.cos(ang)[None, :, None, :].astype(x.dtype)
    sin = jnp.sin(ang)[None, :, None, :].astype(x.dtype)
    x1, x2 = x[..., :half], x[..., half:]
    return jnp.concatenate([x1 * cos - x2 * sin, x1 * sin + x2 * cos], axis=-1)

def axial_angles(n_tok):
    rows = n_tok // GRID_W
    r = jnp.repeat(jnp.arange(rows, dtype=jnp.float32), GRID_W)
    col = jnp.tile(jnp.arange(GRID_W, dtype=jnp.float32), rows)
    nf = ROPE_DIM // 4
    f = ROPE_BASE ** (-jnp.arange(nf, dtype=jnp.float32) / nf)
    return jnp.concatenate([r[:, None] * f, col[:, None] * f], axis=-1)

def retnet_angles(n_tok):
    nf = DK_R // 2
    theta = ROPE_BASE ** (-jnp.arange(nf, dtype=jnp.float32) / nf)
    return jnp.arange(n_tok, dtype=jnp.float32)[:, None] * theta

def squared_relu_mlp(h, w1, w2):
    return jnp.square(jax.nn.relu(h @ w1)) @ w2

def mla_heads(z, q_norm_g, w_uq, kv_norm_g, w_ukv, qn_g, kn_g, ang):
    b, t = z.shape[:2]
    cq = z[..., :Q_LORA]
    ckv = z[..., Q_LORA:Q_LORA + KV_LORA]
    kr = z[..., Q_LORA + KV_LORA:]
    q = (rmsnorm(cq, q_norm_g) @ w_uq).reshape(b, t, H_A, QK_DIM)
    kv = (rmsnorm(ckv, kv_norm_g) @ w_ukv).reshape(b, t, H_A, NOPE_DIM + V_DIM)
    k = jnp.concatenate([kv[..., :NOPE_DIM], jnp.broadcast_to(kr[:, :, None, :], (b, t, H_A, ROPE_DIM))], axis=-1)
    v = kv[..., NOPE_DIM:]
    q = rmsnorm(q, qn_g)
    k = rmsnorm(k, kn_g)
    if ang is not None:
        q = jnp.concatenate([q[..., :NOPE_DIM], apply_rotary(q[..., NOPE_DIM:], ang)], axis=-1)
        k = jnp.concatenate([k[..., :NOPE_DIM], apply_rotary(k[..., NOPE_DIM:], ang)], axis=-1)
    return q, k, v

def attend(q, k, v):
    s = jnp.einsum('bqhd,bkhd->bhqk', q, k).astype(jnp.float32) * (QK_DIM ** -0.5)
    p = jax.nn.softmax(s, axis=-1).astype(v.dtype)
    return jnp.einsum('bhqk,bkhd->bqhd', p, v)

def blocked_attend(q, k, v):
    b, n_tok = q.shape[:2]
    nb = n_tok // Q_BLOCK
    qb = q.reshape(b, nb, Q_BLOCK, H_A, QK_DIM).swapaxes(0, 1)
    o = lax.map(lambda qq: attend(qq, k, v), qb)
    return o.swapaxes(0, 1).reshape(b, n_tok, H_A * V_DIM)

def ret_heads(z, ang):
    b, t = z.shape[:2]
    rq, rk, rv, rg = jnp.split(z, 4, axis=-1)
    rq = rq.reshape(b, t, H_R, DK_R).astype(jnp.float32)
    rk = rk.reshape(b, t, H_R, DK_R).astype(jnp.float32)
    rv = rv.reshape(b, t, H_R, DV_R).astype(jnp.float32)
    if ang is not None:
        rq = apply_rotary(rq, ang)
        rk = apply_rotary(rk, ang)
    return rq, rk * (DK_R ** -0.5), rv, rg

def retention_scan(q, k, v, log_gamma, s0, strict):
    b, t, h, _ = q.shape
    dv = v.shape[-1]
    n = t // RET_CHUNK
    i = jnp.arange(RET_CHUNK, dtype=jnp.float32)
    diff = i[:, None] - i[None, :]
    mask = (diff > 0) if strict else (diff >= 0)
    intra_decay = jnp.where(mask[None], jnp.exp(jnp.where(mask, diff, 0.0)[None] * log_gamma[:, None, None]), 0.0)
    q_decay = jnp.exp((i + 1)[:, None] * log_gamma[None])
    k_decay = jnp.exp((RET_CHUNK - 1 - i)[:, None] * log_gamma[None])
    chunk_decay = jnp.exp(RET_CHUNK * log_gamma)

    def blocks(a):
        return a.reshape(b, n, RET_CHUNK, h, a.shape[-1]).swapaxes(0, 1)

    def step(s, qkv):
        qc, kc, vc = qkv
        scores = jnp.einsum('bihd,bjhd->bhij', qc, kc) * intra_decay
        o = jnp.einsum('bhij,bjhe->bihe', scores, vc) + jnp.einsum('bihd,bhde->bihe', qc, s) * q_decay[None, :, :, None]
        s = s * chunk_decay[None, :, None, None] + jnp.einsum('bjhd,bjhe->bhde', kc * k_decay[None, :, :, None], vc)
        return s, o

    s_final, o = lax.scan(step, s0, (blocks(q), blocks(k), blocks(v)))
    return o.swapaxes(0, 1).reshape(b, t, h, dv), s_final

def ret_out(o, g):
    b, t = o.shape[:2]
    return head_norm(o).reshape(b, t, H_R * DV_R).astype(g.dtype) * jax.nn.silu(g)

def mla_retention_mixer(h_c, h_l, w_in, q_norm_g, w_uq, kv_norm_g, w_ukv, qn_g, kn_g, lg_f_raw, lg_b_raw, w_out, need_ctx):
    b, n_lat = h_l.shape[:2]
    z_c = h_c @ w_in
    z_l = h_l @ w_in
    q_c, k_c, v_c = mla_heads(z_c[..., :MLA_IN], q_norm_g, w_uq, kv_norm_g, w_ukv, qn_g, kn_g, None)
    q_l, k_l, v_l = mla_heads(z_l[..., :MLA_IN], q_norm_g, w_uq, kv_norm_g, w_ukv, qn_g, kn_g, axial_angles(n_lat))
    k_all = jnp.concatenate([k_c, k_l], axis=1)
    v_all = jnp.concatenate([v_c, v_l], axis=1)
    a_l = blocked_attend(q_l, k_all, v_all)
    lg_f = jnp.log1p(-jnp.exp2(lg_f_raw.astype(jnp.float32)))
    lg_b = jnp.log1p(-jnp.exp2(lg_b_raw.astype(jnp.float32)))
    rq_c, rk_c, rv_c, rg_c = ret_heads(z_c[..., MLA_IN:], None)
    rq_l, rk_l, rv_l, rg_l = ret_heads(z_l[..., MLA_IN:], retnet_angles(n_lat))
    zero = jnp.zeros((b, H_R, DK_R, DV_R), jnp.float32)
    o_cf, s_cf = retention_scan(rq_c, rk_c, rv_c, lg_f, zero, False)
    o_cb, s_cb = retention_scan(rq_c[:, ::-1], rk_c[:, ::-1], rv_c[:, ::-1], lg_b, zero, True)
    o_lf, _ = retention_scan(rq_l, rk_l, rv_l, lg_f, s_cf, False)
    o_lb, _ = retention_scan(rq_l[:, ::-1], rk_l[:, ::-1], rv_l[:, ::-1], lg_b, s_cb, True)
    r_l = ret_out(o_lf + o_lb[:, ::-1], rg_l)
    y_l = jnp.concatenate([a_l, r_l.astype(a_l.dtype)], axis=-1) @ w_out
    if need_ctx:
        a_c = attend(q_c, k_c, v_c).reshape(b, h_c.shape[1], H_A * V_DIM)
        r_c = ret_out(o_cf + o_cb[:, ::-1], rg_c)
        y_c = jnp.concatenate([a_c, r_c.astype(a_c.dtype)], axis=-1) @ w_out
    else:
        y_c = None
    return y_c, y_l

def s5_discretize(a_re, a_im, b_re, b_im, c_re, c_im, log_dt):
    f = lambda t: t.astype(jnp.float32)
    a = lax.complex(f(a_re), f(a_im))
    dt = jnp.exp(f(log_dt))[:, None]
    a_bar = jnp.exp(dt * a)
    b_bar = ((a_bar - 1) / a)[..., None] * lax.complex(f(b_re), f(b_im))
    c_mat = lax.complex(f(c_re), f(c_im))
    return a_bar, b_bar, c_mat

def _affine_compose(e1, e2):
    a1, b1 = e1
    a2, b2 = e2
    return a1 * a2, a2 * b1 + b2

def s5_scan(u, a_bar, b_bar, c_mat, x0):
    b, t = u.shape[:2]
    n = t // S5_CHUNK
    ub = u.reshape(b, n, S5_CHUNK, S5_GROUPS, S5_GROUP).swapaxes(0, 1)

    def step(x, u_blk):
        bu = jnp.einsum('btgh,gph->btgp', u_blk.astype(jnp.complex64), b_bar)
        bu = bu.at[:, 0].add(a_bar * x)
        a = jnp.broadcast_to(a_bar, bu.shape)
        _, xs = lax.associative_scan(_affine_compose, (a, bu), axis=1)
        y = jnp.einsum('btgp,ghp->btgh', xs, c_mat).real
        return xs[:, -1], y

    x_final, ys = lax.scan(step, x0, ub)
    return ys.swapaxes(0, 1).reshape(b, t, S5_GROUPS, S5_GROUP), x_final

def s5_out(y, u, d_skip, w_glu, dtype):
    b, t = u.shape[:2]
    y = (y + d_skip.astype(jnp.float32).reshape(S5_GROUPS, S5_GROUP) * u).reshape(b, t, D_MODEL)
    z = jax.nn.gelu(y).astype(dtype) @ w_glu
    za, zb = jnp.split(z, 2, axis=-1)
    return za * jax.nn.sigmoid(zb)

def s5_mixer(h_c, h_l, p_f, p_b, d_skip, w_glu, need_ctx):
    ab_f, bb_f, c_f = s5_discretize(*p_f)
    ab_b, bb_b, c_b = s5_discretize(*p_b)
    b = h_l.shape[0]
    u_c = h_c.astype(jnp.float32).reshape(b, h_c.shape[1], S5_GROUPS, S5_GROUP)
    u_l = h_l.astype(jnp.float32).reshape(b, h_l.shape[1], S5_GROUPS, S5_GROUP)
    x0 = jnp.zeros((b, S5_GROUPS, S5_STATE), jnp.complex64)
    y_cf, x_cf = s5_scan(u_c, ab_f, bb_f, c_f, x0)
    y_cb, x_cb = s5_scan(u_c[:, ::-1], ab_b, bb_b, c_b, x0)
    y_lf, _ = s5_scan(u_l, ab_f, bb_f, c_f, x_cf)
    y_lb, _ = s5_scan(u_l[:, ::-1], ab_b, bb_b, c_b, x_cb)
    out_l = s5_out(y_lf + y_lb[:, ::-1], u_l, d_skip, w_glu, h_l.dtype)
    out_c = s5_out(y_cf + y_cb[:, ::-1], u_c, d_skip, w_glu, h_c.dtype) if need_ctx else None
    return out_c, out_l

def second_inputs(seed: int = 0) -> dict:
    key = jax.random.key(seed)
    ks = iter(jax.random.split(key, 48))
    f32 = jnp.float32

    def nrm(shape, scale=1.0):
        return jax.random.normal(next(ks), shape, f32) * scale

    def gain(shape):
        return 1.0 + nrm(shape, 0.02)

    D = D_MODEL
    G, P, Hg = S5_GROUPS, S5_STATE, S5_GROUP
    n_idx = jnp.arange(P, dtype=f32)
    decay_init = -(5.0 + jnp.arange(H_R, dtype=f32))
    inputs = {
        'x': nrm((BATCH, SEQ, D)),
        'c': nrm((BATCH, D)),
        'ctx': nrm((BATCH, CTX_LEN, D)),
        'c_ctx': nrm((D,)),
        'ada_w': nrm((DEPTH, D, ADA_CHUNKS * D), 0.5 * D ** -0.5),
        'ada_b': nrm((DEPTH, ADA_CHUNKS * D), 0.02),
        'norm1_g': gain((DEPTH, D)),
        'norm2_g': gain((DEPTH, D)),
        'mlp_w1': nrm((DEPTH, D, D_FF_2), D ** -0.5),
        'mlp_w2': nrm((DEPTH, D_FF_2, D), D_FF_2 ** -0.5),
        'w_in': nrm((N_EVEN, D, IN_WIDTH), D ** -0.5),
        'mla_q_norm_g': gain((N_EVEN, Q_LORA)),
        'mla_w_uq': nrm((N_EVEN, Q_LORA, H_A * QK_DIM), Q_LORA ** -0.5),
        'mla_kv_norm_g': gain((N_EVEN, KV_LORA)),
        'mla_w_ukv': nrm((N_EVEN, KV_LORA, H_A * (NOPE_DIM + V_DIM)), KV_LORA ** -0.5),
        'mla_qn_g': gain((N_EVEN, QK_DIM)),
        'mla_kn_g': gain((N_EVEN, QK_DIM)),
        'ret_lg_f': decay_init + nrm((N_EVEN, H_R), 0.1),
        'ret_lg_b': decay_init + nrm((N_EVEN, H_R), 0.1),
        'w_out': nrm((N_EVEN, MIX_W, D), MIX_W ** -0.5),
    }
    for d in ('f', 'b'):
        inputs['s5_a_re_' + d] = -0.5 + nrm((N_ODD, G, P), 0.01)
        inputs['s5_a_im_' + d] = jnp.pi * n_idx + nrm((N_ODD, G, P), 0.01)
        inputs['s5_b_re_' + d] = nrm((N_ODD, G, P, Hg), (2 * Hg) ** -0.5)
        inputs['s5_b_im_' + d] = nrm((N_ODD, G, P, Hg), (2 * Hg) ** -0.5)
        inputs['s5_c_re_' + d] = nrm((N_ODD, G, Hg, P), P ** -0.5)
        inputs['s5_c_im_' + d] = nrm((N_ODD, G, Hg, P), P ** -0.5)
        inputs['s5_log_dt_' + d] = math.log(DT_MIN) + jax.random.uniform(next(ks), (N_ODD, G), f32) * (math.log(DT_MAX) - math.log(DT_MIN))
    inputs['s5_d'] = nrm((N_ODD, D))
    inputs['s5_w_glu'] = nrm((N_ODD, D, 2 * D), D ** -0.5)
    return inputs

def second_block(x, c, ctx, c_ctx, ada_w, ada_b, norm1_g, norm2_g, mlp_w1, mlp_w2, w_in, mla_q_norm_g, mla_w_uq, mla_kv_norm_g, mla_w_ukv, mla_qn_g, mla_kn_g, ret_lg_f, ret_lg_b, w_out, s5_a_re_f, s5_a_im_f, s5_b_re_f, s5_b_im_f, s5_c_re_f, s5_c_im_f, s5_log_dt_f, s5_a_re_b, s5_a_im_b, s5_b_re_b, s5_b_im_b, s5_c_re_b, s5_c_im_b, s5_log_dt_b, s5_d, s5_w_glu):
    xc = ctx
    b = x.shape[0]
    for l in range(DEPTH):
        need_ctx = l < DEPTH - 1
        mod_l = (jax.nn.silu(c) @ ada_w[l] + ada_b[l]).reshape(b, ADA_CHUNKS, 1, D_MODEL)
        mod_c = (jax.nn.silu(c_ctx) @ ada_w[l] + ada_b[l]).reshape(ADA_CHUNKS, D_MODEL)
        h_l = modulate(rmsnorm(x, norm1_g[l]), mod_l[:, 0], mod_l[:, 1])
        h_c = modulate(rmsnorm(xc, norm1_g[l]), mod_c[0], mod_c[1])
        if l % 2 == 0:
            e = l // 2
            o_c, o_l = mla_retention_mixer(h_c, h_l, w_in[e], mla_q_norm_g[e], mla_w_uq[e], mla_kv_norm_g[e], mla_w_ukv[e], mla_qn_g[e], mla_kn_g[e], ret_lg_f[e], ret_lg_b[e], w_out[e], need_ctx)
        else:
            o = l // 2
            p_f = (s5_a_re_f[o], s5_a_im_f[o], s5_b_re_f[o], s5_b_im_f[o], s5_c_re_f[o], s5_c_im_f[o], s5_log_dt_f[o])
            p_b = (s5_a_re_b[o], s5_a_im_b[o], s5_b_re_b[o], s5_b_im_b[o], s5_c_re_b[o], s5_c_im_b[o], s5_log_dt_b[o])
            o_c, o_l = s5_mixer(h_c, h_l, p_f, p_b, s5_d[o], s5_w_glu[o], need_ctx)
        x = x + mod_l[:, 2] * o_l
        h_l = modulate(rmsnorm(x, norm2_g[l]), mod_l[:, 3], mod_l[:, 4])
        x = x + mod_l[:, 5] * squared_relu_mlp(h_l, mlp_w1[l], mlp_w2[l])
        if need_ctx:
            xc = xc + mod_c[2] * o_c
            h_c = modulate(rmsnorm(xc, norm2_g[l]), mod_c[3], mod_c[4])
            xc = xc + mod_c[5] * squared_relu_mlp(h_c, mlp_w1[l], mlp_w2[l])
    return x


def setup_inputs(seed=0):
    out = dict(first_inputs(seed))
    for name, value in second_inputs(seed + 1).items():
        if name != "x":
            out[name + "_2"] = value
    return out


def reference(
    x, c, ctx, c_ctx, mod_w, mod_b, norm_pre_mix, norm_post_mix, norm_pre_ffn, norm_post_ffn,
    even_w_in, gla_w_gate, gla_b_gate, gla_out_norm, att_q_norm, att_k_norm, even_w_out,
    odd_w_in, hgrn_lower_bounds, hgrn_out_norm, odd_w_out, ffn_w_gate, ffn_w_up, ffn_w_down,
    c_2, ctx_2, c_ctx_2, ada_w_2, ada_b_2, norm1_g_2, norm2_g_2, mlp_w1_2, mlp_w2_2, w_in_2,
    mla_q_norm_g_2, mla_w_uq_2, mla_kv_norm_g_2, mla_w_ukv_2, mla_qn_g_2, mla_kn_g_2,
    ret_lg_f_2, ret_lg_b_2, w_out_2, s5_a_re_f_2, s5_a_im_f_2, s5_b_re_f_2, s5_b_im_f_2,
    s5_c_re_f_2, s5_c_im_f_2, s5_log_dt_f_2, s5_a_re_b_2, s5_a_im_b_2, s5_b_re_b_2, s5_b_im_b_2,
    s5_c_re_b_2, s5_c_im_b_2, s5_log_dt_b_2, s5_d_2, s5_w_glu_2,
):
    x = first_block(
        x, c, ctx, c_ctx, mod_w, mod_b, norm_pre_mix, norm_post_mix, norm_pre_ffn,
        norm_post_ffn, even_w_in, gla_w_gate, gla_b_gate, gla_out_norm, att_q_norm, att_k_norm,
        even_w_out, odd_w_in, hgrn_lower_bounds, hgrn_out_norm, odd_w_out, ffn_w_gate, ffn_w_up,
        ffn_w_down,
    )
    return second_block(
        x, c_2, ctx_2, c_ctx_2, ada_w_2, ada_b_2, norm1_g_2, norm2_g_2, mlp_w1_2, mlp_w2_2,
        w_in_2, mla_q_norm_g_2, mla_w_uq_2, mla_kv_norm_g_2, mla_w_ukv_2, mla_qn_g_2,
        mla_kn_g_2, ret_lg_f_2, ret_lg_b_2, w_out_2, s5_a_re_f_2, s5_a_im_f_2, s5_b_re_f_2,
        s5_b_im_f_2, s5_c_re_f_2, s5_c_im_f_2, s5_log_dt_f_2, s5_a_re_b_2, s5_a_im_b_2,
        s5_b_re_b_2, s5_b_im_b_2, s5_c_re_b_2, s5_c_im_b_2, s5_log_dt_b_2, s5_d_2, s5_w_glu_2,
    )


_drawn_inputs = setup_inputs


def setup_inputs(seed=0):
    import zlib

    import numpy as np

    out = dict(_drawn_inputs(seed))
    spreads = {}
    factors = {'norm_post_mix': 3.748,
     'norm_pre_ffn': 3.39,
     'norm_post_ffn': 4.23,
     'gla_b_gate': 8.0,
     'gla_out_norm': 5.585,
     'att_q_norm': 8.0,
     'att_k_norm': 8.0,
     'hgrn_lower_bounds': 8.0,
     'hgrn_out_norm': 6.597,
     'norm1_g_2': 8.0,
     'norm2_g_2': 6.705,
     'mla_q_norm_g_2': 8.0,
     'mla_w_uq_2': 4.082,
     'mla_kv_norm_g_2': 8.0,
     'mla_qn_g_2': 8.0,
     'mla_kn_g_2': 8.0,
     's5_a_re_f_2': 64.0,
     's5_a_im_f_2': 59.496,
     's5_b_re_f_2': 64.0,
     's5_b_im_f_2': 64.0,
     's5_c_re_f_2': 64.0,
     's5_c_im_f_2': 64.0,
     's5_log_dt_f_2': 64.0,
     's5_a_re_b_2': 64.0,
     's5_a_im_b_2': 59.832,
     's5_b_re_b_2': 64.0,
     's5_b_im_b_2': 64.0,
     's5_c_re_b_2': 64.0,
     's5_c_im_b_2': 64.0,
     's5_log_dt_b_2': 64.0}
    for name, (base, spread) in spreads.items():
        noise = np.random.default_rng([zlib.crc32(name.encode()), seed]).standard_normal(out[name].shape)
        drawn = base * np.exp(spread * noise) if base else spread * noise
        out[name] = jnp.asarray(drawn.astype(out[name].dtype))
    for name, factor in factors.items():
        out[name] = (out[name] * factor).astype(out[name].dtype)
    return out
```

```python
from contextlib import ExitStack
import math

import numpy as np

import concourse.bass as bass
from concourse import mybir

F32 = mybir.dt.float32
U8 = mybir.dt.uint8
ALU = mybir.AluOpType
ACT = mybir.ActivationFunctionType
AX = mybir.AxisListType

D = 1024
KT = 8
T = 512
TC = 256
FF1 = 2816
FF2 = 4096
EPS = 1e-6
LEVELS = (64, 32, 16, 8, 4, 2, 1)

VEC = {}


def _vec_layout():
    at = 0
    for name, n in (
        ("c", 8), ("cc", 8), ("c2", 8), ("cc2", 8),
        ("mod_b", 96), ("ada_b", 96),
        ("pre_mix", 16), ("post_mix", 16), ("pre_ffn", 16), ("post_ffn", 16),
        ("n1", 16), ("n2", 16),
        ("gla_b", 4), ("gla_n", 1), ("aq_n", 1), ("ak_n", 1),
        ("lb", 32), ("hg_n", 1),
        ("mq_n", 2), ("mkv_n", 1), ("mqn", 1), ("mkn", 1),
        ("lgf", 8), ("lgb", 8), ("s5d", 8), ("eps", 1), ("one", 1),
    ):
        VEC[name] = (at, n)
        at += n
    return at


NVEC = _vec_layout()

CST = {}


def _cst_layout():
    at = 0
    for name, n in (
        ("ident", 128), ("ones", 128), ("bd", 128), ("rotE", 128), ("rotM", 128), ("rotR", 128),
        ("smask", 516), ("distF", 512), ("distR", 512), ("mF", 128), ("mR", 128), ("bd32", 128),
        ("cosE", 256), ("sinE", 256), ("cosM", 256), ("sinM", 256), ("cosR", 256), ("sinR", 256),
    ):
        CST[name] = (at, n)
        at += n
    return at


NCST = _cst_layout()


class Lane:

    def __init__(self, name, sem):
        self.name, self.sem, self.items, self.n, self.held = name, sem, [], 0, []

    def do(self, f, after=(), mark=True, inc=1, sem=None):
        waits = list(after) + self.held
        self.held = []
        if mark:
            self.n += 1
        self.items.append([waits, f, self.sem if mark else None, 1])
        return (self.sem, self.n)

    def dma(self, out, in_, sem, after=()):
        waits = list(after) + self.held
        self.held = []
        self.items.append([waits, lambda e: e.dma_start(out, in_), sem, 16])

    def last(self):
        if self.items and self.items[-1][2] is None:
            self.n += 1
            self.items[-1][2] = self.sem
        return (self.sem, self.n)

    def play(self, e):
        seen = {}
        for waits, f, sem, inc in self.items:
            need = {}
            for s, v in waits:
                if v > need.get(id(s), (s, 0))[1]:
                    need[id(s)] = (s, v)
            for k, (s, v) in need.items():
                if v > seen.get(k, 0):
                    e.wait_ge(s, v)
                    seen[k] = v
            if f is not None:
                i = f(e)
                if sem is not None:
                    i.then_inc(sem, inc)


class Vec(Lane):
    def tt(self, out, a, b, op, after=()):
        return self.do(lambda e: e.tensor_tensor(out, a, b, op), after)

    def mul(self, out, a, b, after=()):
        return self.tt(out, a, b, ALU.mult, after)

    def add(self, out, a, b, after=()):
        return self.tt(out, a, b, ALU.add, after)

    def sub(self, out, a, b, after=()):
        return self.tt(out, a, b, ALU.subtract, after)

    def ts(self, out, a, s1, op0, s2=None, op1=None, after=()):
        if op1 is None:
            return self.do(lambda e: e.tensor_scalar(out, a, s1, None, op0), after)
        return self.do(lambda e: e.tensor_scalar(out, a, s1, s2, op0, op1), after)

    def stt(self, out, a, s, b, op0, op1, after=()):
        return self.do(lambda e: e.scalar_tensor_tensor(out=out, in0=a, scalar=s, in1=b, op0=op0, op1=op1), after)

    def copy(self, out, a, after=()):
        return self.do(lambda e: e.tensor_copy(out, a), after)

    def zero(self, out, after=()):
        return self.do(lambda e: e.memset(out, 0.0), after)


class Act(Lane):
    def act(self, out, a, func, scale=1.0, bias=0.0, accum=None, after=()):
        if accum is None:
            return self.do(lambda e: e.activation(out, a, func, bias=bias, scale=scale), after)
        return self.do(lambda e: e.activation(out, a, func, bias=bias, scale=scale, accum_out=accum), after)

    def copy(self, out, a, after=()):
        return self.do(lambda e: e.activation(out, a, ACT.Copy), after)


class Pe(Lane):
    def mm(self, out, lhsT, rhs, start, stop, after=(), mark=False):
        return self.do(lambda e: e.matmul(out, lhsT, rhs, start=start, stop=stop, skip_group_check=True), after, mark)

    def tr(self, out, a, ident, after=(), mark=False):
        return self.do(lambda e: e.transpose(out, a, ident), after, mark)


class Ring:

    def __init__(self, sp, slots, sems):
        self.sp, self.slots, self.sems = sp, slots, sems
        self.at, self.count, self.users = 0, [0] * len(slots), [[] for _ in slots]

    def load(self, *parts):
        i = self.at % len(self.slots)
        self.at += 1
        for k, (view, src) in enumerate(parts):
            self.sp.dma(view(self.slots[i]), src, self.sems[i], self.users[i] if k == 0 else ())
            self.count[i] += 16
        return i, (self.sems[i], self.count[i])

    def free(self, i, token):
        self.users[i] = [token]

    def scratch(self):
        i = self.at % len(self.slots)
        self.at += 1
        return i, list(self.users[i])


class Banks:

    def __init__(self, tiles):
        self.tiles, self.readers, self.at = tiles, [[] for _ in tiles], 0

    def take(self, lo=0, hi=8):
        i = lo + (self.at - lo) % (hi - lo)
        self.at = i + 1
        return i

    def free(self, i, *tokens):
        self.readers[i] = list(tokens)


class Program:
    def __init__(self, nc, ctx, io, stop=None):
        self.nc, self.ctx, self.io, self.stop = nc, ctx, io, stop
        sem = lambda n: ctx.enter_context(nc.semaphore(n))
        self.sb = lambda n, shape, dt=F32: ctx.enter_context(nc.sbuf_tensor("sb_" + n, shape, dt))
        self.pe, self.act, self.dve, self.pool, self.sp = (
            Pe("pe", sem("pe_n")), Act("act", sem("act_n")), Vec("dve", sem("dve_n")),
            Vec("pool", sem("pool_n")), Lane("sp", sem("sp_n")))
        self.vec = self.sb("vec", [128, NVEC])
        self.cst = self.sb("cst", [128, NCST])
        self.msk = self.sb("msk", [128, 15, 128], U8)
        self.X = self.sb("X", [128, KT, T])
        self.H = self.sb("H", [128, KT, T])
        self.SX = self.sb("SX", [128, 2, KT, 2])
        self.M = self.sb("M", [128, 48, 2])
        self.CO = self.sb("CO", [128, 4, 2, KT])
        self.RS = self.sb("RS", [128, T])
        self.NW = 22816
        self.R = self.sb("R", [128, self.NW])
        self.slots = [self.sb(f"slot{i}", [128, 4096]) for i in range(4)]
        self.ring = Ring(self.sp, self.slots, [sem(f"ring{i}") for i in range(4)])
        self.ps = [ctx.enter_context(nc.psum_tensor(f"ps{i}", [128, 512], F32)) for i in range(8)]
        self.read = [[] for _ in range(8)]
        self.turn = {}
        self.s_in, self.s_x, self.s_ld, self.s_out = sem("s_in"), sem("s_x"), sem("s_ld"), sem("s_out")
        self.n_ld = 0
        self.at = 0

    def alloc(self, *shape):
        n = int(np.prod(shape))
        assert self.at + n <= self.NW, (self.at, n)
        v = self.R[:, self.at:self.at + n]
        self.at += n
        if len(shape) == 2:
            v = v.rearrange("p (a b) -> p a b", b=shape[1])
        if len(shape) == 3:
            v = v.rearrange("p (a b c) -> p a b c", b=shape[1], c=shape[2])
        if len(shape) == 4:
            v = v.rearrange("p (a b c d) -> p a b c d", b=shape[1], c=shape[2], d=shape[3])
        return v

    def v(self, name, i=0, n=1):
        a, _ = VEC[name]
        return self.vec[:, a + i:a + i + n]

    def c(self, name, n=None, p0=0, p1=128):
        a, w = CST[name]
        return self.cst[p0:p1, a:a + (w if n is None else n)]

    def bank(self, lo=0, hi=8):
        i = lo + self.turn.get((lo, hi), 0) % (hi - lo)
        self.turn[lo, hi] = self.turn.get((lo, hi), 0) + 1
        return i, self.ps[i], list(self.read[i])

    def fence(self):
        lanes = (self.pe, self.act, self.dve, self.pool)
        tokens = [l.last() for l in lanes]
        for l in lanes:
            l.held = l.held + tokens
        self.phase = tokens
        self.read = [[] for _ in range(8)]
        self.at = 0

    def load(self, out, src):
        self.sp.dma(out, src, self.s_ld, self.phase)
        self.n_ld += 16
        return (self.s_ld, self.n_ld)

    def wslot(self, W, c0, c1, l=None):
        n = c1 - c0
        src = W if l is None else W[l]
        view = lambda s: s[:, 0:KT * n].rearrange("p (k n) -> p k n", k=KT)
        i, tok = self.ring.load((view, src[:, c0:c1].rearrange("(k p) n -> p k n", p=128)))
        return i, view(self.slots[i]), tok

    def begin(self):
        io = self.io
        for out, name in ((self.vec[:, :], "vec"), (self.cst[:, :], "cst"), (self.R[:, 64:64 + 1920].rearrange("p (a b) -> p a b", b=128), "msk")):
            self.sp.dma(out, io[name], self.s_in)
        t_in = (self.s_in, 48)
        self.sp.dma(self.X[:, :, :], io["xT"], self.s_x)
        self.t_x = (self.s_x, 16)
        for lane in (self.pe, self.act, self.dve, self.pool):
            lane.held.append(t_in)
        e = self.R[:, 0:32]
        a, _ = VEC["c"]
        src = self.vec[:, a:a + 32]
        t = self.act.act(e, src, ACT.Exp, scale=-1.0)
        t = self.dve.ts(e, e, 1.0, ALU.add, after=[t])
        t = self.dve.do(lambda g: g.reciprocal(self.R[:, 32:64], e), [t])
        src4 = src.rearrange("p (b w k) -> p b w k", b=2, w=2)
        r4 = self.R[:, 32:64].rearrange("p (b w k) -> p b w k", b=2, w=2)
        for b in range(2):
            for w in range(2):
                t = self.dve.mul(self.SX[:, b, :, w], src4[:, b, w, :], r4[:, b, w, :], after=[t])
        self.t_sx = t
        self.dve.copy(self.msk[:, :, :], self.R[:, 64:64 + 1920].rearrange("p (a b) -> p a b", b=128))
        self.epsc = self.v("eps")
        self.act.held.append(self.t_x)
        self.dve.held.append(self.t_x)

    def mods(self, W, bias, blk, l, pre, post, pre2, post2):
        i, ps, rd = self.bank(7, 8)
        for g in range(12):
            s, view, tok = self.wslot(W, 512 * g, 512 * g + 512, l)
            for m in range(4):
                mt = 4 * g + m
                for k in range(KT):
                    tm = self.pe.mm(ps[:, 2 * mt:2 * mt + 2], view[:, k, 128 * m:128 * m + 128],
                                    self.SX[:, blk, k, :], k == 0, k == KT - 1,
                                    after=[tok, self.t_sx] + rd, mark=(k == KT - 1 and m == 3))
            self.ring.free(s, tm)
        P = ps[:, 0:96].rearrange("p (m w) -> p m w", w=2)
        bb = self.v(bias, 48 * l, 48)
        for w in range(2):
            t = self.dve.add(self.M[:, :, w], P[:, :, w], bb, after=[tm])
        self.read[i] = [t]
        for j, (idx, name, one) in enumerate(((1, pre, 1.0), (2, post, 0.0), (4, pre2, 1.0), (5, post2, 0.0))):
            for w in range(2):
                m = self.M[:, 8 * idx:8 * idx + 8, w]
                if name is None:
                    tc = self.dve.copy(self.CO[:, j, w, :], m, after=[t])
                else:
                    tc = self.dve.stt(self.CO[:, j, w, :], m, one, self.v(name, 8 * l, 8), ALU.add, ALU.mult, after=[t])
        self.t_co = tc

    def rstd(self, out, ps_view, n, after, eps=EPS):
        t = self.act.act(out, ps_view, ACT.Ln, scale=1.0 / n, bias=self.epsc[0:out.shape[0], 0:1], after=after)
        return self.act.act(out, out, ACT.Exp, scale=-0.5, after=[t]), t

    def norm_mod(self, n0, j, shift, after=()):
        n = T - n0
        i, ps, rd = self.bank(6, 7)
        for t in range(KT):
            ta = self.act.act(self.H[:, t, n0:T], self.X[:, t, n0:T], ACT.Square, after=after)
            tp = self.pe.mm(ps[:, 0:n], self.c("ones"), self.H[:, t, n0:T], t == 0, t == KT - 1,
                            after=[ta] + rd, mark=(t == KT - 1))
        te, tl = self.rstd(self.RS[:, 0:n], ps[:, 0:n], D, [tp])
        self.read[i] = [tl]
        self.t_h = [None] * KT
        for t in range(KT):
            tv = self.dve.mul(self.H[:, t, n0:T], self.X[:, t, n0:T], self.RS[:, 0:n], after=[te, tp])
            for w, a, b in ((1, 0, TC), (0, TC, T)):
                if b <= n0:
                    continue
                h = self.H[:, t, a:b]
                sc, sh = self.CO[:, j, w, t:t + 1], self.M[:, 8 * shift + t, w:w + 1]
                if t % 2:
                    tt = self.act.act(h, h, ACT.Identity, scale=sc, bias=sh, after=[tv, self.t_co])
                else:
                    tt = self.dve.ts(h, h, sc, ALU.mult, sh, ALU.add, after=[tv, self.t_co])
            self.t_h[t] = tt

    def resid(self, Y, n0, j, norm, after):
        n = T - n0
        if norm:
            i, ps, rd = self.bank(6, 7)
            for t in range(KT):
                ta = self.act.act(self.H[:, t, 0:n], Y[:, t, :], ACT.Square, after=[after[t]])
                tp = self.pe.mm(ps[:, 0:n], self.c("ones"), self.H[:, t, 0:n], t == 0, t == KT - 1,
                                after=[ta] + rd, mark=(t == KT - 1))
            te, tl = self.rstd(self.RS[:, 0:n], ps[:, 0:n], D, [tp])
            self.read[i] = [tl]
        for t in range(KT):
            tv = after[t]
            if norm:
                tv = self.dve.mul(Y[:, t, :], Y[:, t, :], self.RS[:, 0:n], after=[te, after[t]])
            for w, a, b in ((1, 0, TC), (0, TC, T)):
                if b <= n0:
                    continue
                self.dve.stt(self.X[:, t, a:b], Y[:, t, a - n0:b - n0], self.CO[:, j, w, t:t + 1],
                             self.X[:, t, a:b], ALU.mult, ALU.add, after=[tv, self.t_co])

    def fm(self, w, m0, m, n0, out, after, lo=0, hi=4, po=0, eng=None, K=KT, rhs=None, **kw):
        n = T - n0
        i, ps, rd = self.bank(lo, hi)
        for k in range(K):
            r = self.H[:, k, n0:T] if rhs is None else rhs(k)
            h = [self.t_h[k]] if rhs is None else []
            tm = self.pe.mm(ps[po:po + m, 0:n], w[:, k, m0:m0 + m], r, k == 0, k == K - 1,
                            after=list(after) + rd + h, mark=(k == K - 1))
        self.read[i] = [out(ps[po:po + m, 0:n], tm)]
        return tm

    def tm(self, w, c0, c1, jt, out, after, lo=0, hi=4):
        i, ps, rd = self.bank(lo, hi)
        for k in range(KT):
            tk = self.pe.mm(ps[:, 0:c1 - c0], self.H[:, k, 128 * jt:128 * jt + 128], w[:, k, c0:c1],
                            k == 0, k == KT - 1, after=list(after) + rd + [self.t_h[k]], mark=(k == KT - 1))
        self.read[i] = [out(ps[:, 0:c1 - c0], tk)]
        return tk

    def down(self, W, S, n, k_of, kt, after, Y):
        for k0 in range(0, kt, 4):
            kn = min(4, kt - k0)
            view = lambda s: s[:, 0:kn * D].rearrange("p (k n) -> p k n", k=kn)
            s, tok = self.ring.load((view, W[128 * k0:128 * (k0 + kn), :].rearrange("(k p) n -> p k n", p=128)))
            w = view(self.slots[s])
            for k in range(k0, k0 + kn):
                for t in range(KT):
                    tm = self.pe.mm(self.ps[t][:, 0:n], w[:, k - k0, 128 * t:128 * t + 128], k_of(k),
                                    k == 0, k == kt - 1, after=[tok] + list(after[k]) + (self.read[t] if k == 0 else []),
                                    mark=(k == kt - 1 or t == KT - 1))
                    if k == kt - 1:
                        lane = self.act if t % 2 else self.dve
                        self.read[t] = [lane.copy(Y[:, t, :], self.ps[t][:, 0:n], after=[tm])]
            self.ring.free(s, tm)
        return [self.read[t][0] for t in range(KT)]

    def ffn_swiglu(self, l, n0):
        n = T - n0
        self.fence()
        self.norm_mod(n0, 2, 3)
        G = self.alloc(22, n)
        tmp = [self.alloc(n) for _ in range(2)]
        io = self.io
        free = [[], []]
        done = []
        for g in range(11):
            view = lambda s: s[:, :].rearrange("p (u k n) -> p u k n", u=2, k=KT)
            cols = slice(256 * g, 256 * g + 256)
            s, tok = self.ring.load(
                (lambda s: view(s)[:, 0], io["ffn_w_gate"][l][:, cols].rearrange("(k p) n -> p k n", p=128)),
                (lambda s: view(s)[:, 1], io["ffn_w_up"][l][:, cols].rearrange("(k p) n -> p k n", p=128)))
            w = view(self.slots[s])
            for m in range(2):
                x = 2 * g + m
                tb = tmp[x % 2]
                got = []

                def gate(ps, t, tb=tb, x=x):
                    t = self.act.act(tb, ps, ACT.Silu, after=[t] + free[x % 2])
                    got.append(t)
                    return t

                def up(ps, t, tb=tb, x=x):
                    t = self.dve.mul(G[:, x, :], ps, tb, after=[t, got[0]])
                    free[x % 2] = [t]
                    done.append([t])
                    return t

                self.fm(w[:, 0], 128 * m, 128, n0, gate, [tok], 0, 6)
                tm = self.fm(w[:, 1], 128 * m, 128, n0, up, [tok], 0, 6)
            self.ring.free(s, tm)
        Yr = self.alloc(KT, n)
        ys = self.down(io["ffn_w_down"][l], None, n, lambda k: G[:, k, :], 22, done, Yr)
        self.fence_keep()
        self.resid(Yr, n0, 3, True, ys)

    def fence_keep(self):
        at = self.at
        self.fence()
        self.at = at

    def ffn_sq(self, l, n0):
        n = T - n0
        self.fence()
        self.norm_mod(n0, 2, 3)
        G = self.alloc(32, n)
        done = []
        io = self.io
        for g in range(8):
            s, w, tok = self.wslot(io["mlp_w1_2"], 512 * g, 512 * g + 512, l)
            for m in range(4):
                x = 4 * g + m

                def out(ps, t, x=x):
                    t = self.act.act(G[:, x, :], ps, ACT.Relu, after=[t])
                    done.append([self.pool.mul(G[:, x, :], G[:, x, :], G[:, x, :], after=[t])])
                    return t

                tm = self.fm(w, 128 * m, 128, n0, out, [tok], 0, 6)
            self.ring.free(s, tm)
        Y = self.alloc(KT, n)
        ys = self.down(io["mlp_w2_2"][l], None, n, lambda k: G[:, k, :], 32, done, Y)
        self.fence_keep()
        self.resid(Y, n0, 3, False, ys)

    def cumsum(self, B, g, after):
        n = B.shape[1] * B.shape[2]
        return self.dve.do(lambda e: e.tensor_tensor_scan(
            B.rearrange("p c x -> p (c x)"), self.c("smask", n), g.rearrange("p c x -> p (c x)"), 0.0,
            ALU.mult, ALU.add), after)

    def levels(self, *args):
        last = []
        for _ in self.levels_steps(*args, last):
            pass
        return last

    def levels_steps(self, q, ks, Bs, c0, nc, scale, heads, bufs, after, lo, hi, last):
        last += [None] * len(heads)
        for h, (pb, sz, P, dg) in enumerate(heads):
            i, ps, rd = self.bank(lo, hi)
            for c in range(nc):
                for d, kk in enumerate(dg):
                    tm = self.pe.mm(ps[:, 128 * c:128 * c + 128], kk[pb:pb + sz, 128 * (c0 + c):128 * (c0 + c) + 128],
                                    q[pb:pb + sz, 128 * c:128 * c + 128], d == 0, d == len(dg) - 1,
                                    after=after + rd, mark=(c == nc - 1 and d == len(dg) - 1))
            eye = self.c("ident").unsqueeze(1).broadcast_to([128, nc, 128])
            S = ps[:, 0:128 * nc].rearrange("p (c x) -> p c x", c=nc)
            last[h] = self.dve.stt(P, S, 2.0 if len(dg) == 1 else 1.0, eye, ALU.mult, ALU.mult,
                                   after=[tm] + self.free_p[h])
            self.read[i] = [last[h]]
        for s in range(2):
            B, k = Bs[s], ks[s]
            sh = 1 - s
            for li, L in enumerate(LEVELS):
                u = self.turn.get("lvl", 0)
                self.turn["lvl"] = u + 1
                E, U, V = bufs[u % len(bufs)]
                fr = self.lvl_free[u % len(bufs)]
                halves = lambda x: x.rearrange("p c (b h l) -> p c b h l", h=2, l=L)
                Ev = halves(E.rearrange("p (c x) -> p c x", c=nc))
                Bt = halves(B[:, c0:c0 + nc, sh:sh + 128])
                Bm = halves(B[:, c0:c0 + nc, 0:128])[:, :, :, 1, 0:1].broadcast_to([E.shape[0], nc, 64 // L, L])
                t1 = self.dve.sub(Ev[:, :, :, 0, :], Bm, Bt[:, :, :, 0, :], after=after + fr)
                t2 = self.dve.sub(Ev[:, :, :, 1, :], Bt[:, :, :, 1, :], Bm, after=after + fr)
                te = self.act.act(E, E, ACT.Exp, scale=scale, after=[t1, t2])
                tu = self.pool.mul(U, k[:, 128 * c0:128 * (c0 + nc)], E, after=[te] + after + fr)
                tv = self.dve.mul(V, q, E, after=[te] + after + fr)
                for h, (pb, sz, P, dg) in enumerate(heads):
                    i, ps, rd = self.bank(lo, hi)
                    for c in range(nc):
                        cs = slice(128 * c, 128 * c + 128)
                        tm = self.pe.mm(ps[:, cs], U[pb:pb + sz, cs], V[pb:pb + sz, cs], True, True,
                                        after=[tu, tv] + rd, mark=(c == nc - 1))
                    mk = self.msk[:, 7 * s + li:7 * s + li + 1, :].broadcast_to([128, nc, 128])
                    S = ps[:, 0:128 * nc].rearrange("p (c x) -> p c x", c=nc)
                    last[h] = self.dve.do(lambda e, P=P, mk=mk, S=S: e.copy_predicated(P, mk, S), [tm, last[h]])
                    self.read[i] = [last[h]]
                self.lvl_free[u % len(bufs)] = [tm]
                yield

    def across(self, ks, Bs, scale, W, after):
        out = []
        for s in range(2):
            B, k = Bs[s], ks[s]
            w, x, e = W[s], W[2 + s], W[4 + s]
            w3 = w.rearrange("p (c x) -> p c x", c=4)
            P = w.shape[0]
            if s == 0:
                t = self.dve.sub(w3, B[:, :, 128:129].broadcast_to([P, 4, 128]), B[:, :, 1:129], after=after + self.w_free)
                t = self.act.act(w, w, ACT.Exp, scale=scale, after=[t])
            else:
                t = self.act.act(w3, B[:, :, 0:128], ACT.Exp, scale=scale, after=after + self.w_free)
            t = self.pool.mul(w, w, k, after=[t] + after)
            ta = self.act.act(e, B[:, :, 128], ACT.Exp, scale=scale, after=after + self.w_free)
            T_ = lambda c: e[:, c:c + 1]
            K_ = lambda c: w[:, 128 * c:128 * c + 128]
            o = [t, ta] + self.w_free
            if s == 0:
                seq = ((0, K_(0), T_(1)), (1, K_(1), T_(2)), (2, x[:, 0, :], T_(2)))
            else:
                seq = ((0, K_(1), T_(0)), (1, K_(0), T_(3)), (2, x[:, 0, :], T_(3)))
            for j, a, b in seq:
                o.append(self.dve.ts(x[:, j, :], a, b, ALU.mult, after=o))
            out.append([t] + o[-3:])
        return out

    def queries(self, q, Bs, c0, nc, scale, Q, after):
        out = []
        for s in range(2):
            B = Bs[s][:, c0:c0 + nc]
            e = Q[s]
            e3 = e.rearrange("p (c x) -> p c x", c=nc)
            P = e.shape[0]
            if s == 0:
                t = self.act.act(e3, B[:, :, 1:129], ACT.Exp, scale=scale, after=after + self.w_free)
            else:
                t = self.dve.sub(e3, B[:, :, 128:129].broadcast_to([P, nc, 128]), B[:, :, 0:128], after=after + self.w_free)
                t = self.act.act(e, e, ACT.Exp, scale=scale, after=[t])
            out.append(self.dve.mul(e, e, q, after=[t] + after))
        return out

    def cross_scores(self, pb, sz, W, Q, q0, dst, after, lo, hi, chunks=(0, 1, 2, 3)):
        K = lambda s, j: W[s][pb:pb + sz, 128 * j:128 * j + 128]
        X = lambda s, j: W[2 + s][pb:pb + sz, j, :]
        pairs = {(0, 1): [(0, K(0, 0))], (1, 0): [(1, K(1, 1))], (2, 3): [(0, K(0, 2))], (3, 2): [(1, K(1, 3))],
                 (0, 2): [(0, X(0, 0)), (1, X(1, 1))], (1, 2): [(0, K(0, 1)), (1, X(1, 2))],
                 (0, 3): [(0, X(0, 2)), (1, K(1, 0))], (1, 3): [(0, X(0, 1)), (1, X(1, 0))]}
        todo = [p for p in pairs if p[1] in chunks]
        out = []
        for a in range(0, len(todo), 4):
            i, ps, rd = self.bank(lo, hi)
            part = todo[a:a + 4]
            for n, (J, I) in enumerate(part):
                for m, (s, k) in enumerate(pairs[J, I]):
                    tm = self.pe.mm(ps[:, 128 * n:128 * n + 128], k, Q[s][pb:pb + sz, 128 * (I - q0):128 * (I - q0) + 128],
                                    m == 0, m == len(pairs[J, I]) - 1, after=after + rd,
                                    mark=(n == len(part) - 1 and m == len(pairs[J, I]) - 1))
            for n, (J, I) in enumerate(part):
                out.append(self.act.copy(dst(J, I), ps[:, 128 * n:128 * n + 128], after=[tm] + self.free_cross))
            self.read[i] = [out[-1]]
        return out

    def readout(self, o, og, gain, dst, n, after, tmp, lo, hi, dv=128, mat="ones"):
        r, sq = tmp
        ta = self.act.act(sq, o, ACT.Square, after=after)
        i, ps, rd = self.bank(lo, hi)
        tp = self.pe.mm(ps[:, 0:n], self.c(mat), sq, True, True, after=[ta] + rd, mark=True)
        te, tl = self.rstd(r, ps[:, 0:n], dv, [tp] + after)
        self.read[i] = [tl]
        t = self.dve.mul(dst, o, r, after=[te, ta] + after)
        t2 = self.dve.stt(dst, dst, gain, og, ALU.mult, ALU.mult, after=[t] + after)
        return t, t2

    def rms_heads(self, x, mat, K, n, dh, gain, after, tmp, lo, hi):
        r, sq = tmp
        ta = self.act.act(sq[0:K], x, ACT.Square, after=after)
        i, ps, rd = self.bank(lo, hi)
        tp = self.pe.mm(ps[0:K, 0:n], self.c(mat, K, 0, K), sq[0:K], True, True, after=[ta] + rd, mark=True)
        te, tl = self.rstd(r[0:K], ps[0:K, 0:n], dh, [tp] + after)
        self.read[i] = [tl]
        t = self.dve.stt(x, x, gain, r[0:K], ALU.mult, ALU.mult, after=[te] + after)
        return t

    def rope(self, x, K, mat, cs, sn, after, tmp, lo, hi):
        i, ps, rd = self.bank(lo, hi)
        tp = self.pe.mm(ps[0:K, 0:TC], self.c(mat, K, 0, K), x, True, True, after=after + rd, mark=True)
        t1 = self.dve.mul(tmp[0:K], ps[0:K, 0:TC], self.c(sn, None, 0, K), after=[tp] + after)
        self.read[i] = [t1]
        t2 = self.dve.mul(x, x, self.c(cs, None, 0, K), after=[tp])
        return self.dve.add(x, x, tmp[0:K], after=[t1, t2])

    def attend(self, q, k, sz, pb, vv, dst, q0, nq, nk, scale, after, st, lo, hi, po):
        for c in range(nq):
            u = self.turn.get("att", 0)
            self.turn["att"] = u + 1
            P, PT, m, r = st["P"][u % 2], st["PT"][u % 2], st["m"][:, u:u + 1], st["r"][:, 2 * u:2 * u + 2]
            i, ps, rd = self.bank(lo, hi)
            qs = slice(q0 + 128 * c, q0 + 128 * c + 128)
            tm = self.pe.mm(ps[:, 0:nk], q[pb:pb + sz, qs], k[pb:pb + sz, 0:nk], True, True, after=after + rd, mark=True)
            t1 = self.dve.do(lambda e, m=m, ps=ps: e.reduce_max(m, ps[:, 0:nk], AX.X), [tm])
            t2 = self.dve.ts(m, m, -scale, ALU.mult, after=[t1])
            t3 = self.act.act(P[:, 0:nk], ps[:, 0:nk], ACT.Exp, scale=scale, bias=m, accum=r[:, 0:1],
                              after=[t2] + st["fp"][u % 2])
            self.read[i] = [t3]
            t4 = self.dve.do(lambda e, r=r: e.reciprocal(r[:, 1:2], r[:, 0:1]), [t3])
            t5 = self.dve.ts(P[:, 0:nk], P[:, 0:nk], r[:, 1:2], ALU.mult, after=[t4, t3])
            i, ps, rd = self.bank(lo, hi)
            for j in range(nk // 128):
                tm = self.pe.tr(ps[:, 128 * j:128 * j + 128], P[:, 128 * j:128 * j + 128], self.c("ident"),
                                after=[t5] + rd, mark=(j == nk // 128 - 1))
            st["fp"][u % 2] = [tm]
            lane = self.act if u % 2 else self.dve
            t6 = lane.copy(PT[:, 0:nk], ps[:, 0:nk], after=[tm] + st["fpt"][u % 2])
            self.read[i] = [t6]
            i, ps, rd = self.bank(lo, hi)
            for j in range(nk // 128):
                tm = self.pe.mm(ps[po:po + 64, 0:128], vv(j), PT[:, 128 * j:128 * j + 128], j == 0,
                                j == nk // 128 - 1, after=[t6] + rd + after, mark=(j == nk // 128 - 1))
            st["fpt"][u % 2] = [tm]
            st["out"] = self.act.copy(dst(c), ps[po:po + 64, 0:128], after=[tm])
            self.read[i] = [st["out"]]

    def att_state(self, n):
        self.turn["att"] = 0
        return {"P": [self.alloc(T) for _ in range(2)], "PT": [self.alloc(T) for _ in range(2)],
                "m": self.alloc(n), "r": self.alloc(2 * n), "fp": [[], []], "fpt": [[], []]}

    def even(self):
        io = self.io
        W = io["even_w_in"][0]
        self.fence()
        gw = self.alloc(2 * 256)
        t_gw = self.load(gw[0:32], io["gla_gw"])
        self.norm_mod(0, 0, 0)
        q, k, og = self.alloc(2, T), self.alloc(2, T), self.alloc(4, T)
        z, aq, kk = self.alloc(T), self.alloc(4, T), self.alloc(2, T)
        vg, va = self.alloc(4, T), self.alloc(4, 128)
        cp = lambda dst, sc=None: (lambda ps, t: self.act.act(dst, ps, ACT.Copy, scale=sc or 1.0, after=[t]))
        s, w, tok = self.wslot(W, 0, 512)
        for m in range(2):
            self.fm(w, 128 * m, 128, 0, cp(q[:, m, :], 0.125), [tok])
        for m in range(2):
            tl = self.fm(w, 256 + 128 * m, 128, 0, cp(k[:, m, :]), [tok])
        self.ring.free(s, tl)
        n = 32 + 256
        view = lambda s: s[:, 0:KT * n].rearrange("p (k n) -> p k n", k=KT)
        s, tok = self.ring.load(
            (lambda s: view(s)[:, :, 0:32], W[:, 1536:1568].rearrange("(k p) n -> p k n", p=128)),
            (lambda s: view(s)[:, :, 32:288], W[:, 2080:2336].rearrange("(k p) n -> p k n", p=128)))
        w = view(self.slots[s])
        self.fm(w, 0, 32, 0, cp(z[0:32, :]), [tok])
        t_z = (self.act.sem, self.act.n)
        for g in range(2):
            for half in range(2):
                self.fm(w, 32 + 64 * g, 64, 0, cp(kk[64 * half:64 * half + 64, g, :]), [tok], po=64 * half)
        for j in range(4):
            tl = self.tm(w, 160, 288, j, lambda ps, t, j=j: self.act.copy(va[:, j, :], ps, after=[t]), [tok])
        self.ring.free(s, tl)
        s, w, tok = self.wslot(W, 512, 1024)
        for j in range(4):
            tl = self.tm(w, 0, 512, j, lambda ps, t, j=j: self.act.copy(vg[:, j, :], ps, after=[t]), [tok])
        self.ring.free(s, tl)
        s, w, tok = self.wslot(W, 1568, 2080)
        for m in range(4):
            tl = self.fm(w, 128 * m, 128, 0, cp(aq[:, m, :]), [tok])
        self.ring.free(s, tl)
        s, w, tok = self.wslot(W, 1024, 1536)
        for m in range(4):
            tl = self.fm(w, 128 * m, 128, 0, lambda ps, t, m=m: self.act.act(og[:, m, :], ps, ACT.Silu, after=[t]), [tok])
        self.ring.free(s, tl)
        self.fence_keep()
        MIX = self.H
        mark = self.at
        Bs = [[None, None], [None, None]]
        Bf = self.alloc(4, 4 * 129)
        gp, Lt, aL = self.alloc(4 * 129), self.alloc(T), self.alloc(T)
        tz = self.dve.zero(gp)
        gp3 = gp.rearrange("p (c x) -> p c x", x=129)
        tB = [tz]
        for m in range(2):
            for d in range(2):
                i, ps, rd = self.bank(0, 4)
                tm = self.pe.mm(ps[:, :], gw[0:32, 256 * d + 128 * m:256 * d + 128 * m + 128], z[0:32, :], True, True,
                                after=[t_gw, t_z] + rd, mark=True)
                t = self.act.act(Lt, ps[:, :], ACT.Identity, bias=self.v("gla_b", 2 * d + m), after=[tm] + tB)
                self.read[i] = [t]
                ta = self.act.act(aL, Lt, ACT.Abs, after=[t])
                ta = self.act.act(aL, aL, ACT.Exp, scale=-1.0, after=[ta])
                ta = self.act.act(aL, aL, ACT.Ln, bias=self.v("one"), after=[ta])
                L3, a3 = Lt.rearrange("p (c x) -> p c x", c=4), aL.rearrange("p (c x) -> p c x", c=4)
                t = self.dve.stt(gp3[:, :, 1:129], L3, 0.0, a3, ALU.min, ALU.subtract, after=[t, ta] + tB)
                B = Bf[:, 2 * d + m, :].rearrange("p (c x) -> p c x", x=129)
                tB = [self.cumsum(B, gp3, [t])]
                Bs[m][d] = B
        self.fence_keep()
        SC = 1.0 / 16.0
        bufs = [(self.alloc(T), self.alloc(T), self.alloc(T)) for _ in range(1)]
        WW = [self.alloc(T), self.alloc(T), self.alloc(3, 128), self.alloc(3, 128), self.alloc(4), self.alloc(4)]
        QQ = [self.alloc(T), self.alloc(T)]
        tmp = (Lt, aL)
        self.w_free, self.lvl_free, self.free_p, self.free_cross = [], [[]] * len(bufs), [[], []], []
        si, fr = self.ring.scratch()
        self.free_p = [fr, fr]
        self.free_cross = fr
        PP = [self.slots[si][:, 2048 * h:2048 * h + 2048].rearrange("p (j x) -> p j x", j=4) for h in range(2)]
        for m in range(2):
            ks, qm = [k[:, m, :]] * 2, q[:, m, :]
            tw = self.across(ks, Bs[m], SC, WW, [])
            tq = self.queries(qm, Bs[m], 0, 4, SC, QQ, [])
            heads = []
            for h in range(2):
                heads.append((64 * h, 64, self.diag_view(si, 2048 * h), [k[:, m, :]]))
            last = self.levels(qm, ks, Bs[m], 0, 4, SC, heads, bufs, [], 0, 4)
            tx = []
            for h in range(2):
                tx.append(self.cross_scores(64 * h, 64, WW, QQ, 0, lambda J, I, h=h: PP[h][:, J, 128 * I:128 * I + 128],
                                            tw[0] + tw[1] + tq, 4, 6))
            to = []
            for h in range(2):
                hd = 2 * m + h
                i, ps, rd = self.bank(6, 8)
                for J in range(4):
                    a = 0 if J < 2 else TC
                    tm = self.pe.mm(ps[:, a:T], vg[:, J, 128 * hd:128 * hd + 128], PP[h][:, J, a:T], J == 0, J == 3,
                                    after=[last[h]] + tx[h] + rd, mark=(J == 3))
                t1, t2 = self.readout(ps[:, :], og[:, hd, :], self.v("gla_n"), MIX[:, hd, :], T, [tm] + to, tmp, 4, 6)
                self.read[i] = [t1]
                to = [t1]
                self.free_p[h] = [tm]
            self.free_cross = [tm]
            self.w_free = [tm]
        self.ring.users[si] = [tm]
        self.fence_keep()
        self.at = mark
        tmp = (self.alloc(T), self.alloc(T))
        rt = self.alloc(TC)
        st = self.att_state(32)
        tk, tr = [], [[], []]
        prev = []
        for x, gain, n in ((kk[:, 0, :], "ak_n", 0), (kk[:, 1, :], "ak_n", 0)) + tuple((aq[:, m, :], "aq_n", 1) for m in range(4)):
            t = self.rms_heads(x, "bd", 128, T, 64, self.v(gain), prev, tmp, 0, 4)
            t = self.rope(x[:, TC:T], 128, "rotE", "cosE", "sinE", [t] + prev, rt, 0, 4)
            prev = [t]
        for h in range(8):
            m, pb, g = h // 2, 64 * (h % 2), h // 4
            for q0, nq, nk in ((0, 2, TC), (TC, 2, T)):
                self.attend(aq[:, m, :], kk[:, g, :], 64, pb, lambda j, g=g: va[:, j, 64 * g:64 * g + 64],
                            lambda c, m=m, pb=pb, q0=q0: MIX[pb:pb + 64, 4 + m, q0 + 128 * c:q0 + 128 * c + 128],
                            q0, nq, nk, 0.125, prev, st, 0, 8, pb)
        self.fence()
        if self.stop == "evenmix":
            return
        Y = self.alloc(KT, T)
        ys = self.down(io["even_w_out"][0], None, T, lambda k: MIX[:, k, :], 8, [[]] * 8, Y)
        self.fence_keep()
        self.resid(Y, 0, 1, True, ys)

    def diag_view(self, si, off):
        v = self.slots[si][:, off:off + 640].unsqueeze(1).broadcast_to([128, 4, 640])
        v = v[:, :, 0:128]
        return bass.AP(v.tensor, v.offset, [list(v.ap[0]), [640, 4], [1, 128]])

    def finish(self):
        self.fence()
        tokens, self.phase = self.phase, None
        self.sp.dma(self.io["outX"], (self.H if 'mix' in self.stop else self.X)[:, :, :] if self.stop else self.X[:, :, TC:T], self.s_out, tokens)
        self.sp.items.append([[(self.s_out, 16)], None, None, 0])
        with self.nc.Block() as block:
            @block.sync
            def _(e):
                self.sp.play(e)

            @block.gpsimd
            def _(e):
                self.pool.play(e)

            @block.scalar
            def _(e):
                self.act.play(e)

            @block.tensor
            def _(e):
                self.pe.play(e)

            @block.vector
            def _(e):
                self.dve.play(e)

    def together(self, *gens):
        gens = list(gens)
        while gens:
            for g in list(gens):
                if next(g, self) is self:
                    gens.remove(g)

    def odd(self):
        io = self.io
        W = io["odd_w_in"][0]
        self.fence()
        self.norm_mod(0, 0, 0)
        V, MIX = self.alloc(4, D), self.alloc(KT, TC)
        for g in range(2):
            s, w, tok = self.wslot(W, 3072 + 512 * g, 3584 + 512 * g)
            for j in range(4):
                dst = V[:, j, 512 * g:512 * g + 512]
                tl = self.tm(w, 0, 512, j, lambda ps, t, dst=dst: self.act.copy(dst, ps, after=[t]), [tok], 0, 2)
            self.ring.free(s, tl)
        e, p = self.alloc(4, 8), self.alloc(4, 8)
        mx = self.alloc(2, 8)
        lb = self.v("lb", 0, 32).rearrange("p (a h) -> p a h", h=8)
        l4 = lb.rearrange("p (d l) h -> p d l h", l=2)
        e4, p4 = (x.rearrange("p (d l) h -> p d l h", l=2) for x in (e, p))
        t = self.dve.tt(mx, l4[:, :, 0, :], l4[:, :, 1, :], ALU.max)
        for l in range(2):
            t = self.dve.sub(e4[:, :, l, :], l4[:, :, l, :], mx, after=[t])
        t = self.act.act(e, e, ACT.Exp, after=[t])
        t = self.dve.add(mx, e4[:, :, 0, :], e4[:, :, 1, :], after=[t])
        t = self.dve.do(lambda g: g.reciprocal(mx, mx), [t])
        for l in range(2):
            t = self.dve.mul(p4[:, :, l, :], e4[:, :, l, :], mx, after=[t])
        t = self.dve.ts(p4[:, :, 1, :], p4[:, :, 1, :], 2.0 ** -60, ALU.max, after=[t])
        t_lb = t
        sets = []
        for _ in range(2):
            sets.append(dict(q=self.alloc(TC), og=self.alloc(TC), k=[self.alloc(T), self.alloc(T)],
                             B=[self.alloc(4, 129), self.alloc(4, 129)]))
        sg, sf = [self.alloc(TC) for _ in range(2)], self.alloc(T)
        gp = [self.alloc(4, 129) for _ in range(2)]
        tz = [self.dve.zero(g) for g in gp]
        bufs = [(self.alloc(TC), self.alloc(TC), self.alloc(TC)) for _ in range(2)]
        WW = [self.alloc(T), self.alloc(T), self.alloc(3, 128), self.alloc(3, 128), self.alloc(4), self.alloc(4)]
        QQ = [self.alloc(TC), self.alloc(TC)]
        PB = self.alloc(4 * TC)
        PP = PB.rearrange("p (j x) -> p j x", j=4)
        diag = bass.AP(PB.tensor, PB[:, 512:513].offset, [list(PB.ap[0]), [384, 2], [1, 128]])
        tmp = (self.alloc(TC), self.alloc(TC))
        self.w_free, self.lvl_free, self.free_p, self.free_cross = [], [[], []], [[]], []
        done = [[], []]
        ready = {}
        gf = [[], []]

        def project(h):
            u = h % 2
            S = sets[u]
            view = lambda s: s[:, :].rearrange("p (a k n) -> p a k n", a=4, k=KT)
            s, tok = self.ring.load(*[
                (lambda s, a=a: view(s)[:, a], W[:, c + 128 * h:c + 128 * h + 128].rearrange("(k p) n -> p k n", p=128))
                for a, c in enumerate((0, 4096, 1024, 2048))])
            w = view(self.slots[s])
            toks = []
            for a, key in ((0, "q"), (1, "og")):
                def silu(ps, t, a=a, key=key):
                    t = self.act.act(sg[a], ps, ACT.Sigmoid, after=[t] + gf[a])
                    t = self.dve.mul(S[key], ps, sg[a], after=[t] + done[u])
                    gf[a] = [t]
                    toks.append(t)
                    return t
                self.fm(w[:, a], 0, 128, TC, silu, [tok], 0, 2)
                yield
            for d in range(2):
                p1, p0 = p[:, 2 * d + 1, h:h + 1], p[:, 2 * d, h:h + 1]

                def gate(ps, t, d=d, p1=p1, p0=p0):
                    g, B, k = gp[d], S["B"][d], S["k"][d]
                    t1 = self.act.act(sf, ps, ACT.Sigmoid, after=[t] + self.sf_free)
                    t2 = self.act.act(k, ps, ACT.Sigmoid, scale=-1.0, after=[t] + done[u])
                    t3 = self.dve.ts(g[:, :, 1:129], sf.rearrange("p (c x) -> p c x", c=4), p0, ALU.mult, p1, ALU.add,
                                     after=[t1, t_lb] + self.g_free[d] + tz)
                    self.sf_free = [t3]
                    tk = self.dve.ts(k, k, p0, ALU.mult, after=[t2, t_lb])
                    t4 = self.act.act(g[:, :, 1:129], g[:, :, 1:129], ACT.Ln, after=[t3])
                    t5 = self.cumsum(B, g, [t4] + done[u])
                    self.g_free[d] = [t5]
                    toks.extend([tk, t5])
                    return t2
                tl = self.fm(w[:, 2 + d], 0, 128, 0, gate, [tok], 0, 2)
                yield
            self.ring.free(s, tl)
            ready[h] = toks

        self.sf_free, self.g_free = [], [[], []]

        def mix(h):
            u = h % 2
            S, af = sets[u], ready[h]
            tw = self.across(S["k"], S["B"], 1.0, WW, af)
            yield
            tq = self.queries(S["q"], S["B"], 2, 2, 1.0, QQ, af)
            last = []
            yield from self.levels_steps(S["q"], S["k"], S["B"], 2, 2, 1.0, [(0, 128, diag, S["k"])], bufs, af, 2, 5, last)
            tx = self.cross_scores(0, 128, WW, QQ, 2, lambda J, I: PP[:, J, 128 * (I - 2):128 * (I - 2) + 128],
                                   tw[0] + tw[1] + tq, 5, 6, (2, 3))
            yield
            i, ps, rd = self.bank(6, 7)
            for J in range(4):
                tm = self.pe.mm(ps[:, 0:TC], V[:, J, 128 * h:128 * h + 128], PP[:, J, :], J == 0, J == 3,
                                after=[last[0]] + tx + rd, mark=(J == 3))
            t1, t2 = self.readout(ps[:, 0:TC], S["og"], self.v("hg_n"), MIX[:, h, :], TC, [tm] + self.ro_free, tmp, 7, 8)
            self.read[i] = [t1]
            self.ro_free = [t1]
            self.free_p[0] = self.free_cross = self.w_free = [tm]
            done[u] = [t2, t1]
            yield

        self.ro_free = []
        self.together(project(0))
        for h in range(8):
            if h < 7:
                self.together(mix(h), project(h + 1))
            else:
                self.together(mix(h))
        self.fence_keep()
        if self.stop == "oddmix":
            self.act.copy(self.H[:, :, TC:T], MIX)
            return
        Y = self.alloc(KT, TC)
        ys = self.down(io["odd_w_out"][0], None, TC, lambda k: MIX[:, k, :], 8, [[]] * 8, Y)
        self.fence_keep()
        self.resid(Y, TC, 1, True, ys)

    def mla(self):
        io = self.io
        W = io["w_in_2"][0]
        self.fence()
        self.sp.dma(self.X[:, :, 0:TC], io["x2T"], self.s_x, self.phase)
        self.norm_mod(0, 0, 0, after=[(self.s_x, 32)])
        cp = lambda dst, sc=None: (lambda ps, t: self.act.act(dst, ps, ACT.Copy, scale=sc or 1.0, after=[t]))
        rq, rk, rg, rv = (self.alloc(4, T) for _ in range(4))
        cq, ckv, kr, vv = self.alloc(2, T), self.alloc(T), self.alloc(T), self.alloc(4, T)
        s, w, tok = self.wslot(W, 0, 416)
        for m in range(2):
            self.fm(w, 128 * m, 128, 0, cp(cq[:, m, :]), [tok])
        self.fm(w, 256, 128, 0, cp(ckv), [tok])
        tl = self.fm(w, 384, 32, 0, cp(kr[64:96, :]), [tok], po=64)
        self.ring.free(s, tl)
        for c0, dst, sc in ((416, rq, 1.0), (928, rk, 0.125)):
            s, w, tok = self.wslot(W, c0, c0 + 512)
            for m in range(4):
                tl = self.fm(w, 128 * m, 128, 0, cp(dst[:, m, :], sc), [tok])
            self.ring.free(s, tl)
        s, w, tok = self.wslot(W, 1440, 1952)
        for j in range(4):
            tl = self.tm(w, 0, 512, j, lambda ps, t, j=j: self.act.copy(rv[:, j, :], ps, after=[t]), [tok])
        self.ring.free(s, tl)
        s, w, tok = self.wslot(W, 1952, 2464)
        for m in range(4):
            tl = self.fm(w, 128 * m, 128, 0, lambda ps, t, m=m: self.act.act(rg[:, m, :], ps, ACT.Silu, after=[t]), [tok])
        self.ring.free(s, tl)
        self.fence_keep()
        MIX = self.H
        mark = self.at
        tmp = (self.alloc(T), self.alloc(T))
        rt = self.alloc(TC)
        QH, KH = self.alloc(4, T), self.alloc(4, T)
        st = self.att_state(32)
        vu = lambda s: s[:, 0:1536].rearrange("p (k n) -> p k n", k=2)
        vk = lambda s: s[:, 1536:2560]
        s, tok = self.ring.load((vu, io["mla_w_uq_2"][0].rearrange("(k p) n -> p k n", p=128)),
                                (vk, io["mla_w_ukv_2"][0]))
        wu, wk = vu(self.slots[s]), vk(self.slots[s])
        i, ps, rd = self.bank(0, 4)
        for m in range(2):
            ta = self.act.act(tmp[m], cq[:, m, :], ACT.Square)
            tp = self.pe.mm(ps[:, :], self.c("ones"), tmp[m], m == 0, m == 1,
                            after=[ta] + rd, mark=True)
        te, tl = self.rstd(self.RS[:, :], ps[:, :], 256, [tp])
        self.read[i] = [tl]
        for m in range(2):
            tn = self.dve.stt(cq[:, m, :], cq[:, m, :], self.v("mq_n", m), self.RS[:, :], ALU.mult, ALU.mult, after=[te, tp])
        tk = self.rms_heads(ckv, "ones", 128, T, 128, self.v("mkv_n"), [tn], tmp, 0, 4)
        v3 = wk.rearrange("p (h x) -> p h x", x=128)[:, :, 64:128]
        for j in range(4):
            i, ps, rd = self.bank(0, 4)
            tm = self.pe.mm(ps[:, :].rearrange("p (h x) -> p h x", x=64), ckv[:, 128 * j:128 * j + 128], v3, True, True,
                            after=[tk, tok] + rd, mark=True)
            tv = self.act.copy(vv[:, j, :], ps[:, :], after=[tm])
            self.read[i] = [tv]
        free = []
        for half in range(2):
            prev = [tv, tk]
            for x in range(4):
                h = 4 * half + x
                q, k = QH[0:96, x, :], KH[0:96, x, :]
                got = []

                def outq(ps, t, q=q):
                    got.append(self.act.copy(q, ps, after=[t] + free))
                    return got[-1]

                self.fm(wu, 96 * h, 96, 0, outq, [tok, tn], 0, 4, K=2, rhs=lambda kk: cq[:, kk, :])
                i, ps, rd = self.bank(0, 4)
                tm = self.pe.mm(ps[0:64, :], wk[:, 128 * h:128 * h + 64], ckv, True, True, after=[tok, tk] + rd, mark=True)
                t1 = self.act.copy(KH[0:64, x, :], ps[0:64, :], after=[tm] + free)
                self.read[i] = [t1]
                t2 = self.pool.copy(KH[64:96, x, :], kr[64:96, :], after=free)
                for y, gain, dep in ((q, "mqn", [got[0]]), (k, "mkn", [t1, t2])):
                    t = self.rms_heads(y, "ones", 96, T, 96, self.v(gain)[0:96], dep + prev, tmp, 0, 4)
                    t = self.rope(y[:, TC:T], 96, "rotM", "cosM", "sinM", [t], rt, 0, 4)
                    prev = [t]
            self.ring.free(s, tm)
            for x in range(4):
                h = 4 * half + x
                pb = 64 * (h % 2)
                for q0, nq, nk in ((0, 2, TC), (TC, 2, T)):
                    self.attend(QH[:, x, :], KH[:, x, :], 96, 0, lambda j, h=h: vv[:, j, 64 * h:64 * h + 64],
                                lambda c, h=h, pb=pb, q0=q0: MIX[pb:pb + 64, h // 2, q0 + 128 * c:q0 + 128 * c + 128],
                                q0, nq, nk, 96 ** -0.5, prev, st, 0, 8, pb)
            free = [st["out"]]
        self.fence_keep()
        self.at = mark
        lg = self.alloc(6, 16)
        raw = self.v("lgf", 0, 16)
        y, w1, eq, num, den, lgm = (lg[:, j, :] for j in range(6))
        t = self.act.act(y, raw, ACT.Exp, scale=math.log(2.0))
        t = self.dve.ts(w1, y, -1.0, ALU.mult, 1.0, ALU.add, after=[t])
        te = self.dve.ts(eq, w1, 1.0, ALU.is_equal, after=[t])
        tl = self.act.act(num, w1, ACT.Ln, after=[t])
        tn = self.dve.add(num, num, eq, after=[te, tl])
        td = self.dve.stt(den, w1, 1.0, eq, ALU.subtract, ALU.add, after=[te])
        td = self.dve.do(lambda g: g.reciprocal(den, den), [td])
        t = self.dve.mul(num, num, den, after=[tn, td])
        t_lg = self.dve.stt(lgm, num, -1.0, y, ALU.mult, ALU.mult, after=[t])
        rt2 = self.alloc(TC)
        prev = []
        for x in (rq, rk):
            for m in range(4):
                t = self.rope(x[:, m, TC:T], 128, "rotR", "cosR", "sinR", prev, rt2, 0, 4)
                prev = [t]
        F, R_, DJ, t1 = self.alloc(T), self.alloc(T), [self.alloc(T), self.alloc(T)], self.alloc(128)
        PJ = self.alloc(4, T)
        o, sq, r = self.alloc(T), self.alloc(T), self.alloc(T)
        dfree, pfree, ofree, ffree = [], [], [], []
        B_ = lambda x, m: x[:, 128 * m:128 * m + 128]
        for m in range(4):
            oi, ops, ord_ = self.bank(6, 8)
            for hh in range(2):
                h, hb = 2 * m + hh, 64 * hh
                ta = self.act.act(F, self.c("distF"), ACT.Exp, scale=lgm[:, h:h + 1], after=[t_lg] + ffree)
                tb = self.act.act(R_, self.c("distR"), ACT.Exp, scale=lgm[:, 8 + h:9 + h], after=[t_lg] + ffree)
                g = self.pool
                a = [ta, tb] + dfree
                u1 = g.mul(t1, B_(F, 0), self.c("mF"), after=a)
                u2 = g.mul(B_(DJ[0], 0), B_(R_, 0), self.c("mR"), after=a)
                u3 = g.add(B_(DJ[0], 0), B_(DJ[0], 0), t1, after=[u1, u2])
                g.copy(B_(DJ[1], 1), B_(DJ[0], 0), after=[u3])
                g.copy(B_(DJ[0], 1), B_(F, 1))
                g.copy(B_(DJ[1], 0), B_(R_, 1))
                g.add(B_(DJ[0], 2), B_(F, 2), B_(R_, 2))
                g.add(B_(DJ[1], 3), B_(F, 2), B_(R_, 2))
                g.add(B_(DJ[0], 3), B_(F, 3), B_(R_, 1))
                td = g.add(B_(DJ[1], 2), B_(F, 1), B_(R_, 3))
                ffree = [td]
                tp = []
                for J in range(4):
                    a0 = 0 if J < 2 else TC
                    i, ps, rd = self.bank(0, 4)
                    tm = self.pe.mm(ps[:, a0:T], rk[hb:hb + 64, m, 128 * J:128 * J + 128], rq[hb:hb + 64, m, a0:T], True, True,
                                    after=prev + rd, mark=True)
                    tp.append(self.dve.mul(PJ[:, J, a0:T], ps[:, a0:T], DJ[J % 2][:, 0:T - a0], after=[tm, td] + pfree))
                    self.read[i] = [tp[-1]]
                dfree = [tp[-1]]
                for J in range(4):
                    a0 = 0 if J < 2 else TC
                    tm = self.pe.mm(ops[hb:hb + 64, a0:T], rv[:, J, 64 * h:64 * h + 64], PJ[:, J, a0:T], J == 0, J == 3,
                                    after=[tp[J]] + ord_, mark=(J == 3))
                pfree = [tm]
            to = self.act.copy(o, ops[:, :], after=[tm] + ofree)
            self.read[oi] = [to]
            i, ps, rd = self.bank(4, 6)
            tp = self.pe.mm(ps[:, :], self.c("bd"), o, True, True, after=[to] + rd, mark=True)
            tm_ = self.dve.stt(o, ps[:, :], -1.0 / 64, o, ALU.mult, ALU.add, after=[tp])
            self.read[i] = [tm_]
            ta = self.act.act(sq, o, ACT.Square, after=[tm_])
            i, ps, rd = self.bank(4, 6)
            tp = self.pe.mm(ps[:, :], self.c("bd"), sq, True, True, after=[ta] + rd, mark=True)
            te, tl = self.rstd(r, ps[:, :], 64, [tp] + ofree)
            self.read[i] = [tl]
            t = self.dve.mul(o, o, r, after=[te, ta])
            t = self.dve.mul(MIX[:, 4 + m, :], o, rg[:, m, :], after=[t])
            ofree = [t]
        self.fence()
        if self.stop == "mlamix":
            return
        Y = self.alloc(KT, T)
        ys = self.down(io["w_out_2"][0], None, T, lambda k: MIX[:, k, :], 8, [[]] * 8, Y)
        self.fence_keep()
        self.resid(Y, 0, 1, False, ys)

    def cmul(self, o, a, b, t1, t2, after, sign=1):
        g, h = self.dve, self.pool
        x1 = g.mul(o[0], a[0], b[0], after=after)
        x2 = h.mul(t1, a[1], b[1], after=after)
        x3 = g.mul(o[1], a[0], b[1], after=after)
        x4 = h.mul(t2, a[1], b[0], after=after)
        ops = (ALU.subtract, ALU.add) if sign == 1 else (ALU.add, ALU.subtract)
        y1 = g.tt(o[0], o[0], t1, ops[0], after=[x1, x2])
        y2 = g.tt(o[1], o[1], t2, ops[1], after=[x3, x4])
        return y2

    def s5(self):
        io = self.io
        TC2 = TC // 8
        self.fence()
        self.norm_mod(0, 0, 0)
        self.fence()
        big = self.alloc(9216)
        Vr, Vi, Pr, Pi, T1, T2 = (self.alloc(2048) for _ in range(6))
        sm = self.alloc(12, 32)
        aw = self.alloc(2, 9, 32)
        sl = [self.ring.scratch() for _ in range(3)]
        LW = self.slots[sl[0][0]][:, :].rearrange("p (f t x) -> p f t x", f=4, t=8)
        sb_ = self.slots[sl[1][0]][:, :].rearrange("p (i q x) -> p i q x", i=4, q=32)
        Bb, Cc = (sb_[:, 0], sb_[:, 1]), (sb_[:, 2], sb_[:, 3])
        sc_ = self.slots[sl[2][0]]
        Br = [sc_[:, 1024 * i:1024 * i + 1024].rearrange("p (q x) -> p q x", q=32) for i in range(2)]
        Y = sc_[:, 2048:4096].rearrange("p (f n) -> p f n", f=8)
        fr = sl[0][1] + sl[1][1] + sl[2][1]
        U = self.H
        ldt = self.alloc(3, 32)
        bd32 = self.c("bd32")
        v3 = lambda x: x.rearrange("p (q n) -> p q n", q=32)
        free = fr
        for d in range(2):
            if d:
                self.fence_keep()
                free = self.phase
            self.sp.dma(ldt, io["s5v"][d].rearrange("i p q -> p i q"), self.s_ld, free)
            self.sp.dma(sb_[:, 2:4], io["s5m"][d][2:4].rearrange("i p q x -> p i q x"), self.s_ld, free)
            for i in range(2):
                self.sp.dma(Br[i], io["s5m"][d][i], self.s_ld, free)
            self.n_ld += 64
            tl = [(self.s_ld, self.n_ld)]
            V_, A_ = self.dve, self.act
            ar, ai, ld = (ldt[:, i, :] for i in range(3))
            dt, re, th, mag, c, s, k, r8, x, y, fre, fim = (sm[:, i, :] for i in range(12))
            t = A_.act(dt, ld, ACT.Exp, after=tl)
            t1 = V_.mul(re, dt, ar, after=[t])
            t = V_.mul(th, dt, ai, after=[t])
            tm = A_.act(mag, re, ACT.Exp, after=[t1])
            t8 = A_.act(r8, re, ACT.Exp, scale=8.0, after=[t1])
            t = V_.ts(k, th, float(np.float32(1 / (2 * math.pi))), ALU.mult, after=[t])
            t = V_.ts(k, k, 12582912.0, ALU.add, after=[t])
            t = V_.ts(k, k, -12582912.0, ALU.add, after=[t])
            for part in (6.28125, 0.0019350051879882812, 3.0199159819e-07):
                t = V_.stt(th, k, -part, th, ALU.mult, ALU.add, after=[t])
            t = V_.ts(th, th, 3.1415925, ALU.min, -3.1415925, ALU.max, after=[t])
            ts = A_.act(s, th, ACT.Sin, after=[t])
            t = A_.act(x, th, ACT.Abs, after=[t])
            t = V_.ts(x, x, -1.0, ALU.mult, float(np.float32(math.pi / 2)), ALU.add, after=[t])
            tc = A_.act(c, x, ACT.Sin, after=[t])
            p = lambda j: (aw[:, 0, j, :], aw[:, 1, j, :])
            t = V_.do(lambda e: e.memset(aw[:, 0, 0, :], 1.0))
            t0 = V_.zero(aw[:, 1, 0, :])
            t = V_.mul(aw[:, 0, 1, :], mag, c, after=[tm, tc])
            t = V_.mul(aw[:, 1, 1, :], mag, s, after=[tm, ts])
            for j in range(2, 9):
                t = self.cmul(p(j), p(1), p(j - 1), x, y, [t])
            tp = [t, t0]
            t = V_.ts(x, aw[:, 0, 1, :], -1.0, ALU.add, after=[t])
            ta = V_.mul(fre, x, ar, after=[t])
            tb = V_.mul(y, aw[:, 1, 1, :], ai, after=[t])
            tr = V_.add(fre, fre, y, after=[ta, tb])
            ta = V_.mul(fim, aw[:, 1, 1, :], ar, after=[tr])
            tb = V_.mul(x, x, ai, after=[tr])
            ti = V_.sub(fim, fim, x, after=[ta, tb])
            ta = V_.mul(x, ar, ar, after=[ti])
            tb = V_.mul(y, ai, ai, after=[ti])
            t = V_.add(x, x, y, after=[ta, tb])
            t = V_.do(lambda e: e.reciprocal(x, x), [t])
            ta = V_.mul(fre, fre, x, after=[t])
            tb = V_.mul(fim, fim, x, after=[t])
            bc = lambda q, n=32: q.unsqueeze(2).broadcast_to([128, 32, n])
            b1, b2 = (z[:, 0:1024].rearrange("p (q x) -> p q x", q=32) for z in (T1, T2))
            tB = self.cmul(Bb, (bc(fre), bc(fim)), Br, b1, b2, [ta, tb] + tl)
            tC = V_.ts(Cc[1], Cc[1], -1.0, ALU.mult, after=tl)
            P3 = (v3(Pr), v3(Pi))
            w = [(x, y), (c, s)]
            cur = (c, s)
            t = [tb, ts, tc, tB]
            nxt = (x, y)
            for _ in range(3):
                t = [self.cmul(nxt, cur, cur, k, th, t)]
                cur, nxt = nxt, cur
            tq = V_.do(lambda e: e.memset(P3[0][:, :, 0:1], 1.0), free)
            tq = V_.zero(P3[1][:, :, 0:1])
            t = t + [tq]
            b1, b2 = v3(T1), v3(T2)
            for lv in range(6):
                n = 1 << lv
                o = tuple(q[:, :, n:2 * n] for q in P3)
                a = tuple(q[:, :, 0:n] for q in P3)
                t = [self.cmul(o, (bc(cur[0], n), bc(cur[1], n)), a, b1[:, :, 0:n], b2[:, :, 0:n], t)]
                if lv < 5:
                    t = [self.cmul(nxt, cur, cur, k, th, t)]
                    cur, nxt = nxt, cur
            tP = t
            W = big[:, 0:8192].rearrange("p (f s i x) -> p f s i x", f=4, s=8, i=2)
            room = [[z[:, 512 * i:512 * i + 512] for i in range(4)] for z in (T1, T2)]
            rfree = [tP, tP]
            wfree = list(tP)
            for fh in range(2):
                fs = slice(4 * fh, 4 * fh + 4)
                q4 = lambda z: z.rearrange("p (j f) x -> p j (f x)", j=4)[:, :, 128 * fh:128 * fh + 128]
                a4 = lambda z: z.rearrange("p (j f) -> p j f", j=4)[:, :, fs].unsqueeze(3).broadcast_to([128, 4, 4, 32])
                f4 = lambda z: z.rearrange("p (f j x) -> p j f x", j=4, f=4)
                c4 = lambda z: z.rearrange("p (j f) x -> p j f x", j=4)[:, :, fs, :]
                tw = []
                for s_ in range(8):
                    rm = room[s_ % 2]
                    pw = p(7 - s_)
                    t = self.cmul((f4(rm[0]), f4(rm[1])), (a4(pw[0]), a4(pw[1])), (c4(Bb[0]), c4(Bb[1])),
                                  f4(rm[2]), f4(rm[3]), [tB] + tp + rfree[s_ % 2])
                    for i in range(2):
                        bi, ps, rd = self.bank(0, 8)
                        for f in range(4):
                            lh = rm[i][:, 128 * f:128 * f + 128]
                            tm = self.pe.mm(ps[:, 128 * f:128 * f + 128], lh, self.c("ident"), True, True,
                                            after=[t] + rd, mark=(f == 3))
                        te = self.act.copy(W[:, :, s_, i, :], ps[:, :].rearrange("p (f x) -> p f x", f=4),
                                           after=[tm] + wfree)
                        self.read[bi] = [te]
                    rfree[s_ % 2] = [tm]
                for j in range(4):
                    for i in range(2):
                        b = 4 * i + j
                        ps = self.ps[b]
                        for f in range(4):
                            for s_ in range(8):
                                u = U[32 * j:32 * j + 32, 4 * fh + f, :]
                                if d == 0:
                                    u = u.rearrange("p (n s) -> p n s", s=8)[:, :, s_]
                                    o = ps[:, 64 * f:64 * f + 64]
                                else:
                                    u = u.rearrange("p (g n) -> p g n", g=2)[:, :, 255 - s_::-8]
                                    o = ps[:, 64 * f:64 * f + 64].rearrange("p (g n) -> p g n", g=2)
                                tm = self.pe.mm(o, W[32 * j:32 * j + 32, f, s_, i, :], u, s_ == 0, s_ == 7,
                                                after=[te] + self.read[b], mark=(f == 3 and s_ == 7))
                        dst = (Vr, Vi)[i].rearrange("p (j f n) -> p j (f n)", j=4, f=8)[:, j, 256 * fh:256 * fh + 256]
                        lane = (self.act, self.dve)[i]
                        t = lane.copy(dst, ps[:, 0:256], after=[tm] + free)
                        self.read[b] = [t]
                        tw.append(t)
                wfree = [tm]
                if fh == 0:
                    tv = list(tw)
            tv = tv + tw
            pr, pi = Pr, Pi
            al = tv + tP + rfree[0] + rfree[1]
            g, h = self.dve, self.pool
            x1 = g.mul(T1, pr, Vr, after=al)
            x2 = h.mul(T2, pi, Vi, after=al)
            y1 = g.add(T1, T1, T2, after=[x1, x2])
            x3 = g.mul(T2, pr, Vi, after=[y1])
            x4 = h.mul(Vr, pi, Vr, after=[x1])
            y2 = g.sub(T2, T2, Vr, after=[x3, x4])
            tr_ = g.copy(v3(Vi), r8.unsqueeze(2).broadcast_to([128, 32, 64]), after=[x2, x3, t8])
            tr_ = g.zero(v3(Vi)[:, :, 0:1], after=[tr_])
            z1 = g.do(lambda e: e.tensor_tensor_scan(Vr, Vi, T1, 0.0, ALU.mult, ALU.add), [tr_, y1, y2])
            z2 = g.do(lambda e: e.tensor_tensor_scan(T1, Vi, T2, 0.0, ALU.mult, ALU.add), [z1, y2])
            x1 = h.mul(T2, pi, T1, after=[z2])
            x2 = g.mul(Vi, pr, Vr, after=[z2])
            y1 = g.sub(Vi, Vi, T2, after=[x1, x2])
            x3 = g.mul(T2, pr, T1, after=[y1])
            x4 = h.mul(Vr, pi, Vr, after=[x2])
            tx = g.add(Vr, Vr, T2, after=[x3, x4])
            XR, XI = v3(Vi), v3(Vr)
            CA = [big[:, 4608 * i:4608 * i + 4608].rearrange("p (k j f x) -> p k j f x", k=9, j=4, f=4) for i in range(2)]
            cfree = [tm, tx]
            rfree = [[tx], [tx]]
            lfree = []
            for fh in range(2):
                fs = slice(4 * fh, 4 * fh + 4)
                a4 = lambda z: z.rearrange("p (j f) -> p j f", j=4)[:, :, fs].unsqueeze(3).broadcast_to([128, 4, 4, 32])
                c4 = lambda z: z.rearrange("p (j f) x -> p j f x", j=4)[:, :, fs, :]
                f4 = lambda z: z.rearrange("p (f j x) -> p j f x", j=4, f=4)
                for k_ in range(9):
                    rm = room[k_ % 2]
                    pw = p(k_)
                    t = self.cmul((CA[0][:, k_], CA[1][:, k_]), (a4(pw[0]), a4(pw[1])), (c4(Cc[0]), c4(Cc[1])),
                                  f4(rm[2]), f4(rm[3]), [tC] + tp + cfree + rfree[k_ % 2], sign=-1)
                    rfree[k_ % 2] = [t]
                tl_ = []
                for f in range(4):
                    bi, ps, rd = self.bank(0, 4)
                    for j in range(4):
                        q = 8 * j + 4 * fh + f
                        for i in range(2):
                            tm = self.pe.mm(ps[32 * j:32 * j + 32, 0:256].rearrange("p (t x) -> p t x", x=32),
                                            Bb[i][:, q, :], CA[i][:, 0:8, j, f, :], i == 0, i == 1,
                                            after=[t, tB] + rd, mark=(j == 3 and i == 1))
                    src = ps[:, 0:256].rearrange("p (t x) -> p t x", x=32).unsqueeze(2).broadcast_to([128, 8, 4, 32])
                    mk = bd32.rearrange("p (j x) -> p j x", j=4).unsqueeze(1).broadcast_to([128, 8, 4, 32])
                    tl_.append(self.dve.mul(LW[:, f].rearrange("p t (j x) -> p t j x", j=4), src, mk,
                                            after=[tm] + lfree + free))
                    self.read[bi] = [tl_[-1]]
                for f in range(4):
                    F_ = 4 * fh + f
                    bi, ps, rd = self.bank(4, 8)
                    lat = U[:, F_, TC:T] if d == 0 else U[:, F_, T - 1:TC - 1:-1]
                    lat = lat.rearrange("p (n s) -> p s n", s=8)
                    o = ps[:, 0:256].rearrange("p (s n) -> p s n", s=8)
                    for tau in range(8):
                        self.pe.mm(o[:, tau:8, :], LW[:, f, tau, :], lat[:, 0:8 - tau, :], tau == 0, False,
                                   after=[tl_[f]] + rd)
                    for j in range(4):
                        q = 8 * j + F_
                        for s_ in range(8):
                            for i, XX in enumerate((XR, XI)):
                                tm = self.pe.mm(o[32 * j:32 * j + 32, s_, :], CA[i][:, s_ + 1, j, f, :],
                                                XX[:, q, 31:63], False, s_ == 7 and i == 1, after=[tx],
                                                mark=(j == 3 and s_ == 7 and i == 1))
                    yf = Y[:, F_, :]
                    if d == 0:
                        ty = self.dve.copy(yf.rearrange("p (n s) -> p s n", s=8), o, after=[tm] + free)
                    else:
                        yv = yf[:, 255::-1].rearrange("p (n s) -> p s n", s=8)
                        ty = self.dve.add(yv, o, yv, after=[tm])
                    self.read[bi] = [ty]
                cfree = lfree = [tm]
        self.fence_keep()
        self.at = 0
        G = self.alloc(KT, TC)
        O = self.alloc(KT, TC)
        sgm = [self.alloc(TC), self.alloc(TC)]
        tg = []
        for f in range(8):
            t = self.dve.stt(Y[:, f, :], U[:, f, TC:T], self.v("s5d", f), Y[:, f, :], ALU.mult, ALU.add)
            tg.append(self.act.act(G[:, f, :], Y[:, f, :], ACT.Gelu_apprx_tanh, after=[t]))
        for i, _ in sl:
            self.ring.free(i, tg[-1])
        sfree = [[], []]
        ys = []
        for g_ in range(4):
            view = lambda s: s[:, :].rearrange("p (u k n) -> p u k n", u=2, k=KT)
            Wg = io["s5_w_glu_2"][0]
            s, tok = self.ring.load(*[
                (lambda s, a=a: view(s)[:, a], Wg[:, D * a + 256 * g_:D * a + 256 * g_ + 256].rearrange("(k p) n -> p k n", p=128))
                for a in range(2)])
            w = view(self.slots[s])
            for m in range(2):
                xx = 2 * g_ + m

                def zb(ps, t, xx=xx):
                    t = self.act.act(sgm[xx % 2], ps, ACT.Sigmoid, after=[t] + sfree[xx % 2])
                    sfree[xx % 2] = [t]
                    return t

                def za(ps, t, xx=xx):
                    t = self.dve.mul(O[:, xx, :], ps, sgm[xx % 2], after=[t] + sfree[xx % 2])
                    sfree[xx % 2] = [t]
                    ys.append(t)
                    return t

                rh = lambda k: G[:, k, :]
                self.fm(w[:, 1], 128 * m, 128, TC, zb, [tok, tg[-1]], 0, 6, rhs=rh)
                tm = self.fm(w[:, 0], 128 * m, 128, TC, za, [tok, tg[-1]], 0, 6, rhs=rh)
            self.ring.free(s, tm)
        if self.stop == "s5mix":
            for f in range(8):
                self.dve.copy(self.H[:, f, TC:T], O[:, f, :], after=ys)
            return
        self.resid(O, TC, 1, False, ys)


def constants():
    c = np.zeros((128, NCST), np.float32)

    def put(name, a, rows=128):
        at, n = CST[name]
        c[:rows, at:at + a.shape[1]] = a

    p = np.arange(128)
    x = np.arange(512)
    put("ident", np.eye(128, dtype=np.float32))
    put("ones", np.ones((128, 128), np.float32))
    put("bd", (p[:, None] // 64 == p[None, :] // 64).astype(np.float32))
    put("bd32", (p[:, None] // 32 == p[None, :] // 32).astype(np.float32))
    r = np.zeros((128, 128), np.float32)
    r[p[1::2], p[0::2]] = -1
    r[p[0::2], p[1::2]] = 1
    put("rotE", r)
    r = np.zeros((128, 128), np.float32)
    a = 64 + np.arange(16)
    r[a + 16, a] = -1
    r[a, a + 16] = 1
    put("rotM", r)
    r = np.zeros((128, 128), np.float32)
    a = np.concatenate([np.arange(32), 64 + np.arange(32)])
    r[a + 32, a] = -1
    r[a, a + 32] = 1
    put("rotR", r)
    m = np.ones((128, 516), np.float32)
    m[:, ::129] = 0
    put("smask", m)
    put("distF", np.maximum(x[None] - p[:, None], 0).astype(np.float32))
    put("distR", np.maximum(128 * (x[None] // 128) + p[:, None] - x[None] % 128, 0).astype(np.float32))
    put("mF", (p[None] >= p[:, None]).astype(np.float32))
    put("mR", (p[:, None] > p[None]).astype(np.float32))
    f4 = np.float32
    n = np.arange(256)
    row, col = (n // 64).astype(f4), (n % 64).astype(f4)
    inv = (f4(10000.0) ** (-np.arange(0, 32, 2, dtype=f4) / f4(32))).astype(f4)
    ang = np.concatenate([row[:, None] * inv, col[:, None] * inv], -1).astype(f4)
    fe = (p % 64) // 2
    put("cosE", np.cos(ang)[:, fe].T.astype(f4))
    put("sinE", np.sin(ang)[:, fe].T.astype(f4))
    f = (f4(10000.0) ** (-np.arange(8, dtype=f4) / f4(8))).astype(f4)
    ang = np.concatenate([row[:, None] * f, col[:, None] * f], -1).astype(f4)
    co, si = np.ones((128, 256), f4), np.zeros((128, 256), f4)
    for half in range(2):
        co[64 + 16 * half:80 + 16 * half] = np.cos(ang).T
        si[64 + 16 * half:80 + 16 * half] = np.sin(ang).T
    put("cosM", co)
    put("sinM", si)
    th = (f4(10000.0) ** (-np.arange(32, dtype=f4) / f4(32))).astype(f4)
    ang = (n.astype(f4)[:, None] * th).astype(f4)
    put("cosR", np.cos(ang)[:, p % 32].T.astype(f4))
    put("sinR", np.sin(ang)[:, p % 32].T.astype(f4))
    k = np.zeros((128, 15, 128), np.float32)
    for li, L in enumerate(LEVELS):
        same = p[:, None] // (2 * L) == p[None] // (2 * L)
        late = (p // L) % 2 == 1
        k[:, li] = same & ~late[:, None] & late[None]
        k[:, 7 + li] = same & late[:, None] & ~late[None]
    k[:, 14] = np.eye(128)
    return c, k


def layouts(a):
    f = lambda x: np.ascontiguousarray(x)
    vec = np.zeros((128, NVEC), np.float32)

    def put(name, x, rows=128):
        at, n = VEC[name]
        assert x.shape == (rows, n), (name, x.shape)
        vec[:rows, at:at + n] = x

    col = lambda x: np.asarray(x).reshape(-1, 128).T
    put("c", col(a["c"]))
    put("cc", col(a["c_ctx"]))
    put("c2", col(a["c_2"]))
    put("cc2", col(a["c_ctx_2"]))
    put("mod_b", col(a["mod_b"]))
    put("ada_b", col(a["ada_b_2"]))
    for n, m in (("pre_mix", "norm_pre_mix"), ("post_mix", "norm_post_mix"), ("pre_ffn", "norm_pre_ffn"),
                 ("post_ffn", "norm_post_ffn"), ("n1", "norm1_g_2"), ("n2", "norm2_g_2"), ("gla_b", "gla_b_gate"),
                 ("gla_n", "gla_out_norm"), ("lb", "hgrn_lower_bounds"), ("hg_n", "hgrn_out_norm"),
                 ("mq_n", "mla_q_norm_g_2"), ("mkv_n", "mla_kv_norm_g_2"), ("s5d", "s5_d_2")):
        put(n, col(a[m]))
    put("aq_n", np.tile(np.asarray(a["att_q_norm"]).reshape(64, 1), (2, 1)))
    put("ak_n", np.tile(np.asarray(a["att_k_norm"]).reshape(64, 1), (2, 1)))
    put("mqn", np.asarray(a["mla_qn_g_2"]).reshape(96, 1), 96)
    put("mkn", np.asarray(a["mla_kn_g_2"]).reshape(96, 1), 96)
    put("lgf", np.tile(np.asarray(a["ret_lg_f_2"]).reshape(1, 8), (128, 1)))
    put("lgb", np.tile(np.asarray(a["ret_lg_b_2"]).reshape(1, 8), (128, 1)))
    put("eps", np.full((128, 1), EPS, np.float32))
    put("one", np.ones((128, 1), np.float32))
    gw = np.zeros((32, 2, 256), np.float32)
    for d in range(2):
        gw[16 * d:16 * d + 16, d] = np.asarray(a["gla_w_gate"])[0, d]
    fm = lambda x: np.asarray(x).reshape(-1, 8, 128).transpose(2, 1, 0)
    xT = np.concatenate([fm(a["ctx"]), fm(a["x"])], 2)
    cst, msk = constants()
    out = {"vec": vec, "cst": cst, "msk": msk, "xT": f(xT), "x2T": f(fm(a["ctx_2"])), "gla_gw": gw.reshape(32, 512)}
    g = np.array([[8 * ff + 2 * j + h for h in range(2)] for j in range(4) for ff in range(8)])
    s5v = np.zeros((2, 3, 128, 32), np.float32)
    s5m = np.zeros((2, 4, 128, 32, 32), np.float32)
    for i, d in enumerate("fb"):
        for n, name in enumerate(("s5_a_re_", "s5_a_im_")):
            x = np.asarray(a[name + d + "_2"])[0]
            s5v[i, n] = x[g].transpose(1, 2, 0).reshape(128, 32)
        s5v[i, 2] = np.repeat(np.asarray(a["s5_log_dt_" + d + "_2"])[0][g].T, 64, 0)
        for n, name in enumerate(("s5_b_re_", "s5_b_im_", "s5_c_re_", "s5_c_im_")):
            x = np.asarray(a[name + d + "_2"])[0][g]
            if n >= 2:
                x = x.transpose(0, 1, 3, 2)
            for h in range(2):
                s5m[i, n, 64 * h:64 * h + 64, :, 16 * h:16 * h + 16] = x[:, h].transpose(1, 0, 2)
    out["s5v"], out["s5m"] = s5v, s5m
    for name in WEIGHTS:
        out[name] = f(np.asarray(a[name]))
    return out


WEIGHTS = ("mod_w", "even_w_in", "even_w_out", "odd_w_in", "odd_w_out", "ffn_w_gate", "ffn_w_up", "ffn_w_down",
           "ada_w_2", "mlp_w1_2", "mlp_w2_2", "w_in_2", "mla_w_uq_2", "mla_w_ukv_2", "w_out_2", "s5_w_glu_2")


def build(nc, shapes, stop=None):
    io = {}
    for name, (shape, dt) in shapes.items():
        io[name] = nc.dram_tensor(name, shape, dt, kind="ExternalInput").ap()
    n = T if stop else TC
    io["outX"] = nc.dram_tensor("outX", (128, KT, n), F32, kind="ExternalOutput").ap()
    with ExitStack() as ctx:
        p = Program(nc, ctx, io, stop)
        run_program(p, stop)


def run_program(p, stop):
    steps = [
        ("even", lambda: (p.begin(), p.mods(p.io["mod_w"], "mod_b", 0, 0, "pre_mix", "post_mix", "pre_ffn", "post_ffn"),
                          p.even())),
        ("ffn0", lambda: p.ffn_swiglu(0, 0)),
        ("odd", lambda: (p.mods(p.io["mod_w"], "mod_b", 0, 1, "pre_mix", "post_mix", "pre_ffn", "post_ffn"), p.odd())),
        ("ffn1", lambda: p.ffn_swiglu(1, TC)),
        ("mla", lambda: (p.mods(p.io["ada_w_2"], "ada_b", 1, 0, "n1", None, "n2", None), p.mla())),
        ("mlp0", lambda: p.ffn_sq(0, 0)),
        ("s5", lambda: (p.mods(p.io["ada_w_2"], "ada_b", 1, 1, "n1", None, "n2", None), p.s5())),
        ("mlp1", lambda: p.ffn_sq(1, TC)),
    ]
    for name, f in steps:
        f()
        if stop and name == stop.replace("mix", ""):
            break
    p.finish()


def kernel(**inputs):
    import concourse.bacc as bacc
    from concourse.bass_utils import run_bass_kernel_spmd

    arrays = layouts(inputs)
    nc = bacc.Bacc("TRN2", target_bir_lowering=False, num_devices=1)
    build(nc, {n: (x.shape, mybir.dt.from_np(x.dtype)) for n, x in arrays.items()})
    r = run_bass_kernel_spmd(nc, [arrays], core_ids=[0])
    out = r.results[0]["outX"]
    return np.ascontiguousarray(out.transpose(2, 1, 0).reshape(1, TC, D))
```

```python
from contextlib import ExitStack
import itertools
import math

import numpy as np

import concourse.bass as bass
from concourse import mybir

F32 = mybir.dt.float32
U8 = mybir.dt.uint8
ALU = mybir.AluOpType
ACT = mybir.ActivationFunctionType
AX = mybir.AxisListType

D = 1024
KT = 8
T = 512
TC = 256
FF1 = 2816
FF2 = 4096
EPS = 1e-6
LEVELS = (64, 32, 16, 8, 4, 2, 1)

VEC = {}


def _vec_layout():
    at = 0
    for name, n in (
        ("c", 8), ("cc", 8), ("c2", 8), ("cc2", 8),
        ("mod_b", 96), ("ada_b", 96),
        ("pre_mix", 16), ("post_mix", 16), ("pre_ffn", 16), ("post_ffn", 16),
        ("n1", 16), ("n2", 16),
        ("gla_b", 4), ("gla_n", 1), ("aq_n", 1), ("ak_n", 1),
        ("lb", 32), ("hg_n", 1),
        ("mq_n", 2), ("mkv_n", 1), ("mqn", 1), ("mkn", 1),
        ("lgf", 8), ("lgb", 8), ("s5d", 8), ("eps", 1), ("one", 1),
    ):
        VEC[name] = (at, n)
        at += n
    return at


NVEC = _vec_layout()

CST = {}


def _cst_layout():
    at = 0
    for name, n in (
        ("ident", 128), ("ones", 128), ("bd", 128), ("rotE", 128), ("rotM", 128), ("rotR", 128),
        ("smask", 516), ("distF", 512), ("distR", 512), ("mF", 128), ("mR", 128), ("bd32", 128),
        ("cosE", 256), ("sinE", 256), ("cosM", 256), ("sinM", 256), ("cosR", 256), ("sinR", 256),
    ):
        CST[name] = (at, n)
        at += n
    return at


NCST = _cst_layout()


class Lane:

    def __init__(self, name, sem):
        self.name, self.sem, self.items, self.n, self.held = name, sem, [], 0, []

    def do(self, f, after=(), mark=True, inc=1, sem=None):
        waits = list(after) + self.held
        self.held = []
        if mark:
            self.n += 1
        self.items.append([waits, f, self.sem if mark else None, 1])
        return (self.sem, self.n)

    def dma(self, out, in_, sem, after=()):
        waits = list(after) + self.held
        self.held = []
        self.items.append([waits, lambda e: e.dma_start(out, in_), sem, 16])

    def last(self):
        if self.items and self.items[-1][2] is None:
            self.n += 1
            self.items[-1][2] = self.sem
        return (self.sem, self.n)

    def play(self, e):
        seen = {}
        for waits, f, sem, inc in self.items:
            need = {}
            for s, v in waits:
                if v > need.get(id(s), (s, 0))[1]:
                    need[id(s)] = (s, v)
            for k, (s, v) in need.items():
                if v > seen.get(k, 0):
                    e.wait_ge(s, v)
                    seen[k] = v
            if f is not None:
                i = f(e)
                if sem is not None:
                    i.then_inc(sem, inc)


class Vec(Lane):
    def tt(self, out, a, b, op, after=()):
        return self.do(lambda e: e.tensor_tensor(out, a, b, op), after)

    def mul(self, out, a, b, after=()):
        return self.tt(out, a, b, ALU.mult, after)

    def add(self, out, a, b, after=()):
        return self.tt(out, a, b, ALU.add, after)

    def sub(self, out, a, b, after=()):
        return self.tt(out, a, b, ALU.subtract, after)

    def ts(self, out, a, s1, op0, s2=None, op1=None, after=()):
        if op1 is None:
            return self.do(lambda e: e.tensor_scalar(out, a, s1, None, op0), after)
        return self.do(lambda e: e.tensor_scalar(out, a, s1, s2, op0, op1), after)

    def stt(self, out, a, s, b, op0, op1, after=()):
        return self.do(lambda e: e.scalar_tensor_tensor(out=out, in0=a, scalar=s, in1=b, op0=op0, op1=op1), after)

    def copy(self, out, a, after=()):
        return self.do(lambda e: e.tensor_copy(out, a), after)

    def zero(self, out, after=()):
        return self.do(lambda e: e.memset(out, 0.0), after)


LN_EXP = "natural_log_exp_and_others"
TABLES = {ACT.Exp: LN_EXP, ACT.Ln: LN_EXP, ACT.Sigmoid: "sigmoid_and_others", ACT.Silu: "silu_and_others",
          ACT.Sin: "silu_and_others", ACT.Gelu_apprx_tanh: "gelu_apprx_tanh_and_others"}


class Act(Lane):
    table = None

    def need(self, func):
        t = TABLES.get(func)
        if t and t != self.table:
            self.table = t
            held, self.held = self.held, []
            self.do(lambda e: e.preload_act_table_set(t), mark=False)
            self.held = held

    def act(self, out, a, func, scale=1.0, bias=0.0, accum=None, after=()):
        self.need(func)
        if accum is None:
            return self.do(lambda e: e.activation(out, a, func, bias=bias, scale=scale), after)
        return self.do(lambda e: e.activation(out, a, func, bias=bias, scale=scale, accum_out=accum), after)

    def copy(self, out, a, after=()):
        return self.do(lambda e: e.activation(out, a, ACT.Copy), after)


class Pe(Lane):
    def mm(self, out, lhsT, rhs, start, stop, after=(), mark=False):
        return self.do(lambda e: e.matmul(out, lhsT, rhs, start=start, stop=stop, skip_group_check=True), after, mark)

    def tr(self, out, a, ident, after=(), mark=False):
        return self.do(lambda e: e.transpose(out, a, ident), after, mark)


class Ring:

    def __init__(self, sp, slots, sems):
        self.sp, self.slots, self.sems = sp, slots, sems
        self.held = set()
        self.at, self.count, self.users = 0, [0] * len(slots), [[] for _ in slots]

    def next(self):
        while self.at % len(self.slots) in self.held:
            self.at += 1
        self.at += 1
        return (self.at - 1) % len(self.slots)

    def load(self, *parts):
        i = self.next()
        for k, (view, src) in enumerate(parts):
            self.sp.dma(view(self.slots[i]), src, self.sems[i], self.users[i] if k == 0 else ())
            self.count[i] += 16
        return i, (self.sems[i], self.count[i])

    def free(self, i, *tokens):
        self.users[i] = list(tokens)
        self.held.discard(i)

    def scratch(self):
        i = self.next()
        self.held.add(i)
        return i, list(self.users[i])


class Program:
    def __init__(self, nc, ctx, io, stop=None):
        self.nc, self.ctx, self.io, self.stop = nc, ctx, io, stop
        sem = lambda n: ctx.enter_context(nc.semaphore(n))
        self.sb = lambda n, shape, dt=F32: ctx.enter_context(nc.sbuf_tensor("sb_" + n, shape, dt))
        self.pe, self.act, self.dve, self.pool, self.sp = (
            Pe("pe", sem("pe_n")), Act("act", sem("act_n")), Vec("dve", sem("dve_n")),
            Vec("pool", sem("pool_n")), Lane("sp", sem("sp_n")))
        self.vec = self.sb("vec", [128, NVEC])
        self.cst = self.sb("cst", [128, NCST])
        self.msk = self.sb("msk", [128, 15, 128], U8)
        self.X = self.sb("X", [128, KT, T])
        self.H = self.sb("H", [128, KT, T])
        self.SX = self.sb("SX", [128, 2, KT, 2])
        self.MM = [self.sb(f"M{i}", [128, 48, 2]) for i in range(2)]
        self.COS = [self.sb(f"CO{i}", [128, 4, 2, KT]) for i in range(2)]
        self.t_cos = [None, None]
        self.RW = self.sb("RW", [128, 512])
        self.RS = self.sb("RS", [128, T])
        self.NW = 22816 - 512 - 160
        self.R = self.sb("R", [128, self.NW])
        self.slots = [self.sb(f"slot{i}", [128, 4096]) for i in range(4)]
        self.ring = Ring(self.sp, self.slots, [sem(f"ring{i}") for i in range(4)])
        self.ps = [ctx.enter_context(nc.psum_tensor(f"ps{i}", [128, 512], F32)) for i in range(8)]
        self.drained = [[] for _ in range(8)]
        self.turn = {}
        self.s_in, self.s_x, self.s_ld, self.s_out = sem("s_in"), sem("s_x"), sem("s_ld"), sem("s_out")
        self.n_ld = 0
        self.at = 0

    def alloc(self, *shape):
        n = int(np.prod(shape))
        assert self.at + n <= self.NW, (self.at, n)
        v = self.R[:, self.at:self.at + n]
        self.at += n
        if len(shape) == 2:
            v = v.rearrange("p (a b) -> p a b", b=shape[1])
        if len(shape) == 3:
            v = v.rearrange("p (a b c) -> p a b c", b=shape[1], c=shape[2])
        if len(shape) == 4:
            v = v.rearrange("p (a b c d) -> p a b c d", b=shape[1], c=shape[2], d=shape[3])
        return v

    def v(self, name, i=0, n=1):
        a, _ = VEC[name]
        return self.vec[:, a + i:a + i + n]

    def c(self, name, n=None, p0=0, p1=128):
        a, w = CST[name]
        return self.cst[p0:p1, a:a + (w if n is None else n)]

    def bank(self, lo=0, hi=8):
        i = lo + self.turn.get((lo, hi), 0) % (hi - lo)
        self.turn[lo, hi] = self.turn.get((lo, hi), 0) + 1
        return i, self.ps[i], list(self.drained[i])

    def fence(self):
        lanes = (self.pe, self.act, self.dve, self.pool)
        tokens = [l.last() for l in lanes]
        for l in lanes:
            l.held = l.held + tokens
        self.phase = tokens
        self.drained = [[] for _ in range(8)]
        self.at = 0

    def load(self, out, src):
        self.sp.dma(out, src, self.s_ld, self.phase)
        self.n_ld += 16
        return (self.s_ld, self.n_ld)

    def wslot(self, W, c0, c1, l=None):
        n = c1 - c0
        src = W if l is None else W[l]
        view = lambda s: s[:, 0:KT * n].rearrange("p (k n) -> p k n", k=KT)
        i, tok = self.ring.load((view, src[:, c0:c1].rearrange("(k p) n -> p k n", p=128)))
        return i, view(self.slots[i]), tok

    def begin(self):
        io = self.io
        for out, name in ((self.vec[:, :], "vec"), (self.cst[:, :], "cst"), (self.R[:, 64:64 + 1920].rearrange("p (a b) -> p a b", b=128), "msk")):
            self.sp.dma(out, io[name], self.s_in)
        t_in = (self.s_in, 48)
        self.sp.dma(self.X[:, :, :], io["xT"], self.s_x)
        self.t_x = (self.s_x, 16)
        for lane in (self.pe, self.act, self.dve, self.pool):
            lane.held.append(t_in)
        e = self.R[:, 0:32]
        a, _ = VEC["c"]
        src = self.vec[:, a:a + 32]
        t = self.act.act(e, src, ACT.Exp, scale=-1.0)
        t = self.dve.ts(e, e, 1.0, ALU.add, after=[t])
        t = self.dve.do(lambda g: g.reciprocal(self.R[:, 32:64], e), [t])
        src4 = src.rearrange("p (b w k) -> p b w k", b=2, w=2)
        r4 = self.R[:, 32:64].rearrange("p (b w k) -> p b w k", b=2, w=2)
        for b in range(2):
            for w in range(2):
                t = self.dve.mul(self.SX[:, b, :, w], src4[:, b, w, :], r4[:, b, w, :], after=[t])
        self.t_sx = t
        self.t_rw = self.dve.zero(self.RW[:, :])
        self.dve.copy(self.msk[:, :, :], self.R[:, 64:64 + 1920].rearrange("p (a b) -> p a b", b=128))
        self.epsc = self.v("eps")
        self.act.held.append(self.t_x)
        self.dve.held.append(self.t_x)

    def use(self, n):
        self.M, self.CO, self.t_co = self.MM[n % 2], self.COS[n % 2], self.t_cos[n % 2]

    def mods_steps(self, par, W, bias, blk, l, pre, post, pre2, post2):
        M, CO = self.MM[par % 2], self.COS[par % 2]
        tt = []
        for r in range(3):
            te = []
            i, ps, rd = self.bank(7, 8)
            for j in range(4):
                g = 4 * r + j
                s, view, tok = self.wslot(W, 512 * g, 512 * g + 512, l)
                for k in range(KT):
                    tm = self.pe.mm(ps[32 * j:32 * j + 2, :], self.SX[:, blk, k, :], view[:, k, :],
                                    k == 0, k == KT - 1, after=[tok, self.t_sx] + rd, mark=(k == KT - 1))
                    if k == 3:
                        yield
                self.ring.free(s, tm)
                te.append(self.act.copy(self.RW[32 * j:32 * j + 2, :], ps[32 * j:32 * j + 2, :],
                                        after=[tm, self.t_rw] + tt))
                yield
            self.drained[i] = te
            i, ps, rd = self.bank(7, 8)
            for m in range(4):
                tm = self.pe.mm(ps[:, 128 * m:128 * m + 128], self.RW[:, 128 * m:128 * m + 128], self.c("ident"),
                                True, True, after=te + rd, mark=(m == 3))
            tt = [tm]
            P = ps[:, :].rearrange("p (m j x) -> p m j x", m=4, j=4)
            at = VEC[bias][0] + 48 * l + 16 * r
            bb = self.vec[:, at:at + 16].rearrange("p (j m) -> p m j", j=4)
            for w in range(2):
                t = self.dve.add(M[:, 16 * r:16 * r + 16, w].rearrange("p (j m) -> p m j", j=4), P[:, :, :, w], bb,
                                 after=[tm])
            self.drained[i] = [t]
            yield
        for j, (idx, name, one) in enumerate(((1, pre, 1.0), (2, post, 0.0), (4, pre2, 1.0), (5, post2, 0.0))):
            for w in range(2):
                m = M[:, 8 * idx:8 * idx + 8, w]
                if name is None:
                    tc = self.dve.copy(CO[:, j, w, :], m, after=[t]) if one == 0.0 else None
                else:
                    tc = self.dve.stt(CO[:, j, w, :], m, one, self.v(name, 8 * l, 8), ALU.add, ALU.mult, after=[t])
        self.t_cos[par % 2] = tc

    def rstd(self, out, ps_view, n, after, eps=EPS):
        t = self.act.act(out, ps_view, ACT.Ln, scale=1.0 / n, bias=self.epsc[0:out.shape[0], 0:1], after=after)
        return self.act.act(out, out, ACT.Exp, scale=-0.5, after=[t]), t

    def norm_mod(self, n0, j, shift, after=()):
        n = T - n0
        i, ps, rd = self.bank(6, 7)
        for t in range(KT):
            ta = self.act.act(self.H[:, t, n0:T], self.X[:, t, n0:T], ACT.Square, after=after)
            tp = self.pe.mm(ps[:, 0:n], self.c("ones"), self.H[:, t, n0:T], t == 0, t == KT - 1,
                            after=[ta] + rd, mark=(t == KT - 1))
        te, tl = self.rstd(self.RS[:, 0:n], ps[:, 0:n], D, [tp])
        self.drained[i] = [tl]
        self.t_h = [None] * KT
        for t in range(KT):
            tv = self.dve.mul(self.H[:, t, n0:T], self.X[:, t, n0:T], self.RS[:, 0:n], after=[te, tp])
            for w, a, b in ((1, 0, TC), (0, TC, T)):
                if b <= n0:
                    continue
                h = self.H[:, t, a:b]
                sc, sh = self.CO[:, j, w, t:t + 1], self.M[:, 8 * shift + t, w:w + 1]
                if t % 2:
                    tt = self.act.act(h, h, ACT.Identity, scale=sc, bias=sh, after=[tv, self.t_co])
                else:
                    tt = self.dve.ts(h, h, sc, ALU.mult, sh, ALU.add, after=[tv, self.t_co])
            self.t_h[t] = tt

    def resid(self, Y, n0, j, norm, after):
        n = T - n0
        if norm:
            i, ps, rd = self.bank(6, 7)
            for t in range(KT):
                ta = self.act.act(self.H[:, t, 0:n], Y[:, t, :], ACT.Square, after=[after[t]])
                tp = self.pe.mm(ps[:, 0:n], self.c("ones"), self.H[:, t, 0:n], t == 0, t == KT - 1,
                                after=[ta] + rd, mark=(t == KT - 1))
            te, tl = self.rstd(self.RS[:, 0:n], ps[:, 0:n], D, [tp])
            self.drained[i] = [tl]
        for t in range(KT):
            tv = after[t]
            if norm:
                tv = self.dve.mul(Y[:, t, :], Y[:, t, :], self.RS[:, 0:n], after=[te, after[t]])
            for w, a, b in ((1, 0, TC), (0, TC, T)):
                if b <= n0:
                    continue
                self.dve.stt(self.X[:, t, a:b], Y[:, t, a - n0:b - n0], self.CO[:, j, w, t:t + 1],
                             self.X[:, t, a:b], ALU.mult, ALU.add, after=[tv, self.t_co])

    def fm(self, w, m0, m, n0, out, after, lo=0, hi=4, po=0, eng=None, K=KT, rhs=None, **kw):
        n = T - n0
        i, ps, rd = self.bank(lo, hi)
        for k in range(K):
            r = self.H[:, k, n0:T] if rhs is None else rhs(k)
            h = [self.t_h[k]] if rhs is None else []
            tm = self.pe.mm(ps[po:po + m, 0:n], w[:, k, m0:m0 + m], r, k == 0, k == K - 1,
                            after=list(after) + rd + h, mark=(k == K - 1))
        self.drained[i] = [out(ps[po:po + m, 0:n], tm)]
        return tm

    def tm(self, w, c0, c1, jt, out, after, lo=0, hi=4):
        i, ps, rd = self.bank(lo, hi)
        for k in range(KT):
            tk = self.pe.mm(ps[:, 0:c1 - c0], self.H[:, k, 128 * jt:128 * jt + 128], w[:, k, c0:c1],
                            k == 0, k == KT - 1, after=list(after) + rd + [self.t_h[k]], mark=(k == KT - 1))
        self.drained[i] = [out(ps[:, 0:c1 - c0], tk)]
        return tk

    def down(self, W, S, n, k_of, kt, after, Y):
        for k0 in range(0, kt, 4):
            kn = min(4, kt - k0)
            view = lambda s: s[:, 0:kn * D].rearrange("p (k n) -> p k n", k=kn)
            s, tok = self.ring.load((view, W[128 * k0:128 * (k0 + kn), :].rearrange("(k p) n -> p k n", p=128)))
            w = view(self.slots[s])
            for k in range(k0, k0 + kn):
                for t in range(KT):
                    tm = self.pe.mm(self.ps[t][:, 0:n], w[:, k - k0, 128 * t:128 * t + 128], k_of(k),
                                    k == 0, k == kt - 1, after=[tok] + list(after[k]) + (self.drained[t] if k == 0 else []),
                                    mark=(k == kt - 1 or t == KT - 1))
                    if k == kt - 1:
                        lane = self.act if t % 2 else self.dve
                        self.drained[t] = [lane.copy(Y[:, t, :], self.ps[t][:, 0:n], after=[tm])]
            self.ring.free(s, tm)
        return [self.drained[t][0] for t in range(KT)]

    def ffn_swiglu(self, l, n0):
        n = T - n0
        self.fence()
        self.norm_mod(n0, 2, 3)
        G = self.alloc(22, n)
        tmp = [self.alloc(n) for _ in range(2)]
        io = self.io
        free = [[], []]
        done = []
        for g in range(11):
            view = lambda s: s[:, :].rearrange("p (u k n) -> p u k n", u=2, k=KT)
            cols = slice(256 * g, 256 * g + 256)
            s, tok = self.ring.load(
                (lambda s: view(s)[:, 0], io["ffn_w_gate"][l][:, cols].rearrange("(k p) n -> p k n", p=128)),
                (lambda s: view(s)[:, 1], io["ffn_w_up"][l][:, cols].rearrange("(k p) n -> p k n", p=128)))
            w = view(self.slots[s])
            for m in range(2):
                x = 2 * g + m
                tb = tmp[x % 2]
                got = []

                def gate(ps, t, tb=tb, x=x):
                    t = self.act.act(tb, ps, ACT.Silu, after=[t] + free[x % 2])
                    got.append(t)
                    return t

                def up(ps, t, tb=tb, x=x):
                    t = self.dve.mul(G[:, x, :], ps, tb, after=[t, got[0]])
                    free[x % 2] = [t]
                    done.append([t])
                    return t

                self.fm(w[:, 0], 128 * m, 128, n0, gate, [tok], 0, 6)
                tm = self.fm(w[:, 1], 128 * m, 128, n0, up, [tok], 0, 6)
            self.ring.free(s, tm)
        Yr = self.alloc(KT, n)
        ys = self.down(io["ffn_w_down"][l], None, n, lambda k: G[:, k, :], 22, done, Yr)
        self.fence_keep()
        self.resid(Yr, n0, 3, True, ys)

    def fence_keep(self):
        at = self.at
        self.fence()
        self.at = at

    def ffn_sq(self, l, n0):
        n = T - n0
        self.fence()
        self.norm_mod(n0, 2, 3)
        G = self.alloc(32, n)
        done = []
        io = self.io
        for g in range(8):
            s, w, tok = self.wslot(io["mlp_w1_2"], 512 * g, 512 * g + 512, l)
            for m in range(4):
                x = 4 * g + m

                def out(ps, t, x=x):
                    t = self.act.act(G[:, x, :], ps, ACT.Relu, after=[t])
                    done.append([self.pool.mul(G[:, x, :], G[:, x, :], G[:, x, :], after=[t])])
                    return t

                tm = self.fm(w, 128 * m, 128, n0, out, [tok], 0, 6)
            self.ring.free(s, tm)
        Y = self.alloc(KT, n)
        ys = self.down(io["mlp_w2_2"][l], None, n, lambda k: G[:, k, :], 32, done, Y)
        self.fence_keep()
        self.resid(Y, n0, 3, False, ys)

    def cumsum(self, B, g, after):
        n = B.shape[1] * B.shape[2]
        return self.dve.do(lambda e: e.tensor_tensor_scan(
            B.rearrange("p c x -> p (c x)"), self.c("smask", n), g.rearrange("p c x -> p (c x)"), 0.0,
            ALU.mult, ALU.add), after)

    def levels(self, *args):
        last = []
        for _ in self.levels_steps(*args, last):
            pass
        return last

    def levels_steps(self, q, ks, Bs, c0, nc, scale, heads, bufs, after, lo, hi, last):
        last += [None] * len(heads)
        for h, (pb, sz, P, dg) in enumerate(heads):
            i, ps, rd = self.bank(lo, hi)
            for c in range(nc):
                for d, kk in enumerate(dg):
                    tm = self.pe.mm(ps[:, 128 * c:128 * c + 128], kk[pb:pb + sz, 128 * (c0 + c):128 * (c0 + c) + 128],
                                    q[pb:pb + sz, 128 * c:128 * c + 128], d == 0, d == len(dg) - 1,
                                    after=after + rd, mark=(c == nc - 1 and d == len(dg) - 1))
            eye = self.c("ident").unsqueeze(1).broadcast_to([128, nc, 128])
            S = ps[:, 0:128 * nc].rearrange("p (c x) -> p c x", c=nc)
            last[h] = self.dve.stt(P, S, 2.0 if len(dg) == 1 else 1.0, eye, ALU.mult, ALU.mult,
                                   after=[tm] + self.free_p[h])
            self.drained[i] = [last[h]]
        Z = [(s, li, L) for s in range(2) for li, L in enumerate(LEVELS)]
        E_, UV, prod = {}, {}, {}

        def split(n):
            s, li, L = Z[n]
            B, sh = Bs[s], 1 - s
            u = self.turn.get("lvl", 0)
            self.turn["lvl"] = u + 1
            x = u % len(bufs)
            E = bufs[x][0]
            halves = lambda z: z.rearrange("p c (b h l) -> p c b h l", h=2, l=L)
            Ev = halves(E.rearrange("p (c x) -> p c x", c=nc))
            Bt = halves(B[:, c0:c0 + nc, sh:sh + 128])
            Bm = halves(B[:, c0:c0 + nc, 0:128])[:, :, :, 1, 0:1].broadcast_to([E.shape[0], nc, 64 // L, L])
            fr = self.e_free[x]
            t1 = self.dve.sub(Ev[:, :, :, 0, :], Bm, Bt[:, :, :, 0, :], after=after + fr)
            t2 = self.dve.sub(Ev[:, :, :, 1, :], Bt[:, :, :, 1, :], Bm, after=after + fr)
            E_[n] = x, self.act.act(E, E, ACT.Exp, scale=scale, after=[t1, t2])

        def product(n):
            s, li, L = Z[n]
            x, te = E_[n]
            E, U, V = bufs[x]
            fr = self.uv_free[x]
            tu = self.pool.mul(U, ks[s][:, 128 * c0:128 * (c0 + nc)], E, after=[te] + after + fr)
            tv = self.dve.mul(V, q, E, after=[te] + after + fr)
            self.e_free[x] = [tu, tv]
            prod[n] = []
            for h, (pb, sz, P, dg) in enumerate(heads):
                i, ps, rd = self.bank(lo, hi)
                for c in range(nc):
                    cs = slice(128 * c, 128 * c + 128)
                    tm = self.pe.mm(ps[:, cs], U[pb:pb + sz, cs], V[pb:pb + sz, cs], True, True,
                                    after=[tu, tv] + rd, mark=(c == nc - 1))
                prod[n].append((i, ps, tm))
            self.uv_free[x] = [tm]

        def keep(n):
            s, li, L = Z[n]
            for h, (pb, sz, P, dg) in enumerate(heads):
                i, ps, tm = prod[n][h]
                mk = self.msk[:, 7 * s + li:7 * s + li + 1, :].broadcast_to([128, nc, 128])
                S = ps[:, 0:128 * nc].rearrange("p (c x) -> p c x", c=nc)
                last[h] = self.dve.do(lambda e, P=P, mk=mk, S=S: e.copy_predicated(P, mk, S), [tm, last[h]])
                self.drained[i] = [last[h]]

        late = (hi - lo) >= 2 * len(heads)
        for n in range(len(Z) + 2):
            if n < len(Z):
                split(n)
            if not late and 2 <= n:
                keep(n - 2)
            if 1 <= n <= len(Z):
                product(n - 1)
            if late and 2 <= n:
                keep(n - 2)
            yield

    def across(self, ks, Bs, scale, W, after):
        out = []
        for s in range(2):
            B, k = Bs[s], ks[s]
            w, x, e = W[s], W[2 + s], W[4 + s]
            w3 = w.rearrange("p (c x) -> p c x", c=4)
            P = w.shape[0]
            if s == 0:
                t = self.dve.sub(w3, B[:, :, 128:129].broadcast_to([P, 4, 128]), B[:, :, 1:129], after=after + self.w_free)
                t = self.act.act(w, w, ACT.Exp, scale=scale, after=[t])
            else:
                t = self.act.act(w3, B[:, :, 0:128], ACT.Exp, scale=scale, after=after + self.w_free)
            t = self.pool.mul(w, w, k, after=[t] + after)
            ta = self.act.act(e, B[:, :, 128], ACT.Exp, scale=scale, after=after + self.w_free)
            T_ = lambda c: e[:, c:c + 1]
            K_ = lambda c: w[:, 128 * c:128 * c + 128]
            o = [t, ta] + self.w_free
            if s == 0:
                seq = ((0, K_(0), T_(1)), (1, K_(1), T_(2)), (2, x[:, 0, :], T_(2)))
            else:
                seq = ((0, K_(1), T_(0)), (1, K_(0), T_(3)), (2, x[:, 0, :], T_(3)))
            for j, a, b in seq:
                o.append(self.dve.ts(x[:, j, :], a, b, ALU.mult, after=o))
            out.append([t] + o[-3:])
        return out

    def queries(self, q, Bs, c0, nc, scale, Q, after):
        out = []
        for s in range(2):
            B = Bs[s][:, c0:c0 + nc]
            e = Q[s]
            e3 = e.rearrange("p (c x) -> p c x", c=nc)
            P = e.shape[0]
            if s == 0:
                t = self.act.act(e3, B[:, :, 1:129], ACT.Exp, scale=scale, after=after + self.w_free)
            else:
                t = self.dve.sub(e3, B[:, :, 128:129].broadcast_to([P, nc, 128]), B[:, :, 0:128], after=after + self.w_free)
                t = self.act.act(e, e, ACT.Exp, scale=scale, after=[t])
            out.append(self.dve.mul(e, e, q, after=[t] + after))
        return out

    def cross_scores(self, pb, sz, W, Q, q0, dst, after, lo, hi, chunks=(0, 1, 2, 3)):
        K = lambda s, j: W[s][pb:pb + sz, 128 * j:128 * j + 128]
        X = lambda s, j: W[2 + s][pb:pb + sz, j, :]
        pairs = {(0, 1): [(0, K(0, 0))], (1, 0): [(1, K(1, 1))], (2, 3): [(0, K(0, 2))], (3, 2): [(1, K(1, 3))],
                 (0, 2): [(0, X(0, 0)), (1, X(1, 1))], (1, 2): [(0, K(0, 1)), (1, X(1, 2))],
                 (0, 3): [(0, X(0, 2)), (1, K(1, 0))], (1, 3): [(0, X(0, 1)), (1, X(1, 0))]}
        todo = [p for p in pairs if p[1] in chunks]
        out = []
        for a in range(0, len(todo), 4):
            i, ps, rd = self.bank(lo, hi)
            part = todo[a:a + 4]
            for n, (J, I) in enumerate(part):
                for m, (s, k) in enumerate(pairs[J, I]):
                    tm = self.pe.mm(ps[:, 128 * n:128 * n + 128], k, Q[s][pb:pb + sz, 128 * (I - q0):128 * (I - q0) + 128],
                                    m == 0, m == len(pairs[J, I]) - 1, after=after + rd,
                                    mark=(n == len(part) - 1 and m == len(pairs[J, I]) - 1))
            for n, (J, I) in enumerate(part):
                out.append(self.act.copy(dst(J, I), ps[:, 128 * n:128 * n + 128], after=[tm] + self.free_cross))
            self.drained[i] = [out[-1]]
        return out

    def readout(self, o, og, gain, dst, n, after, tmp, lo, hi, dv=128, mat="ones"):
        r, sq = tmp
        ta = self.act.act(sq, o, ACT.Square, after=after)
        i, ps, rd = self.bank(lo, hi)
        tp = self.pe.mm(ps[:, 0:n], self.c(mat), sq, True, True, after=[ta] + rd, mark=True)
        te, tl = self.rstd(r, ps[:, 0:n], dv, [tp] + after)
        self.drained[i] = [tl]
        t = self.dve.mul(dst, o, r, after=[te, ta] + after)
        t2 = self.dve.stt(dst, dst, gain, og, ALU.mult, ALU.mult, after=[t] + after)
        return t, t2

    def rms_heads(self, x, mat, K, n, dh, gain, after, tmp, lo, hi):
        r, sq = tmp
        ta = self.act.act(sq[0:K], x, ACT.Square, after=after)
        i, ps, rd = self.bank(lo, hi)
        tp = self.pe.mm(ps[0:K, 0:n], self.c(mat, K, 0, K), sq[0:K], True, True, after=[ta] + rd, mark=True)
        te, tl = self.rstd(r[0:K], ps[0:K, 0:n], dh, [tp] + after)
        self.drained[i] = [tl]
        t = self.dve.stt(x, x, gain, r[0:K], ALU.mult, ALU.mult, after=[te] + after)
        return t

    def rope(self, x, K, mat, cs, sn, after, tmp, lo, hi):
        i, ps, rd = self.bank(lo, hi)
        tp = self.pe.mm(ps[0:K, 0:TC], self.c(mat, K, 0, K), x, True, True, after=after + rd, mark=True)
        t1 = self.dve.mul(tmp[0:K], ps[0:K, 0:TC], self.c(sn, None, 0, K), after=[tp] + after)
        self.drained[i] = [t1]
        t2 = self.dve.mul(x, x, self.c(cs, None, 0, K), after=[tp])
        return self.dve.add(x, x, tmp[0:K], after=[t1, t2])

    def attend_steps(self, units, scale, after, st, lo):
        S = {}
        fp, fpt = [[] for _ in st["P"]], [[] for _ in st["PT"]]

        def scores(u):
            q, k, vv, dst, nk, po = units[u]
            i, ps, rd = self.bank(lo, lo + 2)
            S[u] = i, ps, self.pe.mm(ps[:, 0:nk], q, k, True, True, after=after + rd, mark=True)

        def exps(u):
            q, k, vv, dst, nk, po = units[u]
            i, ps, tm = S[u]
            n = u % len(st["P"])
            P, m, r = st["P"][n], st["m"][:, u:u + 1], st["r"][:, 2 * u:2 * u + 2]
            t1 = self.dve.do(lambda e: e.reduce_max(m, ps[:, 0:nk], AX.X), [tm])
            t2 = self.dve.ts(m, m, -scale, ALU.mult, after=[t1])
            t3 = self.act.act(P[:, 0:nk], ps[:, 0:nk], ACT.Exp, scale=scale, bias=m, accum=r[:, 0:1],
                              after=[t2] + fp[n])
            self.drained[i] = [t3]
            S[u] = t3

        def turn(u):
            q, k, vv, dst, nk, po = units[u]
            n = u % len(st["P"])
            P, r = st["P"][n], st["r"][:, 2 * u:2 * u + 2]
            t4 = self.dve.do(lambda e: e.reciprocal(r[:, 1:2], r[:, 0:1]), [S[u]])
            t5 = self.dve.ts(P[:, 0:nk], P[:, 0:nk], r[:, 1:2], ALU.mult, after=[t4, S[u]])
            i, ps, rd = self.bank(lo + 2, lo + 3)
            for j in range(nk // 128):
                tm = self.pe.tr(ps[:, 128 * j:128 * j + 128], P[:, 128 * j:128 * j + 128], self.c("ident"),
                                after=[t5] + rd, mark=(j == nk // 128 - 1))
            fp[n] = [tm]
            x = u % len(st["PT"])
            S[u] = self.act.copy(st["PT"][x][:, 0:nk], ps[:, 0:nk], after=[tm] + fpt[x])
            self.drained[i] = [S[u]]

        def values(u):
            q, k, vv, dst, nk, po = units[u]
            x = u % len(st["PT"])
            i, ps, rd = self.bank(lo + 2, lo + 3)
            for j in range(nk // 128):
                tm = self.pe.mm(ps[po:po + 64, 0:128], vv(j), st["PT"][x][:, 128 * j:128 * j + 128], j == 0,
                                j == nk // 128 - 1, after=[S[u]] + rd + after, mark=(j == nk // 128 - 1))
            fpt[x] = [tm]
            st["out"] = self.act.copy(dst, ps[po:po + 64, 0:128], after=[tm])
            self.drained[i] = [st["out"]]

        for t in range(len(units) + 3):
            if t < len(units):
                scores(t)
            if 1 <= t <= len(units):
                exps(t - 1)
            if 3 <= t:
                values(t - 3)
            if 2 <= t <= len(units) + 1:
                turn(t - 2)
            yield

    def att_state(self, n, room=None):
        P = [self.alloc(T) for _ in range(4)] if room is None else [room[:, T * i:T * i + T] for i in range(4)]
        return {"P": P[0:2], "PT": P[2:4], "m": self.alloc(n), "r": self.alloc(2 * n)}

    def even(self):
        io = self.io
        W = io["even_w_in"][0]
        self.fence()
        gw = self.alloc(2 * 256)
        t_gw = self.load(gw[0:32], io["gla_gw"])
        self.norm_mod(0, 0, 0)
        q, k, og = self.alloc(2, T), self.alloc(2, T), self.alloc(4, T)
        z, aq, kk = self.alloc(T), self.alloc(4, T), self.alloc(2, T)
        vg, va = self.alloc(4, T), self.alloc(4, 128)
        cp = lambda dst, sc=None: (lambda ps, t: self.act.act(dst, ps, ACT.Copy, scale=sc or 1.0, after=[t]))
        s, w, tok = self.wslot(W, 0, 512)
        for m in range(2):
            self.fm(w, 128 * m, 128, 0, cp(q[:, m, :], 0.125), [tok])
        for m in range(2):
            tl = self.fm(w, 256 + 128 * m, 128, 0, cp(k[:, m, :]), [tok])
        self.ring.free(s, tl)
        n = 32 + 256
        view = lambda s: s[:, 0:KT * n].rearrange("p (k n) -> p k n", k=KT)
        s, tok = self.ring.load(
            (lambda s: view(s)[:, :, 0:32], W[:, 1536:1568].rearrange("(k p) n -> p k n", p=128)),
            (lambda s: view(s)[:, :, 32:288], W[:, 2080:2336].rearrange("(k p) n -> p k n", p=128)))
        w = view(self.slots[s])
        self.fm(w, 0, 32, 0, cp(z[0:32, :]), [tok])
        t_z = (self.act.sem, self.act.n)
        for g in range(2):
            for half in range(2):
                self.fm(w, 32 + 64 * g, 64, 0, cp(kk[64 * half:64 * half + 64, g, :]), [tok], po=64 * half)
        for j in range(4):
            tl = self.tm(w, 160, 288, j, lambda ps, t, j=j: self.act.copy(va[:, j, :], ps, after=[t]), [tok])
        self.ring.free(s, tl)
        s, w, tok = self.wslot(W, 512, 1024)
        for j in range(4):
            tl = self.tm(w, 0, 512, j, lambda ps, t, j=j: self.act.copy(vg[:, j, :], ps, after=[t]), [tok])
        self.ring.free(s, tl)
        s, w, tok = self.wslot(W, 1568, 2080)
        for m in range(4):
            tl = self.fm(w, 128 * m, 128, 0, cp(aq[:, m, :]), [tok])
        self.ring.free(s, tl)
        s, w, tok = self.wslot(W, 1024, 1536)
        for m in range(4):
            tl = self.fm(w, 128 * m, 128, 0, lambda ps, t, m=m: self.act.act(og[:, m, :], ps, ACT.Silu, after=[t]), [tok])
        self.ring.free(s, tl)
        self.fence_keep()
        MIX = self.H
        s_p, fr_p = self.ring.scratch()
        s_a, fr_a = self.ring.scratch()
        Bs = [[None, None], [None, None]]
        Bf = self.alloc(4, 4 * 129)
        gp, Lt, aL = self.alloc(4 * 129), self.alloc(T), self.alloc(T)
        SC = 1.0 / 16.0
        bufs = [(self.alloc(T), self.alloc(T), self.alloc(T)) for _ in range(2)]
        WW = [self.alloc(T), self.alloc(T), self.alloc(3, 128), self.alloc(3, 128), self.alloc(4), self.alloc(4)]
        QQ = [self.alloc(T), self.alloc(T)]
        room = self.slots[s_a]
        st = self.att_state(32, room[:, 0:4 * T])
        PP = [self.slots[s_p][:, 2048 * h:2048 * h + 2048].rearrange("p (j x) -> p j x", j=4) for h in range(2)]

        def linear():
            gp3 = gp.rearrange("p (c x) -> p c x", x=129)
            tB = [self.dve.zero(gp)]
            for m in range(2):
                for d in range(2):
                    i, ps, rd = self.bank(0, 3)
                    tm = self.pe.mm(ps[:, :], gw[0:32, 256 * d + 128 * m:256 * d + 128 * m + 128], z[0:32, :], True, True,
                                    after=[t_gw, t_z] + rd, mark=True)
                    t = self.act.act(Lt, ps[:, :], ACT.Identity, bias=self.v("gla_b", 2 * d + m), after=[tm] + tB)
                    self.drained[i] = [t]
                    ta = self.act.act(aL, Lt, ACT.Abs, after=[t])
                    ta = self.act.act(aL, aL, ACT.Exp, scale=-1.0, after=[ta])
                    ta = self.act.act(aL, aL, ACT.Ln, bias=self.v("one"), after=[ta])
                    L3, a3 = Lt.rearrange("p (c x) -> p c x", c=4), aL.rearrange("p (c x) -> p c x", c=4)
                    t = self.dve.stt(gp3[:, :, 1:129], L3, 0.0, a3, ALU.min, ALU.subtract, after=[t, ta] + tB)
                    B = Bf[:, 2 * d + m, :].rearrange("p (c x) -> p c x", x=129)
                    tB = [self.cumsum(B, gp3, [t])]
                    Bs[m][d] = B
                    yield
            self.w_free, self.e_free, self.uv_free = [], [[], []], [[], []]
            self.free_p, self.free_cross = [fr_p, fr_p], fr_p
            to = []
            for m in range(2):
                ks, qm = [k[:, m, :]] * 2, q[:, m, :]
                heads = [(64 * h, 64, self.diag_view(s_p, 2048 * h), [k[:, m, :]]) for h in range(2)]
                last = []
                tw = self.across(ks, Bs[m], SC, WW, tB)
                yield
                tq = self.queries(qm, Bs[m], 0, 4, SC, QQ, tB)
                yield from self.levels_steps(qm, ks, Bs[m], 0, 4, SC, heads, bufs, tB, 0, 3, last)
                tx = []
                for h in range(2):
                    tx.append(self.cross_scores(64 * h, 64, WW, QQ, 0, lambda J, I, h=h: PP[h][:, J, 128 * I:128 * I + 128],
                                                tw[0] + tw[1] + tq, 3, 4))
                    yield
                for h in range(2):
                    hd = 2 * m + h
                    i, ps, rd = self.bank(3, 4)
                    for J in range(4):
                        a = 0 if J < 2 else TC
                        tm = self.pe.mm(ps[:, a:T], vg[:, J, 128 * hd:128 * hd + 128], PP[h][:, J, a:T], J == 0, J == 3,
                                        after=[last[h]] + tx[h] + rd, mark=(J == 3))
                    t1, t2 = self.readout(ps[:, :], og[:, hd, :], self.v("gla_n"), MIX[:, hd, :], T, [tm] + to + tB,
                                          (Lt, aL), 0, 3)
                    self.drained[i] = [t1]
                    to = [t1]
                    self.free_p[h] = [tm]
                    yield
                self.free_cross = self.w_free = [tm]
            self.ring.free(s_p, tm)

        def softmax():
            tmp = (room[:, 2048:2560], room[:, 2560:3072])
            rt = room[:, 3072:3072 + TC]
            prev = fr_a
            for x, gain in ((kk[:, 0, :], "ak_n"), (kk[:, 1, :], "ak_n")) + tuple((aq[:, m, :], "aq_n") for m in range(4)):
                t = self.rms_heads(x, "bd", 128, T, 64, self.v(gain), prev, tmp, 4, 6)
                t = self.rope(x[:, TC:T], 128, "rotE", "cosE", "sinE", [t] + prev, rt, 4, 6)
                prev = [t]
                yield
            units = []
            for h in range(8):
                m, pb, g = h // 2, 64 * (h % 2), h // 4
                for c in range(4):
                    nk = TC if c < 2 else T
                    cs = slice(128 * c, 128 * c + 128)
                    units.append((aq[pb:pb + 64, m, cs], kk[pb:pb + 64, g, 0:nk],
                                  lambda j, g=g: va[:, j, 64 * g:64 * g + 64], MIX[pb:pb + 64, 4 + m, cs], nk, pb))
            yield from self.attend_steps(units, 0.125, prev, st, 4)
            self.ring.free(s_a, self.pe.last(), self.act.last(), self.dve.last())

        self.together(linear(), softmax(), self.next_mods())
        self.fence()
        if self.stop == "evenmix":
            return
        Y = self.alloc(KT, T)
        ys = self.down(io["even_w_out"][0], None, T, lambda k: MIX[:, k, :], 8, [[]] * 8, Y)
        self.fence_keep()
        self.resid(Y, 0, 1, True, ys)

    def diag_view(self, si, off):
        v = self.slots[si][:, off:off + 640].unsqueeze(1).broadcast_to([128, 4, 640])
        v = v[:, :, 0:128]
        return bass.AP(v.tensor, v.offset, [list(v.ap[0]), [640, 4], [1, 128]])

    def finish(self):
        self.fence()
        tokens, self.phase = self.phase, None
        self.sp.dma(self.io["outX"], (self.H if 'mix' in self.stop else self.X)[:, :, :] if self.stop else self.X[:, :, TC:T], self.s_out, tokens)
        self.sp.items.append([[(self.s_out, 16)], None, None, 0])
        with self.nc.Block() as block:
            @block.sync
            def _(e):
                self.sp.play(e)

            @block.gpsimd
            def _(e):
                self.pool.play(e)

            @block.scalar
            def _(e):
                self.act.play(e)

            @block.tensor
            def _(e):
                self.pe.play(e)

            @block.vector
            def _(e):
                self.dve.play(e)

    def together(self, *gens):
        gens = list(gens)
        while gens:
            for g in list(gens):
                if next(g, self) is self:
                    gens.remove(g)

    def odd(self):
        io = self.io
        W = io["odd_w_in"][0]
        self.fence()
        self.norm_mod(0, 0, 0)
        V, MIX = self.alloc(4, D), self.alloc(KT, TC)
        for g in range(2):
            s, w, tok = self.wslot(W, 3072 + 512 * g, 3584 + 512 * g)
            for j in range(4):
                dst = V[:, j, 512 * g:512 * g + 512]
                tl = self.tm(w, 0, 512, j, lambda ps, t, dst=dst: self.act.copy(dst, ps, after=[t]), [tok], 0, 2)
            self.ring.free(s, tl)
        e, p = self.alloc(4, 8), self.alloc(4, 8)
        mx = self.alloc(2, 8)
        lb = self.v("lb", 0, 32).rearrange("p (a h) -> p a h", h=8)
        l4 = lb.rearrange("p (d l) h -> p d l h", l=2)
        e4, p4 = (x.rearrange("p (d l) h -> p d l h", l=2) for x in (e, p))
        t = self.dve.tt(mx, l4[:, :, 0, :], l4[:, :, 1, :], ALU.max)
        for l in range(2):
            t = self.dve.sub(e4[:, :, l, :], l4[:, :, l, :], mx, after=[t])
        t = self.act.act(e, e, ACT.Exp, after=[t])
        t = self.dve.add(mx, e4[:, :, 0, :], e4[:, :, 1, :], after=[t])
        t = self.dve.do(lambda g: g.reciprocal(mx, mx), [t])
        for l in range(2):
            t = self.dve.mul(p4[:, :, l, :], e4[:, :, l, :], mx, after=[t])
        t = self.dve.ts(p4[:, :, 1, :], p4[:, :, 1, :], 2.0 ** -60, ALU.max, after=[t])
        t_lb = t
        sets = []
        for _ in range(2):
            sets.append(dict(q=self.alloc(TC), og=self.alloc(TC), k=[self.alloc(T), self.alloc(T)],
                             B=[self.alloc(4, 129), self.alloc(4, 129)]))
        sg, sf = self.alloc(T), [self.alloc(T), self.alloc(T)]
        gp = [self.alloc(4, 129) for _ in range(2)]
        tz = [self.dve.zero(g) for g in gp]
        bufs = [(self.alloc(TC), self.alloc(TC), self.alloc(TC)) for _ in range(2)]
        WW = [self.alloc(T), self.alloc(T), self.alloc(3, 128), self.alloc(3, 128), self.alloc(4), self.alloc(4)]
        QQ = [self.alloc(TC), self.alloc(TC)]
        PB = self.alloc(4 * TC)
        PP = PB.rearrange("p (j x) -> p j x", j=4)
        diag = bass.AP(PB.tensor, PB[:, 512:513].offset, [list(PB.ap[0]), [384, 2], [1, 128]])
        tmp = (self.alloc(TC), self.alloc(TC))
        self.w_free, self.e_free, self.uv_free = [], [[], []], [[], []]
        self.free_p, self.free_cross = [[]], []
        done, ready, g_free = [[], []], {}, [[], [], []]

        def project(h):
            u = h % 2
            S = sets[u]
            view = lambda s: s[:, :].rearrange("p (a k n) -> p a k n", a=4, k=KT)
            s, tok = self.ring.load(*[
                (lambda s, a=a: view(s)[:, a], W[:, c + 128 * h:c + 128 * h + 128].rearrange("(k p) n -> p k n", p=128))
                for a, c in enumerate((0, 4096, 1024, 2048))])
            w = view(self.slots[s])
            i0, ps0, rd = self.bank(0, 3)
            for a in range(2):
                for k in range(KT):
                    tm0 = self.pe.mm(ps0[:, TC * a:TC * a + TC], w[:, a, k, :], self.H[:, k, TC:T], k == 0, k == KT - 1,
                                     after=[tok, self.t_h[k]] + rd, mark=(k == KT - 1))
                yield
            pf = []
            for d in range(2):
                i, ps, rd = self.bank(0, 3)
                for k in range(KT):
                    tm = self.pe.mm(ps[:, :], w[:, 2 + d, k, :], self.H[:, k, :], k == 0, k == KT - 1,
                                    after=[tok, self.t_h[k]] + rd, mark=(k == KT - 1))
                    if k == 3:
                        yield
                pf.append((i, ps, tm))
                yield
            self.ring.free(s, tm)
            for _ in range(4):
                yield
            t = self.act.act(sg, ps0[:, :], ACT.Sigmoid, after=[tm0] + g_free[2])
            t0 = self.dve.mul(S["q"], ps0[:, 0:TC], sg[:, 0:TC], after=[t] + done[u])
            t1 = self.dve.mul(S["og"], ps0[:, TC:T], sg[:, TC:T], after=[t] + done[u])
            self.drained[i0] = [t1]
            g_free[2] = [t1]
            toks = [t0, t1]
            sig = []
            for d, (i, ps, tm) in enumerate(pf):
                a = self.act.act(sf[d], ps[:, :], ACT.Sigmoid, after=[tm] + g_free[d])
                b = self.act.act(S["k"][d], ps[:, :], ACT.Sigmoid, scale=-1.0, after=[tm] + done[u])
                self.drained[i] = [b]
                sig.append((a, b))
            fs = []
            for d, (a, b) in enumerate(sig):
                p1, p0, g = p[:, 2 * d + 1, h:h + 1], p[:, 2 * d, h:h + 1], gp[d]
                fs.append(self.dve.ts(g[:, :, 1:129], sf[d].rearrange("p (c x) -> p c x", c=4), p0, ALU.mult, p1, ALU.add,
                                      after=[a, t_lb] + g_free[d] + tz))
                toks.append(self.dve.ts(S["k"][d], S["k"][d], p0, ALU.mult, after=[b, t_lb]))
            for d in range(2):
                g = gp[d]
                t = self.act.act(g[:, :, 1:129], g[:, :, 1:129], ACT.Ln, after=[fs[d]])
                t = self.cumsum(S["B"][d], g, [t] + done[u])
                g_free[d] = [t]
                toks.append(t)
            ready[h] = toks

        def mix(h):
            u = h % 2
            S, af = sets[u], ready[h]
            tw = self.across(S["k"], S["B"], 1.0, WW, af)
            yield
            tq = self.queries(S["q"], S["B"], 2, 2, 1.0, QQ, af)
            last = []
            yield from self.levels_steps(S["q"], S["k"], S["B"], 2, 2, 1.0, [(0, 128, diag, S["k"])], bufs, af, 3, 5, last)
            tx = self.cross_scores(0, 128, WW, QQ, 2, lambda J, I: PP[:, J, 128 * (I - 2):128 * (I - 2) + 128],
                                   tw[0] + tw[1] + tq, 5, 6, (2, 3))
            yield
            i, ps, rd = self.bank(6, 7)
            for J in range(4):
                tm = self.pe.mm(ps[:, 0:TC], V[:, J, 128 * h:128 * h + 128], PP[:, J, :], J == 0, J == 3,
                                after=[last[0]] + tx + rd, mark=(J == 3))
            t1, t2 = self.readout(ps[:, 0:TC], S["og"], self.v("hg_n"), MIX[:, h, :], TC, [tm] + self.ro_free + af, tmp, 5, 6)
            self.drained[i] = [t1]
            self.ro_free = [t1]
            self.free_p[0] = self.free_cross = self.w_free = [tm]
            done[u] = [t2, t1]
            yield

        self.ro_free = []
        extra = self.next_mods()
        self.together(project(0))
        for h in range(8):
            self.together(mix(h), *([project(h + 1)] if h < 7 else []), itertools.islice(extra, 4))
        self.together(extra)
        self.fence_keep()
        if self.stop == "oddmix":
            self.act.copy(self.H[:, :, TC:T], MIX)
            return
        Y = self.alloc(KT, TC)
        ys = self.down(io["odd_w_out"][0], None, TC, lambda k: MIX[:, k, :], 8, [[]] * 8, Y)
        self.fence_keep()
        self.resid(Y, TC, 1, True, ys)

    def mla(self):
        io = self.io
        W = io["w_in_2"][0]
        self.fence()
        self.sp.dma(self.X[:, :, 0:TC], io["x2T"], self.s_x, self.phase)
        self.norm_mod(0, 0, 0, after=[(self.s_x, 32)])
        cp = lambda dst, sc=None: (lambda ps, t: self.act.act(dst, ps, ACT.Copy, scale=sc or 1.0, after=[t]))
        rq, rk, rg, rv = (self.alloc(4, T) for _ in range(4))
        cq, ckv, kr, vv = self.alloc(2, T), self.alloc(T), self.alloc(T), self.alloc(4, T)
        s, w, tok = self.wslot(W, 0, 416)
        for m in range(2):
            self.fm(w, 128 * m, 128, 0, cp(cq[:, m, :]), [tok])
        self.fm(w, 256, 128, 0, cp(ckv), [tok])
        tl = self.fm(w, 384, 32, 0, cp(kr[64:96, :]), [tok], po=64)
        self.ring.free(s, tl)
        for c0, dst, sc in ((416, rq, 1.0), (928, rk, 0.125)):
            s, w, tok = self.wslot(W, c0, c0 + 512)
            for m in range(4):
                tl = self.fm(w, 128 * m, 128, 0, cp(dst[:, m, :], sc), [tok])
            self.ring.free(s, tl)
        s, w, tok = self.wslot(W, 1440, 1952)
        for j in range(4):
            tl = self.tm(w, 0, 512, j, lambda ps, t, j=j: self.act.copy(rv[:, j, :], ps, after=[t]), [tok])
        self.ring.free(s, tl)
        s, w, tok = self.wslot(W, 1952, 2464)
        for m in range(4):
            tl = self.fm(w, 128 * m, 128, 0, lambda ps, t, m=m: self.act.act(rg[:, m, :], ps, ACT.Silu, after=[t]), [tok])
        self.ring.free(s, tl)
        self.fence_keep()
        MIX = self.H
        tmp = (self.alloc(T), self.alloc(T))
        rt = self.alloc(TC)
        QH, KH = self.alloc(4, T), self.alloc(4, T)
        vu = lambda s: s[:, 0:1536].rearrange("p (k n) -> p k n", k=2)
        vk = lambda s: s[:, 1536:2560]
        s, tok = self.ring.load((vu, io["mla_w_uq_2"][0].rearrange("(k p) n -> p k n", p=128)),
                                (vk, io["mla_w_ukv_2"][0]))
        su = s
        self.ring.held.add(su)
        sr = [self.ring.scratch() for _ in range(2)]
        fr_r = sr[0][1] + sr[1][1]
        st = self.att_state(32, None)
        wu, wk = vu(self.slots[s]), vk(self.slots[s])

        def latent():
            i, ps, rd = self.bank(4, 6)
            for m in range(2):
                ta = self.act.act(tmp[m], cq[:, m, :], ACT.Square)
                tp = self.pe.mm(ps[:, :], self.c("ones"), tmp[m], m == 0, m == 1, after=[ta] + rd, mark=True)
            te, tl = self.rstd(self.RS[:, :], ps[:, :], 256, [tp])
            self.drained[i] = [tl]
            for m in range(2):
                tn = self.dve.stt(cq[:, m, :], cq[:, m, :], self.v("mq_n", m), self.RS[:, :], ALU.mult, ALU.mult, after=[te, tp])
            tk = self.rms_heads(ckv, "ones", 128, T, 128, self.v("mkv_n"), [tn], tmp, 4, 6)
            yield
            v3 = wk.rearrange("p (h x) -> p h x", x=128)[:, :, 64:128]
            for j in range(4):
                i, ps, rd = self.bank(4, 6)
                tm = self.pe.mm(ps[:, :].rearrange("p (h x) -> p h x", x=64), ckv[:, 128 * j:128 * j + 128], v3, True, True,
                                after=[tk, tok] + rd, mark=True)
                tv = self.act.copy(vv[:, j, :], ps[:, :], after=[tm])
                self.drained[i] = [tv]
            yield
            free = []
            for half in range(2):
                prev = [tv, tk]
                for x in range(4):
                    h = 4 * half + x
                    q, k = QH[0:96, x, :], KH[0:96, x, :]
                    got = []

                    def outq(ps, t):
                        got.append(self.act.copy(q, ps, after=[t] + free))
                        return got[-1]

                    self.fm(wu, 96 * h, 96, 0, outq, [tok, tn], 4, 6, K=2, rhs=lambda kk: cq[:, kk, :])
                    i, ps, rd = self.bank(4, 6)
                    tm = self.pe.mm(ps[0:64, :], wk[:, 128 * h:128 * h + 64], ckv, True, True, after=[tok, tk] + rd, mark=True)
                    t1 = self.act.copy(KH[0:64, x, :], ps[0:64, :], after=[tm] + free)
                    self.drained[i] = [t1]
                    t2 = self.dve.copy(KH[64:96, x, :], kr[64:96, :], after=free)
                    yield
                    for y, gain, dep in ((q, "mqn", [got[0]]), (k, "mkn", [t1, t2])):
                        t = self.rms_heads(y, "ones", 96, T, 96, self.v(gain)[0:96], dep + prev, tmp, 4, 6)
                        t = self.rope(y[:, TC:T], 96, "rotM", "cosM", "sinM", [t], rt, 4, 6)
                        prev = [t]
                        yield
                if half:
                    self.ring.free(su, tm)
                units = []
                for x in range(4):
                    h = 4 * half + x
                    pb = 64 * (h % 2)
                    for c in range(4):
                        nk = TC if c < 2 else T
                        cs = slice(128 * c, 128 * c + 128)
                        units.append((QH[0:96, x, cs], KH[0:96, x, 0:nk], lambda j, h=h: vv[:, j, 64 * h:64 * h + 64],
                                      MIX[pb:pb + 64, h // 2, cs], nk, pb))
                yield from self.attend_steps(units, 96 ** -0.5, prev, st, 4)
                free = [self.pe.last(), st["out"]]

        lg = self.alloc(6, 16)
        rt2 = self.alloc(TC)
        za, zb = self.slots[sr[0][0]], self.slots[sr[1][0]]
        cut = lambda z, n: z[:, T * n:T * n + T]

        def retention():
            raw = self.v("lgf", 0, 16)
            y, w1, eq, num, den, lgm = (lg[:, j, :] for j in range(6))
            t = self.act.act(y, raw, ACT.Exp, scale=math.log(2.0))
            t = self.dve.ts(w1, y, -1.0, ALU.mult, 1.0, ALU.add, after=[t])
            te = self.dve.ts(eq, w1, 1.0, ALU.is_equal, after=[t])
            tl = self.act.act(num, w1, ACT.Ln, after=[t])
            tn = self.dve.add(num, num, eq, after=[te, tl])
            td = self.dve.stt(den, w1, 1.0, eq, ALU.subtract, ALU.add, after=[te])
            td = self.dve.do(lambda g: g.reciprocal(den, den), [td])
            t = self.dve.mul(num, num, den, after=[tn, td])
            t_lg = self.dve.stt(lgm, num, -1.0, y, ALU.mult, ALU.mult, after=[t])
            prev = []
            for x in (rq, rk):
                for m in range(4):
                    t = self.rope(x[:, m, TC:T], 128, "rotR", "cosR", "sinR", prev, rt2, 0, 2)
                    prev = [t]
                    yield
            F, R_, DJ, t1 = cut(za, 0), cut(za, 1), [cut(za, 2), cut(za, 3)], za[:, 2048:2176]
            PJ = zb[:, 0:2048].rearrange("p (j x) -> p j x", j=4)
            o, sq, r = cut(zb, 4), cut(zb, 5), cut(zb, 6)
            dfree, pfree, ofree, ffree = [], fr_r, fr_r, fr_r
            B_ = lambda x, m: x[:, 128 * m:128 * m + 128]
            for m in range(4):
                oi, ops, ord_ = self.bank(3, 4)
                for hh in range(2):
                    h, hb = 2 * m + hh, 64 * hh
                    ta = self.act.act(F, self.c("distF"), ACT.Exp, scale=lgm[:, h:h + 1], after=[t_lg] + ffree)
                    tb = self.act.act(R_, self.c("distR"), ACT.Exp, scale=lgm[:, 8 + h:9 + h], after=[t_lg] + ffree)
                    g = self.pool
                    a = [ta, tb] + dfree
                    u1 = g.mul(t1, B_(F, 0), self.c("mF"), after=a)
                    u2 = g.mul(B_(DJ[0], 0), B_(R_, 0), self.c("mR"), after=a)
                    u3 = g.add(B_(DJ[0], 0), B_(DJ[0], 0), t1, after=[u1, u2])
                    g.copy(B_(DJ[1], 1), B_(DJ[0], 0), after=[u3])
                    g.copy(B_(DJ[0], 1), B_(F, 1))
                    g.copy(B_(DJ[1], 0), B_(R_, 1))
                    g.add(B_(DJ[0], 2), B_(F, 2), B_(R_, 2))
                    g.add(B_(DJ[1], 3), B_(F, 2), B_(R_, 2))
                    g.add(B_(DJ[0], 3), B_(F, 3), B_(R_, 1))
                    td = g.add(B_(DJ[1], 2), B_(F, 1), B_(R_, 3))
                    ffree = [td]
                    yield
                    tp = []
                    for J in range(4):
                        a0 = 0 if J < 2 else TC
                        i, ps, rd = self.bank(0, 2)
                        tm = self.pe.mm(ps[:, a0:T], rk[hb:hb + 64, m, 128 * J:128 * J + 128], rq[hb:hb + 64, m, a0:T], True, True,
                                        after=prev + rd, mark=True)
                        tp.append(self.dve.mul(PJ[:, J, a0:T], ps[:, a0:T], DJ[J % 2][:, 0:T - a0], after=[tm, td] + pfree))
                        self.drained[i] = [tp[-1]]
                    dfree = [tp[-1]]
                    for J in range(4):
                        a0 = 0 if J < 2 else TC
                        tm = self.pe.mm(ops[hb:hb + 64, a0:T], rv[:, J, 64 * h:64 * h + 64], PJ[:, J, a0:T], J == 0, J == 3,
                                        after=[tp[J]] + ord_, mark=(J == 3))
                    pfree = [tm]
                    yield
                to = self.act.copy(o, ops[:, :], after=[tm] + ofree)
                self.drained[oi] = [to]
                i, ps, rd = self.bank(2, 3)
                tp = self.pe.mm(ps[:, :], self.c("bd"), o, True, True, after=[to] + rd, mark=True)
                tm_ = self.dve.stt(o, ps[:, :], -1.0 / 64, o, ALU.mult, ALU.add, after=[tp])
                self.drained[i] = [tm_]
                ta = self.act.act(sq, o, ACT.Square, after=[tm_])
                i, ps, rd = self.bank(2, 3)
                tp = self.pe.mm(ps[:, :], self.c("bd"), sq, True, True, after=[ta] + rd, mark=True)
                te, tl = self.rstd(r, ps[:, :], 64, [tp] + ofree)
                self.drained[i] = [tl]
                t = self.dve.mul(o, o, r, after=[te, ta])
                t = self.dve.mul(MIX[:, 4 + m, :], o, rg[:, m, :], after=[t])
                ofree = [t]
                yield

        self.together(latent(), retention(), self.next_mods())
        for i_, _ in sr:
            self.ring.free(i_, self.pe.last(), self.act.last(), self.dve.last(), self.pool.last())
        self.fence()
        if self.stop == "mlamix":
            return
        Y = self.alloc(KT, T)
        ys = self.down(io["w_out_2"][0], None, T, lambda k: MIX[:, k, :], 8, [[]] * 8, Y)
        self.fence_keep()
        self.resid(Y, 0, 1, False, ys)

    def cmul(self, o, a, b, t1, t2, after, sign=1):
        g, h = self.dve, self.pool
        x1 = g.mul(o[0], a[0], b[0], after=after)
        x2 = h.mul(t1, a[1], b[1], after=after)
        x3 = g.mul(o[1], a[0], b[1], after=after)
        x4 = h.mul(t2, a[1], b[0], after=after)
        ops = (ALU.subtract, ALU.add) if sign == 1 else (ALU.add, ALU.subtract)
        y1 = g.tt(o[0], o[0], t1, ops[0], after=[x1, x2])
        y2 = g.tt(o[1], o[1], t2, ops[1], after=[x3, x4])
        return y2

    def s5(self):
        io = self.io
        self.fence()
        self.norm_mod(0, 0, 0)
        self.fence()
        T1, T2 = self.alloc(2048), self.alloc(2048)
        P = self.alloc(2, 2048)
        Wb = self.alloc(4, 4, 2, 128)
        CA = self.alloc(2, 5 * 512)
        CA = [CA[:, i, :].rearrange("p (k j f x) -> p k j f x", k=5, j=4, f=4) for i in range(2)]
        V0 = self.alloc(2, 2048)
        aw = self.alloc(2, 5, 32)
        sm = self.RS[:, 0:384].rearrange("p (i q) -> p i q", q=32)
        ldt = self.RS[:, 384:480].rearrange("p (i q) -> p i q", q=32)
        sl = [self.ring.scratch() for _ in range(4)]
        LW = self.slots[sl[0][0]][:, 0:2048].rearrange("p (f t x) -> p f t x", f=4, t=4)
        sb_ = self.slots[sl[1][0]][:, :].rearrange("p (i q x) -> p i q x", i=4, q=32)
        Bb, Cc = (sb_[:, 0], sb_[:, 1]), (sb_[:, 2], sb_[:, 3])
        sc_ = self.slots[sl[2][0]]
        Br = [sc_[:, 1024 * i:1024 * i + 1024].rearrange("p (q x) -> p q x", q=32) for i in range(2)]
        Y = sc_[:, 2048:4096].rearrange("p (f n) -> p f n", f=8)
        V1 = self.slots[sl[3][0]][:, :].rearrange("p (i n) -> p i n", i=2)
        V = [V0, V1]
        WT = [self.slots[sl[0][0]][:, 2048:3072], self.slots[sl[0][0]][:, 3072:4096], sc_[:, 0:1024], sc_[:, 1024:2048]]
        fr = sl[0][1] + sl[1][1] + sl[2][1] + sl[3][1]
        U = self.H
        bd32 = self.c("bd32")
        V_, A_, g, h = self.dve, self.act, self.dve, self.pool
        power = lambda j: (aw[:, 0, j, :], aw[:, 1, j, :])
        dt, re, th, mag, c, s, k, r4, x, y, fre, fim = (sm[:, i, :] for i in range(12))
        ar, ai, ld = (ldt[:, i, :] for i in range(3))
        v3 = lambda z: z.rearrange("p (q n) -> p q n", q=16)
        temps = [(z[:, 1024 * i:1024 * i + 512], z[:, 1024 * i + 512:1024 * i + 1024]) for z in (T1, T2) for i in range(2)]
        f4 = lambda z: z.rearrange("p (f j x) -> p j f x", j=4, f=4)
        a4 = lambda z, fh: z[:, 16 * fh:16 * fh + 16].rearrange("p (j f) -> p j f", j=4).unsqueeze(3).broadcast_to([128, 4, 4, 32])
        c4 = lambda z, fh: z[:, 16 * fh:16 * fh + 16, :].rearrange("p (j f) x -> p j f x", j=4)
        bc = lambda q, n=32: q.unsqueeze(2).broadcast_to([128, q.shape[1], n])
        S = {"W": [], "CA": [], "LW": [], "V": [[], []], "tr": []}

        def prepare(d):
            free = fr + self.phase if d == 0 else S["l"] + [S["ca"], S["x"]]
            self.sp.dma(ldt, io["s5v"][d].rearrange("i p q -> p i q"), self.s_ld, free)
            self.sp.dma(sb_[:, 2:4], io["s5m"][d][2:4].rearrange("i p q x -> p i q x"), self.s_ld, free)
            for i in range(2):
                self.sp.dma(Br[i], io["s5m"][d][i], self.s_ld, free)
            self.n_ld += 64
            tl = [(self.s_ld, self.n_ld)]
            t = A_.act(dt, ld, ACT.Exp, after=tl + free)
            t1 = V_.mul(re, dt, ar, after=[t])
            t = V_.mul(th, dt, ai, after=[t])
            tm = A_.act(mag, re, ACT.Exp, after=[t1])
            t4 = A_.act(r4, re, ACT.Exp, scale=4.0, after=[t1])
            t = V_.ts(k, th, float(np.float32(1 / (2 * math.pi))), ALU.mult, after=[t])
            t = V_.ts(k, k, 12582912.0, ALU.add, after=[t])
            t = V_.ts(k, k, -12582912.0, ALU.add, after=[t])
            for part in (6.28125, 0.0019350051879882812, 3.0199159819e-07):
                t = V_.stt(th, k, -part, th, ALU.mult, ALU.add, after=[t])
            t = V_.ts(th, th, 3.1415925, ALU.min, -3.1415925, ALU.max, after=[t])
            ts = A_.act(s, th, ACT.Sin, after=[t])
            t = A_.act(x, th, ACT.Abs, after=[t])
            t = V_.ts(x, x, -1.0, ALU.mult, float(np.float32(math.pi / 2)), ALU.add, after=[t])
            tc = A_.act(c, x, ACT.Sin, after=[t])
            V_.do(lambda e: e.memset(aw[:, 0, 0, :], 1.0))
            t0 = V_.zero(aw[:, 1, 0, :])
            V_.mul(aw[:, 0, 1, :], mag, c, after=[tm, tc])
            t = V_.mul(aw[:, 1, 1, :], mag, s, after=[tm, ts])
            for j in range(2, 5):
                t = self.cmul(power(j), power(1), power(j - 1), x, y, [t])
            S["pw"] = [t, t0]
            t = V_.ts(x, aw[:, 0, 1, :], -1.0, ALU.add, after=[t])
            ta = V_.mul(fre, x, ar, after=[t])
            tb = V_.mul(y, aw[:, 1, 1, :], ai, after=[t])
            tr = V_.add(fre, fre, y, after=[ta, tb])
            ta = V_.mul(fim, aw[:, 1, 1, :], ar, after=[tr])
            tb = V_.mul(x, x, ai, after=[tr])
            ti = V_.sub(fim, fim, x, after=[ta, tb])
            ta = V_.mul(x, ar, ar, after=[ti])
            tb = V_.mul(y, ai, ai, after=[ti])
            t = V_.add(x, x, y, after=[ta, tb])
            t = V_.do(lambda e: e.reciprocal(x, x), [t])
            ta = V_.mul(fre, fre, x, after=[t])
            tb = V_.mul(fim, fim, x, after=[t])
            b1, b2 = (z[:, 0:1024].rearrange("p (q x) -> p q x", q=32) for z in (T1, T2))
            tB = self.cmul(Bb, (bc(fre), bc(fim)), Br, b1, b2, [ta, tb] + tl)
            tC = V_.ts(Cc[1], Cc[1], -1.0, ALU.mult, after=tl)
            S["B"], S["C"], S["tr"] = [tB], [tC], [tB]
            t = self.cmul((x, y), (c, s), (c, s), k, th, [tb, ts, tc, tB])
            t = self.cmul((c, s), (x, y), (x, y), k, th, [t])
            S["ph"], S["r4"] = [t], t4

        def phases(u):
            fh = u % 2
            hq = lambda z: z[:, 16 * fh:16 * fh + 16]
            P3 = (v3(P[:, 0, :]), v3(P[:, 1, :]))
            V_.do(lambda e: e.memset(P3[0][:, :, 0:1], 1.0), S["tr"])
            t = [V_.zero(P3[1][:, :, 0:1])] + S["ph"] + S["tr"]
            b1, b2 = v3(T1), v3(T2)
            cur, nxt, alt = (hq(c), hq(s)), (hq(x), hq(y)), (hq(fre), hq(fim))
            for lv in range(7):
                n = 1 << lv
                o = tuple(q[:, :, n:2 * n] for q in P3)
                a = tuple(q[:, :, 0:n] for q in P3)
                t = [self.cmul(o, (bc(cur[0], n), bc(cur[1], n)), a, b1[:, :, 0:n], b2[:, :, 0:n], t)]
                if lv < 6:
                    t = [self.cmul(nxt, cur, cur, hq(k), hq(th), t)]
                    cur, nxt = nxt, (alt if lv == 0 else cur)
            S["P"] = t

        def weights(u):
            fh = u % 2
            S["WT"] = []
            for s_ in range(4):
                pw, tp = power(3 - s_), temps[s_]
                S["WT"].append(self.cmul((f4(WT[s_][:, 0:512]), f4(WT[s_][:, 512:1024])), (a4(pw[0], fh), a4(pw[1], fh)),
                                         (c4(Bb[0], fh), c4(Bb[1], fh)), f4(tp[0]), f4(tp[1]),
                                         S["B"] + S["pw"] + S["tr"] + S["scan"] + S["temps"]))

        def inputs(u):
            d, fh = divmod(u, 2)
            for s_ in range(4):
                for i in range(2):
                    bi, ps, rd = self.bank(0, 4)
                    for f in range(4):
                        lh = WT[s_][:, 512 * i + 128 * f:512 * i + 128 * f + 128]
                        tm = self.pe.mm(ps[:, 128 * f:128 * f + 128], lh, self.c("ident"), True, True,
                                        after=[S["WT"][s_]] + rd, mark=(f == 3))
                    te = A_.copy(Wb[:, :, s_, i, :], ps[:, :].rearrange("p (f x) -> p f x", f=4), after=[tm] + S["W"])
                    self.drained[bi] = [te]
            S["tr"] = [tm]
            tv = []
            for j in range(4):
                for i in range(2):
                    bi, ps, rd = self.bank(0, 4)
                    for f in range(4):
                        for s_ in range(4):
                            v = U[32 * j:32 * j + 32, 4 * fh + f, :]
                            o = ps[:, 128 * f:128 * f + 128]
                            if d == 0:
                                v = v.rearrange("p (n s) -> p n s", s=4)[:, :, s_]
                            else:
                                v = v.rearrange("p (g n) -> p g n", g=2)[:, :, 255 - s_::-4]
                                o = o.rearrange("p (g n) -> p g n", g=2)
                            tm = self.pe.mm(o, Wb[32 * j:32 * j + 32, f, s_, i, :], v, s_ == 0, s_ == 3,
                                            after=[te] + rd, mark=(f == 3 and s_ == 3))
                    t = A_.copy(V[u % 2][:, i, 512 * j:512 * j + 512], ps[:, :], after=[tm] + S["V"][u % 2])
                    self.drained[bi] = [t]
                    tv.append(t)
            S["W"] = [tm]
            S["in", u] = tv

        def scan(u):
            fh = u % 2
            pr, pi = P[:, 0, :], P[:, 1, :]
            Vr, Vi = V[u % 2][:, 0, :], V[u % 2][:, 1, :]
            al = S["in", u] + S["P"] + S["WT"][-1:] + S["temps"]
            x1 = g.mul(T1, pr, Vr, after=al)
            x2 = h.mul(T2, pi, Vi, after=al)
            y1 = g.add(T1, T1, T2, after=[x1, x2])
            x4 = h.mul(Vr, pi, Vr, after=[x1])
            x3 = g.mul(T2, pr, Vi, after=[y1])
            y2 = g.sub(T2, T2, Vr, after=[x3, x4])
            tr_ = A_.copy(v3(Vi), bc(r4[:, 16 * fh:16 * fh + 16], 128), after=[x2, x3, S["r4"]])
            tr_ = A_.act(v3(Vi)[:, :, 0:1], v3(Vi)[:, :, 0:1], ACT.Copy, scale=0.0, after=[tr_])
            z1 = g.do(lambda e: e.tensor_tensor_scan(Vr, Vi, T1, 0.0, ALU.mult, ALU.add), [tr_, y1, y2])
            z2 = g.do(lambda e: e.tensor_tensor_scan(T1, Vi, T2, 0.0, ALU.mult, ALU.add), [z1, y2])
            x1 = h.mul(T2, pi, T1, after=[z2])
            x2 = g.mul(Vi, pr, Vr, after=[z2])
            x4 = h.mul(Vr, pi, Vr, after=[x2])
            y1 = g.sub(Vi, Vi, T2, after=[x1, x2])
            x3 = g.mul(T2, pr, T1, after=[y1])
            S["x"] = g.add(Vr, Vr, T2, after=[x3, x4])
            S["scan"] = [S["x"]]

        def readouts(u):
            fh = u % 2
            for k_ in range(5):
                pw, tp = power(k_), temps[k_ % 4]
                t = self.cmul((CA[0][:, k_], CA[1][:, k_]), (a4(pw[0], fh), a4(pw[1], fh)), (c4(Cc[0], fh), c4(Cc[1], fh)),
                              f4(tp[0]), f4(tp[1]), S["C"] + S["pw"] + S["CA"] + S["scan"] + ([tk] if k_ == 4 else []), sign=-1)
                if k_ == 0:
                    tk = t
            S["temps"], S["ca"] = [t], t
            S["l"] = []
            for f in range(4):
                bi, ps, rd = self.bank(4, 8)
                for j in range(4):
                    for i in range(2):
                        tm = self.pe.mm(ps[32 * j:32 * j + 32, 0:128].rearrange("p (t x) -> p t x", x=32),
                                        Bb[i][:, 16 * fh + 4 * j + f, :], CA[i][:, 0:4, j, f, :], i == 0, i == 1,
                                        after=[t] + S["B"] + rd, mark=(j == 3 and i == 1))
                src = ps[:, 0:128].rearrange("p (t x) -> p t x", x=32).unsqueeze(2).broadcast_to([128, 4, 4, 32])
                mk = bd32.rearrange("p (j x) -> p j x", j=4).unsqueeze(1).broadcast_to([128, 4, 4, 32])
                S["l"].append(g.mul(LW[:, f].rearrange("p t (j x) -> p t j x", j=4), src, mk, after=[tm] + S["LW"]))
                self.drained[bi] = [S["l"][-1]]

        def outputs(u):
            d, fh = divmod(u, 2)
            XX = [v3(V[u % 2][:, 1, :]), v3(V[u % 2][:, 0, :])]
            S["o"] = []
            for f in range(4):
                F_ = 4 * fh + f
                bi, ps, rd = self.bank(4, 8)
                lat = U[:, F_, TC:T] if d == 0 else U[:, F_, T - 1:TC - 1:-1]
                lat = lat.rearrange("p (n s) -> p s n", s=4)
                o = ps[:, 0:256].rearrange("p (s n) -> p s n", s=4)
                for tau in range(4):
                    self.pe.mm(o[:, tau:4, :], LW[:, f, tau, :], lat[:, 0:4 - tau, :], tau == 0, False,
                               after=[S["l"][f]] + rd)
                for j in range(4):
                    q = 4 * j + f
                    for s_ in range(4):
                        for i in range(2):
                            tm = self.pe.mm(o[32 * j:32 * j + 32, s_, :], CA[i][:, s_ + 1, j, f, :],
                                            XX[i][:, q, 63:127], False, s_ == 3 and i == 1, after=[S["x"]],
                                            mark=(j == 3 and s_ == 3 and i == 1))
                S["o"].append((bi, o, tm))
            S["CA"] = S["LW"] = S["V"][u % 2] = [tm]

        def collect(u, outs):
            d, fh = divmod(u, 2)
            for f, (bi, o, tm) in enumerate(outs):
                yf = Y[:, 4 * fh + f, :]
                if d == 0:
                    ty = g.copy(yf.rearrange("p (n s) -> p s n", s=4), o, after=[tm] + fr)
                else:
                    yv = yf[:, 255::-1].rearrange("p (n s) -> p s n", s=4)
                    ty = g.add(yv, o, yv, after=[tm])
                self.drained[bi] = [ty]

        S["scan"], S["temps"] = [], []
        prepare(0)
        weights(0)
        inputs(0)
        phases(0)
        S["scan"] = S["P"]
        weights(1)
        inputs(1)
        scan(0)
        readouts(0)
        phases(1)
        outputs(0)
        collect(0, S["o"])
        scan(1)
        readouts(1)
        prepare(1)
        weights(2)
        outputs(1)
        o1 = S["o"]
        inputs(2)
        phases(2)
        S["scan"] = S["P"]
        collect(1, o1)
        weights(3)
        inputs(3)
        scan(2)
        readouts(2)
        phases(3)
        outputs(2)
        collect(2, S["o"])
        scan(3)
        readouts(3)
        outputs(3)
        collect(3, S["o"])
        self.fence_keep()
        self.at = 0
        G = self.alloc(KT, TC)
        O = self.alloc(KT, TC)
        sgm = [self.alloc(TC), self.alloc(TC)]
        tg = []
        for f in range(8):
            t = self.dve.stt(Y[:, f, :], U[:, f, TC:T], self.v("s5d", f), Y[:, f, :], ALU.mult, ALU.add)
            tg.append(self.act.act(G[:, f, :], Y[:, f, :], ACT.Gelu_apprx_tanh, after=[t]))
        for i, _ in sl:
            self.ring.free(i, tg[-1])
        sfree = [[], []]
        ys = []
        for g_ in range(4):
            view = lambda s: s[:, :].rearrange("p (u k n) -> p u k n", u=2, k=KT)
            Wg = io["s5_w_glu_2"][0]
            s, tok = self.ring.load(*[
                (lambda s, a=a: view(s)[:, a], Wg[:, D * a + 256 * g_:D * a + 256 * g_ + 256].rearrange("(k p) n -> p k n", p=128))
                for a in range(2)])
            w = view(self.slots[s])
            for m in range(2):
                xx = 2 * g_ + m

                def zb(ps, t, xx=xx):
                    t = self.act.act(sgm[xx % 2], ps, ACT.Sigmoid, after=[t] + sfree[xx % 2])
                    sfree[xx % 2] = [t]
                    return t

                def za(ps, t, xx=xx):
                    t = self.dve.mul(O[:, xx, :], ps, sgm[xx % 2], after=[t] + sfree[xx % 2])
                    sfree[xx % 2] = [t]
                    ys.append(t)
                    return t

                rh = lambda k: G[:, k, :]
                self.fm(w[:, 1], 128 * m, 128, TC, zb, [tok, tg[-1]], 0, 6, rhs=rh)
                tm = self.fm(w[:, 0], 128 * m, 128, TC, za, [tok, tg[-1]], 0, 6, rhs=rh)
            self.ring.free(s, tm)
        if self.stop == "s5mix":
            for f in range(8):
                self.dve.copy(self.H[:, f, TC:T], O[:, f, :], after=ys)
            return
        self.resid(O, TC, 1, False, ys)


def constants():
    c = np.zeros((128, NCST), np.float32)

    def put(name, a, rows=128):
        at, n = CST[name]
        c[:rows, at:at + a.shape[1]] = a

    p = np.arange(128)
    x = np.arange(512)
    put("ident", np.eye(128, dtype=np.float32))
    put("ones", np.ones((128, 128), np.float32))
    put("bd", (p[:, None] // 64 == p[None, :] // 64).astype(np.float32))
    put("bd32", (p[:, None] // 32 == p[None, :] // 32).astype(np.float32))
    r = np.zeros((128, 128), np.float32)
    r[p[1::2], p[0::2]] = -1
    r[p[0::2], p[1::2]] = 1
    put("rotE", r)
    r = np.zeros((128, 128), np.float32)
    a = 64 + np.arange(16)
    r[a + 16, a] = -1
    r[a, a + 16] = 1
    put("rotM", r)
    r = np.zeros((128, 128), np.float32)
    a = np.concatenate([np.arange(32), 64 + np.arange(32)])
    r[a + 32, a] = -1
    r[a, a + 32] = 1
    put("rotR", r)
    m = np.ones((128, 516), np.float32)
    m[:, ::129] = 0
    put("smask", m)
    put("distF", np.maximum(x[None] - p[:, None], 0).astype(np.float32))
    put("distR", np.maximum(128 * (x[None] // 128) + p[:, None] - x[None] % 128, 0).astype(np.float32))
    put("mF", (p[None] >= p[:, None]).astype(np.float32))
    put("mR", (p[:, None] > p[None]).astype(np.float32))
    f4 = np.float32
    n = np.arange(256)
    row, col = (n // 64).astype(f4), (n % 64).astype(f4)
    inv = (f4(10000.0) ** (-np.arange(0, 32, 2, dtype=f4) / f4(32))).astype(f4)
    ang = np.concatenate([row[:, None] * inv, col[:, None] * inv], -1).astype(f4)
    fe = (p % 64) // 2
    put("cosE", np.cos(ang)[:, fe].T.astype(f4))
    put("sinE", np.sin(ang)[:, fe].T.astype(f4))
    f = (f4(10000.0) ** (-np.arange(8, dtype=f4) / f4(8))).astype(f4)
    ang = np.concatenate([row[:, None] * f, col[:, None] * f], -1).astype(f4)
    co, si = np.ones((128, 256), f4), np.zeros((128, 256), f4)
    for half in range(2):
        co[64 + 16 * half:80 + 16 * half] = np.cos(ang).T
        si[64 + 16 * half:80 + 16 * half] = np.sin(ang).T
    put("cosM", co)
    put("sinM", si)
    th = (f4(10000.0) ** (-np.arange(32, dtype=f4) / f4(32))).astype(f4)
    ang = (n.astype(f4)[:, None] * th).astype(f4)
    put("cosR", np.cos(ang)[:, p % 32].T.astype(f4))
    put("sinR", np.sin(ang)[:, p % 32].T.astype(f4))
    k = np.zeros((128, 15, 128), np.float32)
    for li, L in enumerate(LEVELS):
        same = p[:, None] // (2 * L) == p[None] // (2 * L)
        late = (p // L) % 2 == 1
        k[:, li] = same & ~late[:, None] & late[None]
        k[:, 7 + li] = same & late[:, None] & ~late[None]
    k[:, 14] = np.eye(128)
    return c, k


def layouts(a):
    f = lambda x: np.ascontiguousarray(x)
    vec = np.zeros((128, NVEC), np.float32)

    def put(name, x, rows=128):
        at, n = VEC[name]
        assert x.shape == (rows, n), (name, x.shape)
        vec[:rows, at:at + n] = x

    col = lambda x: np.asarray(x).reshape(-1, 128).T
    put("c", col(a["c"]))
    put("cc", col(a["c_ctx"]))
    put("c2", col(a["c_2"]))
    put("cc2", col(a["c_ctx_2"]))
    put("mod_b", col(a["mod_b"]))
    put("ada_b", col(a["ada_b_2"]))
    for n, m in (("pre_mix", "norm_pre_mix"), ("post_mix", "norm_post_mix"), ("pre_ffn", "norm_pre_ffn"),
                 ("post_ffn", "norm_post_ffn"), ("n1", "norm1_g_2"), ("n2", "norm2_g_2"), ("gla_b", "gla_b_gate"),
                 ("gla_n", "gla_out_norm"), ("lb", "hgrn_lower_bounds"), ("hg_n", "hgrn_out_norm"),
                 ("mq_n", "mla_q_norm_g_2"), ("mkv_n", "mla_kv_norm_g_2"), ("s5d", "s5_d_2")):
        put(n, col(a[m]))
    put("aq_n", np.tile(np.asarray(a["att_q_norm"]).reshape(64, 1), (2, 1)))
    put("ak_n", np.tile(np.asarray(a["att_k_norm"]).reshape(64, 1), (2, 1)))
    put("mqn", np.asarray(a["mla_qn_g_2"]).reshape(96, 1), 96)
    put("mkn", np.asarray(a["mla_kn_g_2"]).reshape(96, 1), 96)
    put("lgf", np.tile(np.asarray(a["ret_lg_f_2"]).reshape(1, 8), (128, 1)))
    put("lgb", np.tile(np.asarray(a["ret_lg_b_2"]).reshape(1, 8), (128, 1)))
    put("eps", np.full((128, 1), EPS, np.float32))
    put("one", np.ones((128, 1), np.float32))
    gw = np.zeros((32, 2, 256), np.float32)
    for d in range(2):
        gw[16 * d:16 * d + 16, d] = np.asarray(a["gla_w_gate"])[0, d]
    fm = lambda x: np.asarray(x).reshape(-1, 8, 128).transpose(2, 1, 0)
    xT = np.concatenate([fm(a["ctx"]), fm(a["x"])], 2)
    cst, msk = constants()
    out = {"vec": vec, "cst": cst, "msk": msk, "xT": f(xT), "x2T": f(fm(a["ctx_2"])), "gla_gw": gw.reshape(32, 512)}
    g = np.array([[8 * (4 * r + ff) + 2 * j + h for h in range(2)] for r in range(2) for j in range(4) for ff in range(4)])
    s5v = np.zeros((2, 3, 128, 32), np.float32)
    s5m = np.zeros((2, 4, 128, 32, 32), np.float32)
    for i, d in enumerate("fb"):
        for n, name in enumerate(("s5_a_re_", "s5_a_im_")):
            x = np.asarray(a[name + d + "_2"])[0]
            s5v[i, n] = x[g].transpose(1, 2, 0).reshape(128, 32)
        s5v[i, 2] = np.repeat(np.asarray(a["s5_log_dt_" + d + "_2"])[0][g].T, 64, 0)
        for n, name in enumerate(("s5_b_re_", "s5_b_im_", "s5_c_re_", "s5_c_im_")):
            x = np.asarray(a[name + d + "_2"])[0][g]
            if n >= 2:
                x = x.transpose(0, 1, 3, 2)
            for h in range(2):
                s5m[i, n, 64 * h:64 * h + 64, :, 16 * h:16 * h + 16] = x[:, h].transpose(1, 0, 2)
    out["s5v"], out["s5m"] = s5v, s5m
    for name in WEIGHTS:
        out[name] = f(np.asarray(a[name]))
    return out


WEIGHTS = ("mod_w", "even_w_in", "even_w_out", "odd_w_in", "odd_w_out", "ffn_w_gate", "ffn_w_up", "ffn_w_down",
           "ada_w_2", "mlp_w1_2", "mlp_w2_2", "w_in_2", "mla_w_uq_2", "mla_w_ukv_2", "w_out_2", "s5_w_glu_2")


def build(nc, shapes, stop=None):
    io = {}
    for name, (shape, dt) in shapes.items():
        io[name] = nc.dram_tensor(name, shape, dt, kind="ExternalInput").ap()
    n = T if stop else TC
    io["outX"] = nc.dram_tensor("outX", (128, KT, n), F32, kind="ExternalOutput").ap()
    with ExitStack() as ctx:
        p = Program(nc, ctx, io, stop)
        run_program(p, stop)


def run_program(p, stop):
    io = p.io
    first = ("pre_mix", "post_mix", "pre_ffn", "post_ffn")
    second = ("n1", None, "n2", None)
    mods = [p.mods_steps(0, io["mod_w"], "mod_b", 0, 0, *first), p.mods_steps(1, io["mod_w"], "mod_b", 0, 1, *first),
            p.mods_steps(2, io["ada_w_2"], "ada_b", 1, 0, *second), p.mods_steps(3, io["ada_w_2"], "ada_b", 1, 1, *second)]
    at = [0]

    def next_mods():
        at[0] += 1
        return mods[at[0]]

    p.next_mods = next_mods
    steps = [
        ("even", lambda: (p.begin(), p.together(mods[0]), p.use(0), p.even())),
        ("ffn0", lambda: p.ffn_swiglu(0, 0)),
        ("odd", lambda: (p.use(1), p.odd())),
        ("ffn1", lambda: p.ffn_swiglu(1, TC)),
        ("mla", lambda: (p.use(2), p.mla())),
        ("mlp0", lambda: p.ffn_sq(0, 0)),
        ("s5", lambda: (p.use(3), p.s5())),
        ("mlp1", lambda: p.ffn_sq(1, TC)),
    ]
    for name, f in steps:
        f()
        if stop and name == stop.replace("mix", ""):
            break
    p.finish()


def kernel(**inputs):
    import concourse.bacc as bacc
    from concourse.bass_utils import run_bass_kernel_spmd

    arrays = layouts(inputs)
    nc = bacc.Bacc("TRN2", target_bir_lowering=False, num_devices=1)
    build(nc, {n: (x.shape, mybir.dt.from_np(x.dtype)) for n, x in arrays.items()})
    r = run_bass_kernel_spmd(nc, [arrays], core_ids=[0])
    out = r.results[0]["outX"]
    return np.ascontiguousarray(out.transpose(2, 1, 0).reshape(1, TC, D))
```

```python
from contextlib import ExitStack
import itertools
import math

import numpy as np

import concourse.bass as bass
from concourse import mybir

F32 = mybir.dt.float32
F32R = mybir.dt.float32r
U8 = mybir.dt.uint8
ALU = mybir.AluOpType
ACT = mybir.ActivationFunctionType
AX = mybir.AxisListType

D = 1024
KT = 8
T = 512
TC = 256
FF1 = 2816
FF2 = 4096
EPS = 1e-6
LEVELS = (64, 32, 16, 8, 4, 2, 1)

VEC = {}


def _vec_layout():
    at = 0
    for name, n in (
        ("c", 8), ("cc", 8), ("c2", 8), ("cc2", 8),
        ("mod_b", 96), ("ada_b", 96),
        ("pre_mix", 16), ("post_mix", 16), ("pre_ffn", 16), ("post_ffn", 16),
        ("n1", 16), ("n2", 16),
        ("gla_b", 4), ("gla_n", 1), ("aq_n", 1), ("ak_n", 1),
        ("lb", 32), ("hg_n", 1),
        ("mq_n", 2), ("mkv_n", 1), ("mqn", 1), ("mkn", 1),
        ("lgf", 8), ("lgb", 8), ("s5d", 8), ("eps", 1), ("one", 1),
    ):
        VEC[name] = (at, n)
        at += n
    return at


NVEC = _vec_layout()

CST = {}


def _cst_layout():
    at = 0
    for name, n in (
        ("ident", 128), ("ones", 128), ("bd", 128), ("rotE", 128), ("rotM", 128), ("rotR", 128),
        ("smask", 516), ("distF", 512), ("distR", 512), ("mF", 128), ("mR", 128), ("bd32", 128),
        ("cosE", 256), ("sinE", 256), ("cosM", 256), ("sinM", 256), ("cosR", 256), ("sinR", 256),
    ):
        CST[name] = (at, n)
        at += n
    return at


NCST = _cst_layout()


class Lane:

    def __init__(self, name, sem):
        self.name, self.sem, self.items, self.n, self.held = name, sem, [], 0, []

    def do(self, f, after=(), mark=True, inc=1, sem=None):
        waits = list(after) + self.held
        self.held = []
        if mark:
            self.n += 1
        self.items.append([waits, f, self.sem if mark else None, 1])
        return (self.sem, self.n)

    def dma(self, out, in_, sem, after=()):
        waits = list(after) + self.held
        self.held = []
        self.items.append([waits, lambda e: e.dma_start(out, in_), sem, 16])

    def last(self):
        if self.items and self.items[-1][2] is None:
            self.n += 1
            self.items[-1][2] = self.sem
        return (self.sem, self.n)

    def play(self, e):
        seen = {}
        for waits, f, sem, inc in self.items:
            need = {}
            for s, v in waits:
                if v > need.get(id(s), (s, 0))[1]:
                    need[id(s)] = (s, v)
            for k, (s, v) in need.items():
                if v > seen.get(k, 0):
                    e.wait_ge(s, v)
                    seen[k] = v
            if f is not None:
                i = f(e)
                if sem is not None:
                    i.then_inc(sem, inc)


class Vec(Lane):
    def tt(self, out, a, b, op, after=()):
        return self.do(lambda e: e.tensor_tensor(out, a, b, op), after)

    def mul(self, out, a, b, after=()):
        return self.tt(out, a, b, ALU.mult, after)

    def add(self, out, a, b, after=()):
        return self.tt(out, a, b, ALU.add, after)

    def sub(self, out, a, b, after=()):
        return self.tt(out, a, b, ALU.subtract, after)

    def ts(self, out, a, s1, op0, s2=None, op1=None, after=()):
        if op1 is None:
            return self.do(lambda e: e.tensor_scalar(out, a, s1, None, op0), after)
        return self.do(lambda e: e.tensor_scalar(out, a, s1, s2, op0, op1), after)

    def stt(self, out, a, s, b, op0, op1, after=()):
        return self.do(lambda e: e.scalar_tensor_tensor(out=out, in0=a, scalar=s, in1=b, op0=op0, op1=op1), after)

    def copy(self, out, a, after=()):
        return self.do(lambda e: e.tensor_copy(out, a), after)

    def zero(self, out, after=()):
        return self.do(lambda e: e.memset(out, 0.0), after)


LN_EXP = "natural_log_exp_and_others"
TABLES = {ACT.Exp: LN_EXP, ACT.Ln: LN_EXP, ACT.Sigmoid: "sigmoid_and_others", ACT.Silu: "silu_and_others",
          ACT.Sin: "silu_and_others", ACT.Gelu_apprx_tanh: "gelu_apprx_tanh_and_others"}


class Act(Lane):
    table = None

    def need(self, func):
        t = TABLES.get(func)
        if t and t != self.table:
            self.table = t
            held, self.held = self.held, []
            self.do(lambda e: e.preload_act_table_set(t), mark=False)
            self.held = held

    def act(self, out, a, func, scale=1.0, bias=0.0, accum=None, after=()):
        self.need(func)
        if accum is None:
            return self.do(lambda e: e.activation(out, a, func, bias=bias, scale=scale), after)
        return self.do(lambda e: e.activation(out, a, func, bias=bias, scale=scale, accum_out=accum), after)

    def copy(self, out, a, after=()):
        return self.do(lambda e: e.activation(out, a, ACT.Copy), after)


class Pe(Lane):
    def mm(self, out, lhsT, rhs, start, stop, after=(), mark=False):
        return self.do(lambda e: e.matmul(out, lhsT, rhs, start=start, stop=stop, skip_group_check=True), after, mark)

    def mm3(self, out, w, x, start, stop, after=(), mark=False):
        for n, (i, j) in enumerate(((0, 1), (0, 0), (1, 0))):
            t = self.mm(out, w[i], x[j], start and n == 0, stop and n == 2, after=after if n == 0 else (),
                        mark=mark and n == 2)
        return t

    def tr(self, out, a, ident, after=(), mark=False):
        return self.do(lambda e: e.transpose(out, a, ident), after, mark)


class Ring:

    def __init__(self, sp, slots, sems):
        self.sp, self.slots, self.sems = sp, slots, sems
        self.held = set()
        self.at, self.count, self.users = 0, [0] * len(slots), [[] for _ in slots]

    def next(self):
        while self.at % len(self.slots) in self.held:
            self.at += 1
        self.at += 1
        return (self.at - 1) % len(self.slots)

    def load(self, *parts):
        i = self.next()
        for k, (view, src) in enumerate(parts):
            self.sp.dma(view(self.slots[i]), src, self.sems[i], self.users[i] if k == 0 else ())
            self.count[i] += 16
        return i, (self.sems[i], self.count[i])

    def free(self, i, *tokens):
        self.users[i] = list(tokens)
        self.held.discard(i)

    def scratch(self):
        i = self.next()
        self.held.add(i)
        return i, list(self.users[i])


class Program:
    def __init__(self, nc, ctx, io, stop=None):
        self.nc, self.ctx, self.io, self.stop = nc, ctx, io, stop
        sem = lambda n: ctx.enter_context(nc.semaphore(n))
        self.sb = lambda n, shape, dt=F32: ctx.enter_context(nc.sbuf_tensor("sb_" + n, shape, dt))
        self.pe, self.act, self.dve, self.pool, self.sp = (
            Pe("pe", sem("pe_n")), Act("act", sem("act_n")), Vec("dve", sem("dve_n")),
            Vec("pool", sem("pool_n")), Lane("sp", sem("sp_n")))
        self.vec = self.sb("vec", [128, NVEC])
        self.cst = self.sb("cst", [128, NCST])
        self.msk = self.sb("msk", [128, 15, 128], U8)
        self.X = self.sb("X", [128, KT, T])
        self.H = self.sb("H", [128, KT, T])
        self.SX = self.sb("SX", [128, 2, KT, 2])
        self.MM = [self.sb(f"M{i}", [128, 48, 2]) for i in range(2)]
        self.COS = [self.sb(f"CO{i}", [128, 4, 2, KT]) for i in range(2)]
        self.t_cos = [None, None]
        self.RW = self.sb("RW", [128, 512])
        self.RS = self.sb("RS", [128, T])
        self.NW = 22816 - 512 - 160
        self.slots = [self.sb(f"slot{i}", [128, 4096]) for i in range(2)]
        with ExitStack() as st:
            a = lambda n, shape, dt=F32: st.enter_context(nc.sbuf_tensor("sb_" + n, shape, dt))
            self.slots += [a(f"slot{i}", [128, 4096]) for i in (2, 3)]
            self.R = a("R", [128, self.NW])
        with ExitStack() as st:
            a = lambda n, shape, dt=F32: st.enter_context(nc.sbuf_tensor("sb_" + n, shape, dt))
            self.HP = a("HP", [128, 2, KT, T], F32R)
            self.WP = a("WP", [128, 4, 2, 1024], F32R)
            self.XP = a("XP", [128, 4, 2, T], F32R)
            self.R2 = a("R2", [128, self.NW - 12288])
        self.ring = Ring(self.sp, self.slots, [sem(f"ring{i}") for i in range(4)])
        self.ps = [ctx.enter_context(nc.psum_tensor(f"ps{i}", [128, 512], F32)) for i in range(8)]
        self.drained = [[] for _ in range(8)]
        self.turn = {}
        self.s_in, self.s_x, self.s_ld, self.s_out = sem("s_in"), sem("s_x"), sem("s_ld"), sem("s_out")
        self.n_ld = 0
        self.at = 0

    def alloc(self, *shape):
        n = int(np.prod(shape))
        assert self.at + n <= self.NW, (self.at, n)
        v = self.R[:, self.at:self.at + n]
        self.at += n
        if len(shape) == 2:
            v = v.rearrange("p (a b) -> p a b", b=shape[1])
        if len(shape) == 3:
            v = v.rearrange("p (a b c) -> p a b c", b=shape[1], c=shape[2])
        if len(shape) == 4:
            v = v.rearrange("p (a b c d) -> p a b c d", b=shape[1], c=shape[2], d=shape[3])
        return v

    def room2(self, *shape):
        n = int(np.prod(shape))
        assert self.at + n <= self.NW - 12288, (self.at, n)
        v = self.R2[:, self.at:self.at + n]
        self.at += n
        return v.rearrange("p (a b) -> p a b", b=shape[1]) if len(shape) == 2 else v

    def v(self, name, i=0, n=1):
        a, _ = VEC[name]
        return self.vec[:, a + i:a + i + n]

    def c(self, name, n=None, p0=0, p1=128):
        a, w = CST[name]
        return self.cst[p0:p1, a:a + (w if n is None else n)]

    def bank(self, lo=0, hi=8):
        i = lo + self.turn.get((lo, hi), 0) % (hi - lo)
        self.turn[lo, hi] = self.turn.get((lo, hi), 0) + 1
        return i, self.ps[i], list(self.drained[i])

    def fence(self):
        lanes = (self.pe, self.act, self.dve, self.pool)
        tokens = [l.last() for l in lanes]
        for l in lanes:
            l.held = l.held + tokens
        self.phase = tokens
        self.drained = [[] for _ in range(8)]
        self.at = 0

    def load(self, out, src):
        self.sp.dma(out, src, self.s_ld, self.phase)
        self.n_ld += 16
        return (self.s_ld, self.n_ld)

    def wslot(self, W, c0, c1, l=None):
        n = c1 - c0
        src = W if l is None else W[l]
        view = lambda s: s[:, 0:KT * n].rearrange("p (k n) -> p k n", k=KT)
        i, tok = self.ring.load((view, src[:, c0:c1].rearrange("(k p) n -> p k n", p=128)))
        return i, view(self.slots[i]), tok

    def begin(self):
        io = self.io
        for out, name in ((self.vec[:, :], "vec"), (self.cst[:, :], "cst"), (self.R[:, 64:64 + 1920].rearrange("p (a b) -> p a b", b=128), "msk")):
            self.sp.dma(out, io[name], self.s_in)
        t_in = (self.s_in, 48)
        self.sp.dma(self.X[:, :, :], io["xT"], self.s_x)
        self.t_x = (self.s_x, 16)
        for lane in (self.pe, self.act, self.dve, self.pool):
            lane.held.append(t_in)
        e = self.R[:, 0:32]
        a, _ = VEC["c"]
        src = self.vec[:, a:a + 32]
        t = self.act.act(e, src, ACT.Exp, scale=-1.0)
        t = self.dve.ts(e, e, 1.0, ALU.add, after=[t])
        t = self.dve.do(lambda g: g.reciprocal(self.R[:, 32:64], e), [t])
        src4 = src.rearrange("p (b w k) -> p b w k", b=2, w=2)
        r4 = self.R[:, 32:64].rearrange("p (b w k) -> p b w k", b=2, w=2)
        for b in range(2):
            for w in range(2):
                t = self.dve.mul(self.SX[:, b, :, w], src4[:, b, w, :], r4[:, b, w, :], after=[t])
        self.t_sx = t
        self.t_rw = self.dve.zero(self.RW[:, :])
        self.dve.copy(self.msk[:, :, :], self.R[:, 64:64 + 1920].rearrange("p (a b) -> p a b", b=128))
        self.epsc = self.v("eps")
        self.act.held.append(self.t_x)
        self.dve.held.append(self.t_x)

    def use(self, n):
        self.M, self.CO, self.t_co = self.MM[n % 2], self.COS[n % 2], self.t_cos[n % 2]

    def mods_steps(self, par, W, bias, blk, l, pre, post, pre2, post2):
        M, CO = self.MM[par % 2], self.COS[par % 2]
        tt = []
        for r in range(3):
            te = []
            i, ps, rd = self.bank(7, 8)
            for j in range(4):
                g = 4 * r + j
                s, view, tok = self.wslot(W, 512 * g, 512 * g + 512, l)
                for k in range(KT):
                    tm = self.pe.mm(ps[32 * j:32 * j + 2, :], self.SX[:, blk, k, :], view[:, k, :],
                                    k == 0, k == KT - 1, after=[tok, self.t_sx] + rd, mark=(k == KT - 1))
                    if k == 3:
                        yield
                self.ring.free(s, tm)
                te.append(self.act.copy(self.RW[32 * j:32 * j + 2, :], ps[32 * j:32 * j + 2, :],
                                        after=[tm, self.t_rw] + tt))
                yield
            self.drained[i] = te
            i, ps, rd = self.bank(7, 8)
            for m in range(4):
                tm = self.pe.mm(ps[:, 128 * m:128 * m + 128], self.RW[:, 128 * m:128 * m + 128], self.c("ident"),
                                True, True, after=te + rd, mark=(m == 3))
            tt = [tm]
            P = ps[:, :].rearrange("p (m j x) -> p m j x", m=4, j=4)
            at = VEC[bias][0] + 48 * l + 16 * r
            bb = self.vec[:, at:at + 16].rearrange("p (j m) -> p m j", j=4)
            for w in range(2):
                t = self.dve.add(M[:, 16 * r:16 * r + 16, w].rearrange("p (j m) -> p m j", j=4), P[:, :, :, w], bb,
                                 after=[tm])
            self.drained[i] = [t]
            yield
        for j, (idx, name, one) in enumerate(((1, pre, 1.0), (2, post, 0.0), (4, pre2, 1.0), (5, post2, 0.0))):
            for w in range(2):
                m = M[:, 8 * idx:8 * idx + 8, w]
                if name is None:
                    tc = self.dve.copy(CO[:, j, w, :], m, after=[t]) if one == 0.0 else None
                else:
                    tc = self.dve.stt(CO[:, j, w, :], m, one, self.v(name, 8 * l, 8), ALU.add, ALU.mult, after=[t])
        self.t_cos[par % 2] = tc

    def rstd(self, out, ps_view, n, after, eps=EPS):
        t = self.act.act(out, ps_view, ACT.Ln, scale=1.0 / n, bias=self.epsc[0:out.shape[0], 0:1], after=after)
        return self.act.act(out, out, ACT.Exp, scale=-0.5, after=[t]), t

    def norm_mod(self, n0, j, shift, after=()):
        n = T - n0
        i, ps, rd = self.bank(6, 7)
        for t in range(KT):
            ta = self.act.act(self.H[:, t, n0:T], self.X[:, t, n0:T], ACT.Square, after=after)
            tp = self.pe.mm(ps[:, 0:n], self.c("ones"), self.H[:, t, n0:T], t == 0, t == KT - 1,
                            after=[ta] + rd, mark=(t == KT - 1))
        te, tl = self.rstd(self.RS[:, 0:n], ps[:, 0:n], D, [tp])
        self.drained[i] = [tl]
        self.t_h = [None] * KT
        for t in range(KT):
            tv = self.dve.mul(self.H[:, t, n0:T], self.X[:, t, n0:T], self.RS[:, 0:n], after=[te, tp])
            for w, a, b in ((1, 0, TC), (0, TC, T)):
                if b <= n0:
                    continue
                h = self.H[:, t, a:b]
                sc, sh = self.CO[:, j, w, t:t + 1], self.M[:, 8 * shift + t, w:w + 1]
                if t % 2:
                    tt = self.act.act(h, h, ACT.Identity, scale=sc, bias=sh, after=[tv, self.t_co])
                else:
                    tt = self.dve.ts(h, h, sc, ALU.mult, sh, ALU.add, after=[tv, self.t_co])
            self.t_h[t] = tt

    def resid(self, Y, n0, j, norm, after, sq=None):
        n = T - n0
        sq = self.H if sq is None else sq
        if norm:
            i, ps, rd = self.bank(6, 7)
            for t in range(KT):
                ta = self.act.act(sq[:, t, 0:n], Y[:, t, :], ACT.Square, after=[after[t]])
                tp = self.pe.mm(ps[:, 0:n], self.c("ones"), sq[:, t, 0:n], t == 0, t == KT - 1,
                                after=[ta] + rd, mark=(t == KT - 1))
            te, tl = self.rstd(self.RS[:, 0:n], ps[:, 0:n], D, [tp])
            self.drained[i] = [tl]
        for t in range(KT):
            tv = after[t]
            if norm:
                tv = self.dve.mul(Y[:, t, :], Y[:, t, :], self.RS[:, 0:n], after=[te, after[t]])
            for w, a, b in ((1, 0, TC), (0, TC, T)):
                if b <= n0:
                    continue
                self.dve.stt(self.X[:, t, a:b], Y[:, t, a - n0:b - n0], self.CO[:, j, w, t:t + 1],
                             self.X[:, t, a:b], ALU.mult, ALU.add, after=[tv, self.t_co])

    def fm(self, w, m0, m, n0, out, after, lo=0, hi=4, po=0, eng=None, K=KT, rhs=None, **kw):
        n = T - n0
        i, ps, rd = self.bank(lo, hi)
        for k in range(K):
            r = self.H[:, k, n0:T] if rhs is None else rhs(k)
            h = [self.t_h[k]] if rhs is None else []
            tm = self.pe.mm(ps[po:po + m, 0:n], w[:, k, m0:m0 + m], r, k == 0, k == K - 1,
                            after=list(after) + rd + h, mark=(k == K - 1))
        self.drained[i] = [out(ps[po:po + m, 0:n], tm)]
        return tm

    def tm(self, w, c0, c1, jt, out, after, lo=0, hi=4):
        i, ps, rd = self.bank(lo, hi)
        for k in range(KT):
            tk = self.pe.mm(ps[:, 0:c1 - c0], self.H[:, k, 128 * jt:128 * jt + 128], w[:, k, c0:c1],
                            k == 0, k == KT - 1, after=list(after) + rd + [self.t_h[k]], mark=(k == KT - 1))
        self.drained[i] = [out(ps[:, 0:c1 - c0], tk)]
        return tk

    def enter_parts(self):
        self.ring.held |= {2, 3}
        self.wp_free = [list(self.phase) for _ in range(4)]

    def leave_parts(self):
        for i in (2, 3):
            self.ring.free(i, *self.phase)

    def parts(self, x, hi, lo, after):
        t = self.act.copy(hi, x, after=after)
        return self.dve.sub(lo, x, hi.bitcast(F32), after=[t])

    def pieces(self, loads):
        def queue():
            x = 0
            for n, load in loads:
                s, tok = self.ring.load(*load)
                for c in range(0, n, 1024):
                    p = (self.WP[:, x, 0, :], self.WP[:, x, 1, :])
                    t = self.parts(self.slots[s][:, c:c + 1024], *p, [tok] + self.wp_free[x])
                    if c + 1024 >= n:
                        self.ring.free(s, t)
                    yield x, p, t
                    x = (x + 1) % 4

        q = queue()
        ahead = list(itertools.islice(q, 3))
        while ahead:
            ahead += itertools.islice(q, 1)
            yield ahead.pop(0)

    def h_parts(self, n0):
        n = T - n0
        self.t_h = [self.parts(self.H[:, k, n0:T], self.HP[:, 0, k, 0:n], self.HP[:, 1, k, 0:n], [self.t_h[k]])
                    for k in range(KT)]
        return lambda k: (self.HP[:, 0, k, 0:n], self.HP[:, 1, k, 0:n])

    def down_loads(self, W, k0, k1):
        def load(a, kn):
            view = lambda s: s[:, 0:kn * D].rearrange("p (k n) -> p k n", k=kn)
            return kn * D, [(view, W[128 * a:128 * (a + kn), :].rearrange("(k p) n -> p k n", p=128))]

        return [load(a, min(4, k1 - a)) for a in range(k0, k1, 4)]

    def down(self, stream, n, kt, k_of, bufs, after, Y, add=False, read=()):
        free = [list(read) for _ in bufs]
        todo = {}

        def part(k):
            if k < kt:
                x = k % len(bufs)
                todo[k] = self.parts(k_of(k), *bufs[x], list(after[k]) + free[x])

        for k in range(3):
            part(k)
        for k in range(kt):
            b, w, tw = next(stream)
            part(k + 3)
            for t in range(KT):
                tm = self.pe.mm3(self.ps[t][:, 0:n], [z[:, 128 * t:128 * t + 128] for z in w], bufs[k % len(bufs)],
                                 k == 0, k == kt - 1, after=[tw, todo[k]] + (self.drained[t] if k == 0 else []),
                                 mark=(k == kt - 1 or t == KT - 1))
                if k == kt - 1:
                    y, ps = Y[:, t, :], self.ps[t][:, 0:n]
                    if add:
                        self.drained[t] = [self.dve.add(y, ps, y, after=[tm])]
                    else:
                        self.drained[t] = [(self.act if t % 2 else self.dve).copy(y, ps, after=[tm])]
            free[k % len(bufs)] = self.wp_free[b] = [tm]
        return [self.drained[t][0] for t in range(KT)]

    def xp(self, n):
        return [(self.XP[:, i, 0, 0:n], self.XP[:, i, 1, 0:n]) for i in range(4)]

    def out_proj(self, W, MIX, n0, norm, j=1):
        n = T - n0
        self.enter_parts()
        Y = self.room2(KT, n)
        bufs = [(self.HP[:, 0, k, 0:n], self.HP[:, 1, k, 0:n]) for k in range(KT)]
        ys = self.down(self.pieces(self.down_loads(W, 0, KT)), n, KT, lambda k: MIX[:, k, :], bufs, [[]] * KT, Y)
        self.fence_keep()
        self.leave_parts()
        self.resid(Y, n0, j, norm, ys)

    def four(self, stream, x, n, cols):
        bs = [self.bank() for _ in range(4)]
        for k in range(KT):
            if k % 2 == 0:
                b, w, tw = next(stream)
            for a, (i, ps, rd) in enumerate(bs):
                c = cols(a, k) % 1024
                tm = self.pe.mm3(ps[:, 0:n], [z[:, c:c + 128] for z in w], x(k), k == 0, k == KT - 1,
                                 after=[tw, self.t_h[k]] + (rd if k == 0 else []), mark=(k == KT - 1 or a == 3))
                if k == KT - 1:
                    bs[a] = (i, ps[:, 0:n], tm)
            self.wp_free[b] = [tm]
        return bs

    def block_load(self, W, c0):
        view = lambda s: s[:, :].rearrange("p (k n) -> p k n", k=KT)
        return 4096, [(view, W[:, c0:c0 + 512].rearrange("(k p) n -> p k n", p=128))]

    def tokens4(self, stream, out):
        bs = [self.bank() for _ in range(4)]
        for k in range(KT):
            if k % 2 == 0:
                b, w, tw = next(stream)
            c = 512 * (k % 2)
            for j, (i, ps, rd) in enumerate(bs):
                tm = self.pe.mm3(ps[:, :], [self.HP[:, a, k, 128 * j:128 * j + 128] for a in range(2)],
                                 [z[:, c:c + 512] for z in w], k == 0, k == KT - 1,
                                 after=[tw, self.t_h[k]] + (rd if k == 0 else []), mark=(k == KT - 1 or j == 3))
                if k == KT - 1:
                    bs[j] = (i, ps[:, :], tm)
            self.wp_free[b] = [tm]
        for j, (i, ps, tm) in enumerate(bs):
            self.drained[i] = [out(j, ps, tm)]

    def features4(self, stream, x, out):
        for m, (i, ps, t) in enumerate(self.four(stream, x, T, lambda a, k: 512 * k + 128 * a)):
            self.drained[i] = [out(m, ps, t)]

    def ffn_swiglu(self, l, n0):
        n = T - n0
        io = self.io
        self.fence()
        self.enter_parts()
        self.norm_mod(n0, 2, 3)
        x_ = self.h_parts(n0)
        cut = (0, 12, 22) if n0 == 0 else (0, 22)
        G = self.room2(max(cut[1], KT), n)
        tmp = [self.room2(n) for _ in range(2)]
        Y = self.H[:, :, n0:T]

        def up_load(g):
            cols = slice(256 * g, 256 * g + 256)
            view = lambda s: s[:, :].rearrange("p (k u n) -> p u k n", u=2, k=KT)
            return 4096, [(lambda s, a=a: view(s)[:, a], io[name][l][:, cols].rearrange("(k p) n -> p k n", p=128))
                          for a, name in enumerate(("ffn_w_gate", "ffn_w_up"))]

        loads = []
        for a, b in zip(cut, cut[1:]):
            loads += [up_load(g) for g in range(a // 2, b // 2)] + self.down_loads(io["ffn_w_down"][l], a, b)
        stream = self.pieces(loads)
        free, read = [[], []], []
        for a, b in zip(cut, cut[1:]):
            done = []
            for g in range(a // 2, b // 2):
                bs = self.four(stream, x_, n, lambda t, k: 512 * k + 256 * (t % 2) + 128 * (t // 2))
                for m in range(2):
                    (i, pg, tg), (j, pu, tu) = bs[2 * m], bs[2 * m + 1]
                    ta = self.act.act(tmp[m], pg, ACT.Silu, after=[tg] + free[m])
                    td = self.dve.mul(G[:, 2 * g + m - a, :], pu, tmp[m], after=[tu, ta])
                    self.drained[i], self.drained[j], free[m] = [ta], [td], [td]
                    done.append([td])
            ys = self.down(stream, n, b - a, lambda k: G[:, k, :], self.xp(n), done, Y, a > 0, read)
            read = [self.pe.last()]
        self.fence_keep()
        self.leave_parts()
        self.resid(Y, n0, 3, True, ys, G)

    def fence_keep(self):
        at = self.at
        self.fence()
        self.at = at

    def ffn_sq(self, l, n0):
        n = T - n0
        io = self.io
        self.fence()
        self.enter_parts()
        self.norm_mod(n0, 2, 3)
        x_ = self.h_parts(n0)
        cut = (0, 16, 32) if n0 == 0 else (0, 32)
        G = self.room2(cut[1], n)
        Y = self.H[:, :, n0:T]

        def up_load(g):
            view = lambda s: s[:, :].rearrange("p (k n) -> p k n", k=KT)
            return 4096, [(view, io["mlp_w1_2"][l][:, 512 * g:512 * g + 512].rearrange("(k p) n -> p k n", p=128))]

        loads = []
        for a, b in zip(cut, cut[1:]):
            loads += [up_load(g) for g in range(a // 4, b // 4)] + self.down_loads(io["mlp_w2_2"][l], a, b)
        stream = self.pieces(loads)
        read = []
        for a, b in zip(cut, cut[1:]):
            done = []
            for g in range(a // 4, b // 4):
                for m, (i, ps, t) in enumerate(self.four(stream, x_, n, lambda t, k: 512 * k + 128 * t)):
                    x = G[:, 4 * g + m - a, :]
                    t = self.act.act(x, ps, ACT.Relu, after=[t])
                    self.drained[i] = [t]
                    done.append([self.pool.mul(x, x, x, after=[t])])
            ys = self.down(stream, n, b - a, lambda k: G[:, k, :], self.xp(n), done, Y, a > 0, read)
            read = [self.pe.last()]
        self.fence_keep()
        self.leave_parts()
        self.resid(Y, n0, 3, False, ys)

    def cumsum(self, B, g, after):
        n = B.shape[1] * B.shape[2]
        return self.dve.do(lambda e: e.tensor_tensor_scan(
            B.rearrange("p c x -> p (c x)"), self.c("smask", n), g.rearrange("p c x -> p (c x)"), 0.0,
            ALU.mult, ALU.add), after)

    def levels(self, *args):
        last = []
        for _ in self.levels_steps(*args, last):
            pass
        return last

    def levels_steps(self, q, ks, Bs, c0, nc, scale, heads, bufs, after, lo, hi, last):
        last += [None] * len(heads)
        for h, (pb, sz, P, dg) in enumerate(heads):
            i, ps, rd = self.bank(lo, hi)
            for c in range(nc):
                for d, kk in enumerate(dg):
                    tm = self.pe.mm(ps[:, 128 * c:128 * c + 128], kk[pb:pb + sz, 128 * (c0 + c):128 * (c0 + c) + 128],
                                    q[pb:pb + sz, 128 * c:128 * c + 128], d == 0, d == len(dg) - 1,
                                    after=after + rd, mark=(c == nc - 1 and d == len(dg) - 1))
            eye = self.c("ident").unsqueeze(1).broadcast_to([128, nc, 128])
            S = ps[:, 0:128 * nc].rearrange("p (c x) -> p c x", c=nc)
            last[h] = self.dve.stt(P, S, 2.0 if len(dg) == 1 else 1.0, eye, ALU.mult, ALU.mult,
                                   after=[tm] + self.free_p[h])
            self.drained[i] = [last[h]]
        Z = [(s, li, L) for s in range(2) for li, L in enumerate(LEVELS)]
        E_, UV, prod = {}, {}, {}

        def split(n):
            s, li, L = Z[n]
            B, sh = Bs[s], 1 - s
            u = self.turn.get("lvl", 0)
            self.turn["lvl"] = u + 1
            x = u % len(bufs)
            E = bufs[x][0]
            halves = lambda z: z.rearrange("p c (b h l) -> p c b h l", h=2, l=L)
            Ev = halves(E.rearrange("p (c x) -> p c x", c=nc))
            Bt = halves(B[:, c0:c0 + nc, sh:sh + 128])
            Bm = halves(B[:, c0:c0 + nc, 0:128])[:, :, :, 1, 0:1].broadcast_to([E.shape[0], nc, 64 // L, L])
            fr = self.e_free[x]
            t1 = self.dve.sub(Ev[:, :, :, 0, :], Bm, Bt[:, :, :, 0, :], after=after + fr)
            t2 = self.dve.sub(Ev[:, :, :, 1, :], Bt[:, :, :, 1, :], Bm, after=after + fr)
            E_[n] = x, self.act.act(E, E, ACT.Exp, scale=scale, after=[t1, t2])

        def product(n):
            s, li, L = Z[n]
            x, te = E_[n]
            E, U, V = bufs[x]
            fr = self.uv_free[x]
            tu = self.pool.mul(U, ks[s][:, 128 * c0:128 * (c0 + nc)], E, after=[te] + after + fr)
            tv = self.dve.mul(V, q, E, after=[te] + after + fr)
            self.e_free[x] = [tu, tv]
            prod[n] = []
            for h, (pb, sz, P, dg) in enumerate(heads):
                i, ps, rd = self.bank(lo, hi)
                for c in range(nc):
                    cs = slice(128 * c, 128 * c + 128)
                    tm = self.pe.mm(ps[:, cs], U[pb:pb + sz, cs], V[pb:pb + sz, cs], True, True,
                                    after=[tu, tv] + rd, mark=(c == nc - 1))
                prod[n].append((i, ps, tm))
            self.uv_free[x] = [tm]

        def keep(n):
            s, li, L = Z[n]
            for h, (pb, sz, P, dg) in enumerate(heads):
                i, ps, tm = prod[n][h]
                mk = self.msk[:, 7 * s + li:7 * s + li + 1, :].broadcast_to([128, nc, 128])
                S = ps[:, 0:128 * nc].rearrange("p (c x) -> p c x", c=nc)
                last[h] = self.dve.do(lambda e, P=P, mk=mk, S=S: e.copy_predicated(P, mk, S), [tm, last[h]])
                self.drained[i] = [last[h]]

        late = (hi - lo) >= 2 * len(heads)
        for n in range(len(Z) + 2):
            if n < len(Z):
                split(n)
            if not late and 2 <= n:
                keep(n - 2)
            if 1 <= n <= len(Z):
                product(n - 1)
            if late and 2 <= n:
                keep(n - 2)
            yield

    def across(self, ks, Bs, scale, W, after):
        out = []
        for s in range(2):
            B, k = Bs[s], ks[s]
            w, x, e = W[s], W[2 + s], W[4 + s]
            w3 = w.rearrange("p (c x) -> p c x", c=4)
            P = w.shape[0]
            if s == 0:
                t = self.dve.sub(w3, B[:, :, 128:129].broadcast_to([P, 4, 128]), B[:, :, 1:129], after=after + self.w_free)
                t = self.act.act(w, w, ACT.Exp, scale=scale, after=[t])
            else:
                t = self.act.act(w3, B[:, :, 0:128], ACT.Exp, scale=scale, after=after + self.w_free)
            t = self.pool.mul(w, w, k, after=[t] + after)
            ta = self.act.act(e, B[:, :, 128], ACT.Exp, scale=scale, after=after + self.w_free)
            T_ = lambda c: e[:, c:c + 1]
            K_ = lambda c: w[:, 128 * c:128 * c + 128]
            o = [t, ta] + self.w_free
            if s == 0:
                seq = ((0, K_(0), T_(1)), (1, K_(1), T_(2)), (2, x[:, 0, :], T_(2)))
            else:
                seq = ((0, K_(1), T_(0)), (1, K_(0), T_(3)), (2, x[:, 0, :], T_(3)))
            for j, a, b in seq:
                o.append(self.dve.ts(x[:, j, :], a, b, ALU.mult, after=o))
            out.append([t] + o[-3:])
        return out

    def queries(self, q, Bs, c0, nc, scale, Q, after):
        out = []
        for s in range(2):
            B = Bs[s][:, c0:c0 + nc]
            e = Q[s]
            e3 = e.rearrange("p (c x) -> p c x", c=nc)
            P = e.shape[0]
            if s == 0:
                t = self.act.act(e3, B[:, :, 1:129], ACT.Exp, scale=scale, after=after + self.w_free)
            else:
                t = self.dve.sub(e3, B[:, :, 128:129].broadcast_to([P, nc, 128]), B[:, :, 0:128], after=after + self.w_free)
                t = self.act.act(e, e, ACT.Exp, scale=scale, after=[t])
            out.append(self.dve.mul(e, e, q, after=[t] + after))
        return out

    def cross_scores(self, pb, sz, W, Q, q0, dst, after, lo, hi, chunks=(0, 1, 2, 3)):
        K = lambda s, j: W[s][pb:pb + sz, 128 * j:128 * j + 128]
        X = lambda s, j: W[2 + s][pb:pb + sz, j, :]
        pairs = {(0, 1): [(0, K(0, 0))], (1, 0): [(1, K(1, 1))], (2, 3): [(0, K(0, 2))], (3, 2): [(1, K(1, 3))],
                 (0, 2): [(0, X(0, 0)), (1, X(1, 1))], (1, 2): [(0, K(0, 1)), (1, X(1, 2))],
                 (0, 3): [(0, X(0, 2)), (1, K(1, 0))], (1, 3): [(0, X(0, 1)), (1, X(1, 0))]}
        todo = [p for p in pairs if p[1] in chunks]
        out = []
        for a in range(0, len(todo), 4):
            i, ps, rd = self.bank(lo, hi)
            part = todo[a:a + 4]
            for n, (J, I) in enumerate(part):
                for m, (s, k) in enumerate(pairs[J, I]):
                    tm = self.pe.mm(ps[:, 128 * n:128 * n + 128], k, Q[s][pb:pb + sz, 128 * (I - q0):128 * (I - q0) + 128],
                                    m == 0, m == len(pairs[J, I]) - 1, after=after + rd,
                                    mark=(n == len(part) - 1 and m == len(pairs[J, I]) - 1))
            for n, (J, I) in enumerate(part):
                out.append(self.act.copy(dst(J, I), ps[:, 128 * n:128 * n + 128], after=[tm] + self.free_cross))
            self.drained[i] = [out[-1]]
        return out

    def readout(self, o, og, gain, dst, n, after, tmp, lo, hi, dv=128, mat="ones"):
        r, sq = tmp
        ta = self.act.act(sq, o, ACT.Square, after=after)
        i, ps, rd = self.bank(lo, hi)
        tp = self.pe.mm(ps[:, 0:n], self.c(mat), sq, True, True, after=[ta] + rd, mark=True)
        te, tl = self.rstd(r, ps[:, 0:n], dv, [tp] + after)
        self.drained[i] = [tl]
        t = self.dve.mul(dst, o, r, after=[te, ta] + after)
        t2 = self.dve.stt(dst, dst, gain, og, ALU.mult, ALU.mult, after=[t] + after)
        return t, t2

    def rms_heads(self, x, mat, K, n, dh, gain, after, tmp, lo, hi):
        r, sq = tmp
        ta = self.act.act(sq[0:K], x, ACT.Square, after=after)
        i, ps, rd = self.bank(lo, hi)
        tp = self.pe.mm(ps[0:K, 0:n], self.c(mat, K, 0, K), sq[0:K], True, True, after=[ta] + rd, mark=True)
        te, tl = self.rstd(r[0:K], ps[0:K, 0:n], dh, [tp] + after)
        self.drained[i] = [tl]
        t = self.dve.stt(x, x, gain, r[0:K], ALU.mult, ALU.mult, after=[te] + after)
        return t

    def rope(self, x, K, mat, cs, sn, after, tmp, lo, hi):
        i, ps, rd = self.bank(lo, hi)
        tp = self.pe.mm(ps[0:K, 0:TC], self.c(mat, K, 0, K), x, True, True, after=after + rd, mark=True)
        t1 = self.dve.mul(tmp[0:K], ps[0:K, 0:TC], self.c(sn, None, 0, K), after=[tp] + after)
        self.drained[i] = [t1]
        t2 = self.dve.mul(x, x, self.c(cs, None, 0, K), after=[tp])
        return self.dve.add(x, x, tmp[0:K], after=[t1, t2])

    def attend_steps(self, units, scale, after, st, lo):
        S = {}
        fp, fpt = [[] for _ in st["P"]], [[] for _ in st["PT"]]

        def scores(u):
            q, k, vv, dst, nk, po = units[u]
            i, ps, rd = self.bank(lo, lo + 2)
            S[u] = i, ps, self.pe.mm(ps[:, 0:nk], q, k, True, True, after=after + rd, mark=True)

        def exps(u):
            q, k, vv, dst, nk, po = units[u]
            i, ps, tm = S[u]
            n = u % len(st["P"])
            P, m, r = st["P"][n], st["m"][:, u:u + 1], st["r"][:, 2 * u:2 * u + 2]
            t1 = self.dve.do(lambda e: e.reduce_max(m, ps[:, 0:nk], AX.X), [tm])
            t2 = self.dve.ts(m, m, -scale, ALU.mult, after=[t1])
            t3 = self.act.act(P[:, 0:nk], ps[:, 0:nk], ACT.Exp, scale=scale, bias=m, accum=r[:, 0:1],
                              after=[t2] + fp[n])
            self.drained[i] = [t3]
            S[u] = t3

        def turn(u):
            q, k, vv, dst, nk, po = units[u]
            n = u % len(st["P"])
            P, r = st["P"][n], st["r"][:, 2 * u:2 * u + 2]
            t4 = self.dve.do(lambda e: e.reciprocal(r[:, 1:2], r[:, 0:1]), [S[u]])
            t5 = self.dve.ts(P[:, 0:nk], P[:, 0:nk], r[:, 1:2], ALU.mult, after=[t4, S[u]])
            i, ps, rd = self.bank(lo + 2, lo + 3)
            for j in range(nk // 128):
                tm = self.pe.tr(ps[:, 128 * j:128 * j + 128], P[:, 128 * j:128 * j + 128], self.c("ident"),
                                after=[t5] + rd, mark=(j == nk // 128 - 1))
            fp[n] = [tm]
            x = u % len(st["PT"])
            S[u] = self.act.copy(st["PT"][x][:, 0:nk], ps[:, 0:nk], after=[tm] + fpt[x])
            self.drained[i] = [S[u]]

        def values(u):
            q, k, vv, dst, nk, po = units[u]
            x = u % len(st["PT"])
            i, ps, rd = self.bank(lo + 2, lo + 3)
            for j in range(nk // 128):
                tm = self.pe.mm(ps[po:po + 64, 0:128], vv(j), st["PT"][x][:, 128 * j:128 * j + 128], j == 0,
                                j == nk // 128 - 1, after=[S[u]] + rd + after, mark=(j == nk // 128 - 1))
            fpt[x] = [tm]
            st["out"] = self.act.copy(dst, ps[po:po + 64, 0:128], after=[tm])
            self.drained[i] = [st["out"]]

        for t in range(len(units) + 3):
            if t < len(units):
                scores(t)
            if 1 <= t <= len(units):
                exps(t - 1)
            if 3 <= t:
                values(t - 3)
            if 2 <= t <= len(units) + 1:
                turn(t - 2)
            yield

    def att_state(self, n, room=None):
        P = [self.alloc(T) for _ in range(4)] if room is None else [room[:, T * i:T * i + T] for i in range(4)]
        return {"P": P[0:2], "PT": P[2:4], "m": self.alloc(n), "r": self.alloc(2 * n)}

    def even(self):
        io = self.io
        W = io["even_w_in"][0]
        self.fence()
        self.enter_parts()
        self.at = 8192
        gw = self.alloc(2 * 256)
        t_gw = self.load(gw[0:32], io["gla_gw"])
        self.norm_mod(0, 0, 0)
        x_ = self.h_parts(0)
        q, k, og = self.alloc(2, T), self.alloc(2, T), self.alloc(4, T)
        z, aq, kk = self.alloc(T), self.alloc(4, T), self.alloc(2, T)
        vg, va = self.alloc(4, T), self.alloc(4, 128)
        cp = lambda dst, sc=None: (lambda ps, t: self.act.act(dst, ps, ACT.Copy, scale=sc or 1.0, after=[t]))
        stream = self.pieces([self.block_load(W, c0) for c0 in (0, 512, 1568, 1024)])
        self.features4(stream, x_, lambda m, ps, t: cp(q[:, m, :], 0.125)(ps, t) if m < 2 else cp(k[:, m - 2, :])(ps, t))
        self.tokens4(stream, lambda j, ps, t: cp(vg[:, j, :])(ps, t))
        self.features4(stream, x_, lambda m, ps, t: cp(aq[:, m, :])(ps, t))
        self.features4(stream, x_, lambda m, ps, t: self.act.act(og[:, m, :], ps, ACT.Silu, after=[t]))
        n = 32 + 256
        view = lambda s: s[:, 0:KT * n].rearrange("p (k n) -> p k n", k=KT)
        s, tok = self.ring.load(
            (lambda s: view(s)[:, :, 0:32], W[:, 1536:1568].rearrange("(k p) n -> p k n", p=128)),
            (lambda s: view(s)[:, :, 32:288], W[:, 2080:2336].rearrange("(k p) n -> p k n", p=128)))
        w = view(self.slots[s])
        self.fm(w, 0, 32, 0, cp(z[0:32, :]), [tok])
        t_z = (self.act.sem, self.act.n)
        for g in range(2):
            for half in range(2):
                self.fm(w, 32 + 64 * g, 64, 0, cp(kk[64 * half:64 * half + 64, g, :]), [tok], po=64 * half)
        for j in range(4):
            tl = self.tm(w, 160, 288, j, lambda ps, t, j=j: self.act.copy(va[:, j, :], ps, after=[t]), [tok])
        self.ring.free(s, tl)
        self.fence_keep()
        self.leave_parts()
        top = self.at
        self.at = 0
        MIX = self.H
        s_p, fr_p = self.ring.scratch()
        s_a, fr_a = self.ring.scratch()
        Bs = [[None, None], [None, None]]
        Bf = self.alloc(4, 4 * 129)
        gp, Lt, aL = self.alloc(4 * 129), self.alloc(T), self.alloc(T)
        SC = 1.0 / 16.0
        bufs = [(self.alloc(T), self.alloc(T), self.alloc(T)) for _ in range(2)]
        assert self.at <= 8192
        self.at = top
        WW = [self.alloc(T), self.alloc(T), self.alloc(3, 128), self.alloc(3, 128), self.alloc(4), self.alloc(4)]
        QQ = [self.alloc(T), self.alloc(T)]
        room = self.slots[s_a]
        st = self.att_state(32, room[:, 0:4 * T])
        PP = [self.slots[s_p][:, 2048 * h:2048 * h + 2048].rearrange("p (j x) -> p j x", j=4) for h in range(2)]

        def linear():
            gp3 = gp.rearrange("p (c x) -> p c x", x=129)
            tB = [self.dve.zero(gp)]
            for m in range(2):
                for d in range(2):
                    i, ps, rd = self.bank(0, 3)
                    tm = self.pe.mm(ps[:, :], gw[0:32, 256 * d + 128 * m:256 * d + 128 * m + 128], z[0:32, :], True, True,
                                    after=[t_gw, t_z] + rd, mark=True)
                    t = self.act.act(Lt, ps[:, :], ACT.Identity, bias=self.v("gla_b", 2 * d + m), after=[tm] + tB)
                    self.drained[i] = [t]
                    ta = self.act.act(aL, Lt, ACT.Abs, after=[t])
                    ta = self.act.act(aL, aL, ACT.Exp, scale=-1.0, after=[ta])
                    ta = self.act.act(aL, aL, ACT.Ln, bias=self.v("one"), after=[ta])
                    L3, a3 = Lt.rearrange("p (c x) -> p c x", c=4), aL.rearrange("p (c x) -> p c x", c=4)
                    t = self.dve.stt(gp3[:, :, 1:129], L3, 0.0, a3, ALU.min, ALU.subtract, after=[t, ta] + tB)
                    B = Bf[:, 2 * d + m, :].rearrange("p (c x) -> p c x", x=129)
                    tB = [self.cumsum(B, gp3, [t])]
                    Bs[m][d] = B
                    yield
            self.w_free, self.e_free, self.uv_free = [], [[], []], [[], []]
            self.free_p, self.free_cross = [fr_p, fr_p], fr_p
            to = []
            for m in range(2):
                ks, qm = [k[:, m, :]] * 2, q[:, m, :]
                heads = [(64 * h, 64, self.diag_view(s_p, 2048 * h), [k[:, m, :]]) for h in range(2)]
                last = []
                tw = self.across(ks, Bs[m], SC, WW, tB)
                yield
                tq = self.queries(qm, Bs[m], 0, 4, SC, QQ, tB)
                yield from self.levels_steps(qm, ks, Bs[m], 0, 4, SC, heads, bufs, tB, 0, 3, last)
                tx = []
                for h in range(2):
                    tx.append(self.cross_scores(64 * h, 64, WW, QQ, 0, lambda J, I, h=h: PP[h][:, J, 128 * I:128 * I + 128],
                                                tw[0] + tw[1] + tq, 3, 4))
                    yield
                for h in range(2):
                    hd = 2 * m + h
                    i, ps, rd = self.bank(3, 4)
                    for J in range(4):
                        a = 0 if J < 2 else TC
                        tm = self.pe.mm(ps[:, a:T], vg[:, J, 128 * hd:128 * hd + 128], PP[h][:, J, a:T], J == 0, J == 3,
                                        after=[last[h]] + tx[h] + rd, mark=(J == 3))
                    t1, t2 = self.readout(ps[:, :], og[:, hd, :], self.v("gla_n"), MIX[:, hd, :], T, [tm] + to + tB,
                                          (Lt, aL), 0, 3)
                    self.drained[i] = [t1]
                    to = [t1]
                    self.free_p[h] = [tm]
                    yield
                self.free_cross = self.w_free = [tm]
            self.ring.free(s_p, tm)

        def softmax():
            tmp = (room[:, 2048:2560], room[:, 2560:3072])
            rt = room[:, 3072:3072 + TC]
            prev = fr_a
            for x, gain in ((kk[:, 0, :], "ak_n"), (kk[:, 1, :], "ak_n")) + tuple((aq[:, m, :], "aq_n") for m in range(4)):
                t = self.rms_heads(x, "bd", 128, T, 64, self.v(gain), prev, tmp, 4, 6)
                t = self.rope(x[:, TC:T], 128, "rotE", "cosE", "sinE", [t] + prev, rt, 4, 6)
                prev = [t]
                yield
            units = []
            for h in range(8):
                m, pb, g = h // 2, 64 * (h % 2), h // 4
                for c in range(4):
                    nk = TC if c < 2 else T
                    cs = slice(128 * c, 128 * c + 128)
                    units.append((aq[pb:pb + 64, m, cs], kk[pb:pb + 64, g, 0:nk],
                                  lambda j, g=g: va[:, j, 64 * g:64 * g + 64], MIX[pb:pb + 64, 4 + m, cs], nk, pb))
            yield from self.attend_steps(units, 0.125, prev, st, 4)
            self.ring.free(s_a, self.pe.last(), self.act.last(), self.dve.last())

        self.together(linear(), softmax(), self.next_mods())
        self.fence()
        if self.stop == "evenmix":
            return
        self.out_proj(io["even_w_out"][0], MIX, 0, True)

    def diag_view(self, si, off):
        v = self.slots[si][:, off:off + 640].unsqueeze(1).broadcast_to([128, 4, 640])
        v = v[:, :, 0:128]
        return bass.AP(v.tensor, v.offset, [list(v.ap[0]), [640, 4], [1, 128]])

    def finish(self):
        self.fence()
        tokens, self.phase = self.phase, None
        self.sp.dma(self.io["outX"], (self.H if 'mix' in self.stop else self.X)[:, :, :] if self.stop else self.X[:, :, TC:T], self.s_out, tokens)
        self.sp.items.append([[(self.s_out, 16)], None, None, 0])
        with self.nc.Block() as block:
            @block.sync
            def _(e):
                self.sp.play(e)

            @block.gpsimd
            def _(e):
                self.pool.play(e)

            @block.scalar
            def _(e):
                self.act.play(e)

            @block.tensor
            def _(e):
                self.pe.play(e)

            @block.vector
            def _(e):
                self.dve.play(e)

    def together(self, *gens):
        gens = list(gens)
        while gens:
            for g in list(gens):
                if next(g, self) is self:
                    gens.remove(g)

    def odd(self):
        io = self.io
        W = io["odd_w_in"][0]
        self.fence()
        self.norm_mod(0, 0, 0)
        V = self.alloc(4, D)
        for g in range(2):
            s, w, tok = self.wslot(W, 3072 + 512 * g, 3584 + 512 * g)
            for j in range(4):
                dst = V[:, j, 512 * g:512 * g + 512]
                tl = self.tm(w, 0, 512, j, lambda ps, t, dst=dst: self.act.copy(dst, ps, after=[t]), [tok], 0, 2)
            self.ring.free(s, tl)
        e, p = self.alloc(4, 8), self.alloc(4, 8)
        mx = self.alloc(2, 8)
        lb = self.v("lb", 0, 32).rearrange("p (a h) -> p a h", h=8)
        l4 = lb.rearrange("p (d l) h -> p d l h", l=2)
        e4, p4 = (x.rearrange("p (d l) h -> p d l h", l=2) for x in (e, p))
        t = self.dve.tt(mx, l4[:, :, 0, :], l4[:, :, 1, :], ALU.max)
        for l in range(2):
            t = self.dve.sub(e4[:, :, l, :], l4[:, :, l, :], mx, after=[t])
        t = self.act.act(e, e, ACT.Exp, after=[t])
        t = self.dve.add(mx, e4[:, :, 0, :], e4[:, :, 1, :], after=[t])
        t = self.dve.do(lambda g: g.reciprocal(mx, mx), [t])
        for l in range(2):
            t = self.dve.mul(p4[:, :, l, :], e4[:, :, l, :], mx, after=[t])
        t = self.dve.ts(p4[:, :, 1, :], p4[:, :, 1, :], 2.0 ** -60, ALU.max, after=[t])
        t_lb = t
        sets = []
        for _ in range(2):
            sets.append(dict(q=self.alloc(TC), og=self.alloc(TC), k=[self.alloc(T), self.alloc(T)],
                             B=[self.alloc(4, 129), self.alloc(4, 129)]))
        sg, sf = self.alloc(T), [self.alloc(T), self.alloc(T)]
        gp = [self.alloc(4, 129) for _ in range(2)]
        tz = [self.dve.zero(g) for g in gp]
        bufs = [(self.alloc(TC), self.alloc(TC), self.alloc(TC)) for _ in range(2)]
        WW = [self.alloc(T), self.alloc(T), self.alloc(3, 128), self.alloc(3, 128), self.alloc(4), self.alloc(4)]
        QQ = [self.alloc(TC), self.alloc(TC)]
        PB = self.alloc(4 * TC)
        PP = PB.rearrange("p (j x) -> p j x", j=4)
        diag = bass.AP(PB.tensor, PB[:, 512:513].offset, [list(PB.ap[0]), [384, 2], [1, 128]])
        tmp = (self.alloc(TC), self.alloc(TC))
        MIX = self.R[:, self.NW - KT * TC:self.NW].rearrange("p (k n) -> p k n", k=KT)
        assert self.at <= self.NW - KT * TC
        self.w_free, self.e_free, self.uv_free = [], [[], []], [[], []]
        self.free_p, self.free_cross = [[]], []
        done, ready, g_free = [[], []], {}, [[], [], []]

        def project(h):
            u = h % 2
            S = sets[u]
            view = lambda s: s[:, :].rearrange("p (a k n) -> p a k n", a=4, k=KT)
            s, tok = self.ring.load(*[
                (lambda s, a=a: view(s)[:, a], W[:, c + 128 * h:c + 128 * h + 128].rearrange("(k p) n -> p k n", p=128))
                for a, c in enumerate((0, 4096, 1024, 2048))])
            w = view(self.slots[s])
            i0, ps0, rd = self.bank(0, 3)
            for a in range(2):
                for k in range(KT):
                    tm0 = self.pe.mm(ps0[:, TC * a:TC * a + TC], w[:, a, k, :], self.H[:, k, TC:T], k == 0, k == KT - 1,
                                     after=[tok, self.t_h[k]] + rd, mark=(k == KT - 1))
                yield
            pf = []
            for d in range(2):
                i, ps, rd = self.bank(0, 3)
                for k in range(KT):
                    tm = self.pe.mm(ps[:, :], w[:, 2 + d, k, :], self.H[:, k, :], k == 0, k == KT - 1,
                                    after=[tok, self.t_h[k]] + rd, mark=(k == KT - 1))
                    if k == 3:
                        yield
                pf.append((i, ps, tm))
                yield
            self.ring.free(s, tm)
            for _ in range(4):
                yield
            t = self.act.act(sg, ps0[:, :], ACT.Sigmoid, after=[tm0] + g_free[2])
            t0 = self.dve.mul(S["q"], ps0[:, 0:TC], sg[:, 0:TC], after=[t] + done[u])
            t1 = self.dve.mul(S["og"], ps0[:, TC:T], sg[:, TC:T], after=[t] + done[u])
            self.drained[i0] = [t1]
            g_free[2] = [t1]
            toks = [t0, t1]
            sig = []
            for d, (i, ps, tm) in enumerate(pf):
                a = self.act.act(sf[d], ps[:, :], ACT.Sigmoid, after=[tm] + g_free[d])
                b = self.act.act(S["k"][d], ps[:, :], ACT.Sigmoid, scale=-1.0, after=[tm] + done[u])
                self.drained[i] = [b]
                sig.append((a, b))
            fs = []
            for d, (a, b) in enumerate(sig):
                p1, p0, g = p[:, 2 * d + 1, h:h + 1], p[:, 2 * d, h:h + 1], gp[d]
                fs.append(self.dve.ts(g[:, :, 1:129], sf[d].rearrange("p (c x) -> p c x", c=4), p0, ALU.mult, p1, ALU.add,
                                      after=[a, t_lb] + g_free[d] + tz))
                toks.append(self.dve.ts(S["k"][d], S["k"][d], p0, ALU.mult, after=[b, t_lb]))
            for d in range(2):
                g = gp[d]
                t = self.act.act(g[:, :, 1:129], g[:, :, 1:129], ACT.Ln, after=[fs[d]])
                t = self.cumsum(S["B"][d], g, [t] + done[u])
                g_free[d] = [t]
                toks.append(t)
            ready[h] = toks

        def mix(h):
            u = h % 2
            S, af = sets[u], ready[h]
            tw = self.across(S["k"], S["B"], 1.0, WW, af)
            yield
            tq = self.queries(S["q"], S["B"], 2, 2, 1.0, QQ, af)
            last = []
            yield from self.levels_steps(S["q"], S["k"], S["B"], 2, 2, 1.0, [(0, 128, diag, S["k"])], bufs, af, 3, 5, last)
            tx = self.cross_scores(0, 128, WW, QQ, 2, lambda J, I: PP[:, J, 128 * (I - 2):128 * (I - 2) + 128],
                                   tw[0] + tw[1] + tq, 5, 6, (2, 3))
            yield
            i, ps, rd = self.bank(6, 7)
            for J in range(4):
                tm = self.pe.mm(ps[:, 0:TC], V[:, J, 128 * h:128 * h + 128], PP[:, J, :], J == 0, J == 3,
                                after=[last[0]] + tx + rd, mark=(J == 3))
            t1, t2 = self.readout(ps[:, 0:TC], S["og"], self.v("hg_n"), MIX[:, h, :], TC, [tm] + self.ro_free + af, tmp, 5, 6)
            self.drained[i] = [t1]
            self.ro_free = [t1]
            self.free_p[0] = self.free_cross = self.w_free = [tm]
            done[u] = [t2, t1]
            yield

        self.ro_free = []
        extra = self.next_mods()
        self.together(project(0))
        for h in range(8):
            self.together(mix(h), *([project(h + 1)] if h < 7 else []), itertools.islice(extra, 4))
        self.together(extra)
        self.fence_keep()
        if self.stop == "oddmix":
            self.act.copy(self.H[:, :, TC:T], MIX)
            return
        self.at = 0
        self.out_proj(io["odd_w_out"][0], MIX, TC, True)

    def mla(self):
        io = self.io
        W = io["w_in_2"][0]
        self.fence()
        self.sp.dma(self.X[:, :, 0:TC], io["x2T"], self.s_x, self.phase)
        self.enter_parts()
        self.norm_mod(0, 0, 0, after=[(self.s_x, 32)])
        x_ = self.h_parts(0)
        self.at = 8192
        cp = lambda dst, sc=None: (lambda ps, t: self.act.act(dst, ps, ACT.Copy, scale=sc or 1.0, after=[t]))
        rq, rk, rg, rv = (self.alloc(4, T) for _ in range(4))
        cq, ckv, kr = self.alloc(2, T), self.alloc(T), self.alloc(T)
        stream = self.pieces([self.block_load(W, c0) for c0 in (416, 928, 1440, 1952)])
        self.features4(stream, x_, lambda m, ps, t: cp(rq[:, m, :])(ps, t))
        self.features4(stream, x_, lambda m, ps, t: cp(rk[:, m, :], 0.125)(ps, t))
        self.tokens4(stream, lambda j, ps, t: cp(rv[:, j, :])(ps, t))
        self.features4(stream, x_, lambda m, ps, t: self.act.act(rg[:, m, :], ps, ACT.Silu, after=[t]))
        s, w, tok = self.wslot(W, 0, 416)
        for m in range(2):
            self.fm(w, 128 * m, 128, 0, cp(cq[:, m, :]), [tok])
        self.fm(w, 256, 128, 0, cp(ckv), [tok])
        tl = self.fm(w, 384, 32, 0, cp(kr[64:96, :]), [tok], po=64)
        self.ring.free(s, tl)
        self.fence_keep()
        self.leave_parts()
        top = self.at
        self.at = 0
        vv = self.alloc(4, T)
        MIX = self.H
        tmp = (self.alloc(T), self.alloc(T))
        rt = self.alloc(TC)
        QH, KH = self.alloc(4, T), self.alloc(4, T)
        vu = lambda s: s[:, 0:1536].rearrange("p (k n) -> p k n", k=2)
        vk = lambda s: s[:, 1536:2560]
        s, tok = self.ring.load((vu, io["mla_w_uq_2"][0].rearrange("(k p) n -> p k n", p=128)),
                                (vk, io["mla_w_ukv_2"][0]))
        su = s
        self.ring.held.add(su)
        sr = [self.ring.scratch() for _ in range(2)]
        fr_r = sr[0][1] + sr[1][1]
        assert self.at <= 8192
        self.at = top
        st = self.att_state(32, None)
        wu, wk = vu(self.slots[s]), vk(self.slots[s])

        def latent():
            i, ps, rd = self.bank(4, 6)
            for m in range(2):
                ta = self.act.act(tmp[m], cq[:, m, :], ACT.Square)
                tp = self.pe.mm(ps[:, :], self.c("ones"), tmp[m], m == 0, m == 1, after=[ta] + rd, mark=True)
            te, tl = self.rstd(self.RS[:, :], ps[:, :], 256, [tp])
            self.drained[i] = [tl]
            for m in range(2):
                tn = self.dve.stt(cq[:, m, :], cq[:, m, :], self.v("mq_n", m), self.RS[:, :], ALU.mult, ALU.mult, after=[te, tp])
            tk = self.rms_heads(ckv, "ones", 128, T, 128, self.v("mkv_n"), [tn], tmp, 4, 6)
            yield
            v3 = wk.rearrange("p (h x) -> p h x", x=128)[:, :, 64:128]
            for j in range(4):
                i, ps, rd = self.bank(4, 6)
                tm = self.pe.mm(ps[:, :].rearrange("p (h x) -> p h x", x=64), ckv[:, 128 * j:128 * j + 128], v3, True, True,
                                after=[tk, tok] + rd, mark=True)
                tv = self.act.copy(vv[:, j, :], ps[:, :], after=[tm])
                self.drained[i] = [tv]
            yield
            free = []
            for half in range(2):
                prev = [tv, tk]
                for x in range(4):
                    h = 4 * half + x
                    q, k = QH[0:96, x, :], KH[0:96, x, :]
                    got = []

                    def outq(ps, t):
                        got.append(self.act.copy(q, ps, after=[t] + free))
                        return got[-1]

                    self.fm(wu, 96 * h, 96, 0, outq, [tok, tn], 4, 6, K=2, rhs=lambda kk: cq[:, kk, :])
                    i, ps, rd = self.bank(4, 6)
                    tm = self.pe.mm(ps[0:64, :], wk[:, 128 * h:128 * h + 64], ckv, True, True, after=[tok, tk] + rd, mark=True)
                    t1 = self.act.copy(KH[0:64, x, :], ps[0:64, :], after=[tm] + free)
                    self.drained[i] = [t1]
                    t2 = self.dve.copy(KH[64:96, x, :], kr[64:96, :], after=free)
                    yield
                    for y, gain, dep in ((q, "mqn", [got[0]]), (k, "mkn", [t1, t2])):
                        t = self.rms_heads(y, "ones", 96, T, 96, self.v(gain)[0:96], dep + prev, tmp, 4, 6)
                        t = self.rope(y[:, TC:T], 96, "rotM", "cosM", "sinM", [t], rt, 4, 6)
                        prev = [t]
                        yield
                if half:
                    self.ring.free(su, tm)
                units = []
                for x in range(4):
                    h = 4 * half + x
                    pb = 64 * (h % 2)
                    for c in range(4):
                        nk = TC if c < 2 else T
                        cs = slice(128 * c, 128 * c + 128)
                        units.append((QH[0:96, x, cs], KH[0:96, x, 0:nk], lambda j, h=h: vv[:, j, 64 * h:64 * h + 64],
                                      MIX[pb:pb + 64, h // 2, cs], nk, pb))
                yield from self.attend_steps(units, 96 ** -0.5, prev, st, 4)
                free = [self.pe.last(), st["out"]]

        lg = self.alloc(6, 16)
        rt2 = self.alloc(TC)
        za, zb = self.slots[sr[0][0]], self.slots[sr[1][0]]
        cut = lambda z, n: z[:, T * n:T * n + T]

        def retention():
            raw = self.v("lgf", 0, 16)
            y, w1, eq, num, den, lgm = (lg[:, j, :] for j in range(6))
            t = self.act.act(y, raw, ACT.Exp, scale=math.log(2.0))
            t = self.dve.ts(w1, y, -1.0, ALU.mult, 1.0, ALU.add, after=[t])
            te = self.dve.ts(eq, w1, 1.0, ALU.is_equal, after=[t])
            tl = self.act.act(num, w1, ACT.Ln, after=[t])
            tn = self.dve.add(num, num, eq, after=[te, tl])
            td = self.dve.stt(den, w1, 1.0, eq, ALU.subtract, ALU.add, after=[te])
            td = self.dve.do(lambda g: g.reciprocal(den, den), [td])
            t = self.dve.mul(num, num, den, after=[tn, td])
            t_lg = self.dve.stt(lgm, num, -1.0, y, ALU.mult, ALU.mult, after=[t])
            prev = []
            for x in (rq, rk):
                for m in range(4):
                    t = self.rope(x[:, m, TC:T], 128, "rotR", "cosR", "sinR", prev, rt2, 0, 2)
                    prev = [t]
                    yield
            F, R_, DJ, t1 = cut(za, 0), cut(za, 1), [cut(za, 2), cut(za, 3)], za[:, 2048:2176]
            PJ = zb[:, 0:2048].rearrange("p (j x) -> p j x", j=4)
            o, sq, r = cut(zb, 4), cut(zb, 5), cut(zb, 6)
            dfree, pfree, ofree, ffree = [], fr_r, fr_r, fr_r
            B_ = lambda x, m: x[:, 128 * m:128 * m + 128]
            for m in range(4):
                oi, ops, ord_ = self.bank(3, 4)
                for hh in range(2):
                    h, hb = 2 * m + hh, 64 * hh
                    ta = self.act.act(F, self.c("distF"), ACT.Exp, scale=lgm[:, h:h + 1], after=[t_lg] + ffree)
                    tb = self.act.act(R_, self.c("distR"), ACT.Exp, scale=lgm[:, 8 + h:9 + h], after=[t_lg] + ffree)
                    g = self.pool
                    a = [ta, tb] + dfree
                    u1 = g.mul(t1, B_(F, 0), self.c("mF"), after=a)
                    u2 = g.mul(B_(DJ[0], 0), B_(R_, 0), self.c("mR"), after=a)
                    u3 = g.add(B_(DJ[0], 0), B_(DJ[0], 0), t1, after=[u1, u2])
                    g.copy(B_(DJ[1], 1), B_(DJ[0], 0), after=[u3])
                    g.copy(B_(DJ[0], 1), B_(F, 1))
                    g.copy(B_(DJ[1], 0), B_(R_, 1))
                    g.add(B_(DJ[0], 2), B_(F, 2), B_(R_, 2))
                    g.add(B_(DJ[1], 3), B_(F, 2), B_(R_, 2))
                    g.add(B_(DJ[0], 3), B_(F, 3), B_(R_, 1))
                    td = g.add(B_(DJ[1], 2), B_(F, 1), B_(R_, 3))
                    ffree = [td]
                    yield
                    tp = []
                    for J in range(4):
                        a0 = 0 if J < 2 else TC
                        i, ps, rd = self.bank(0, 2)
                        tm = self.pe.mm(ps[:, a0:T], rk[hb:hb + 64, m, 128 * J:128 * J + 128], rq[hb:hb + 64, m, a0:T], True, True,
                                        after=prev + rd, mark=True)
                        tp.append(self.dve.mul(PJ[:, J, a0:T], ps[:, a0:T], DJ[J % 2][:, 0:T - a0], after=[tm, td] + pfree))
                        self.drained[i] = [tp[-1]]
                    dfree = [tp[-1]]
                    for J in range(4):
                        a0 = 0 if J < 2 else TC
                        tm = self.pe.mm(ops[hb:hb + 64, a0:T], rv[:, J, 64 * h:64 * h + 64], PJ[:, J, a0:T], J == 0, J == 3,
                                        after=[tp[J]] + ord_, mark=(J == 3))
                    pfree = [tm]
                    yield
                to = self.act.copy(o, ops[:, :], after=[tm] + ofree)
                self.drained[oi] = [to]
                i, ps, rd = self.bank(2, 3)
                tp = self.pe.mm(ps[:, :], self.c("bd"), o, True, True, after=[to] + rd, mark=True)
                tm_ = self.dve.stt(o, ps[:, :], -1.0 / 64, o, ALU.mult, ALU.add, after=[tp])
                self.drained[i] = [tm_]
                ta = self.act.act(sq, o, ACT.Square, after=[tm_])
                i, ps, rd = self.bank(2, 3)
                tp = self.pe.mm(ps[:, :], self.c("bd"), sq, True, True, after=[ta] + rd, mark=True)
                te, tl = self.rstd(r, ps[:, :], 64, [tp] + ofree)
                self.drained[i] = [tl]
                t = self.dve.mul(o, o, r, after=[te, ta])
                t = self.dve.mul(MIX[:, 4 + m, :], o, rg[:, m, :], after=[t])
                ofree = [t]
                yield

        self.together(latent(), retention(), self.next_mods())
        for i_, _ in sr:
            self.ring.free(i_, self.pe.last(), self.act.last(), self.dve.last(), self.pool.last())
        self.fence()
        if self.stop == "mlamix":
            return
        self.out_proj(io["w_out_2"][0], MIX, 0, False)

    def cmul(self, o, a, b, t1, t2, after, sign=1):
        g, h = self.dve, self.pool
        x1 = g.mul(o[0], a[0], b[0], after=after)
        x2 = h.mul(t1, a[1], b[1], after=after)
        x3 = g.mul(o[1], a[0], b[1], after=after)
        x4 = h.mul(t2, a[1], b[0], after=after)
        ops = (ALU.subtract, ALU.add) if sign == 1 else (ALU.add, ALU.subtract)
        y1 = g.tt(o[0], o[0], t1, ops[0], after=[x1, x2])
        y2 = g.tt(o[1], o[1], t2, ops[1], after=[x3, x4])
        return y2

    def s5(self):
        io = self.io
        self.fence()
        self.norm_mod(0, 0, 0)
        self.fence()
        T1, T2 = self.alloc(2048), self.alloc(2048)
        P = self.alloc(2, 2048)
        Wb = self.alloc(4, 4, 2, 128)
        CA = self.alloc(2, 5 * 512)
        CA = [CA[:, i, :].rearrange("p (k j f x) -> p k j f x", k=5, j=4, f=4) for i in range(2)]
        V0 = self.alloc(2, 2048)
        aw = self.alloc(2, 5, 32)
        sm = self.RS[:, 0:384].rearrange("p (i q) -> p i q", q=32)
        ldt = self.RS[:, 384:480].rearrange("p (i q) -> p i q", q=32)
        sl = [self.ring.scratch() for _ in range(4)]
        LW = self.slots[sl[0][0]][:, 0:2048].rearrange("p (f t x) -> p f t x", f=4, t=4)
        sb_ = self.slots[sl[1][0]][:, :].rearrange("p (i q x) -> p i q x", i=4, q=32)
        Bb, Cc = (sb_[:, 0], sb_[:, 1]), (sb_[:, 2], sb_[:, 3])
        sc_ = self.slots[sl[2][0]]
        Br = [sc_[:, 1024 * i:1024 * i + 1024].rearrange("p (q x) -> p q x", q=32) for i in range(2)]
        Y = sc_[:, 2048:4096].rearrange("p (f n) -> p f n", f=8)
        V1 = self.slots[sl[3][0]][:, :].rearrange("p (i n) -> p i n", i=2)
        V = [V0, V1]
        WT = [self.slots[sl[0][0]][:, 2048:3072], self.slots[sl[0][0]][:, 3072:4096], sc_[:, 0:1024], sc_[:, 1024:2048]]
        fr = sl[0][1] + sl[1][1] + sl[2][1] + sl[3][1]
        U = self.H
        bd32 = self.c("bd32")
        V_, A_, g, h = self.dve, self.act, self.dve, self.pool
        power = lambda j: (aw[:, 0, j, :], aw[:, 1, j, :])
        dt, re, th, mag, c, s, k, r4, x, y, fre, fim = (sm[:, i, :] for i in range(12))
        ar, ai, ld = (ldt[:, i, :] for i in range(3))
        v3 = lambda z: z.rearrange("p (q n) -> p q n", q=16)
        temps = [(z[:, 1024 * i:1024 * i + 512], z[:, 1024 * i + 512:1024 * i + 1024]) for z in (T1, T2) for i in range(2)]
        f4 = lambda z: z.rearrange("p (f j x) -> p j f x", j=4, f=4)
        a4 = lambda z, fh: z[:, 16 * fh:16 * fh + 16].rearrange("p (j f) -> p j f", j=4).unsqueeze(3).broadcast_to([128, 4, 4, 32])
        c4 = lambda z, fh: z[:, 16 * fh:16 * fh + 16, :].rearrange("p (j f) x -> p j f x", j=4)
        bc = lambda q, n=32: q.unsqueeze(2).broadcast_to([128, q.shape[1], n])
        S = {"W": [], "CA": [], "LW": [], "V": [[], []], "tr": []}

        def prepare(d):
            free = fr + self.phase if d == 0 else S["l"] + [S["ca"], S["x"]]
            self.sp.dma(ldt, io["s5v"][d].rearrange("i p q -> p i q"), self.s_ld, free)
            self.sp.dma(sb_[:, 2:4], io["s5m"][d][2:4].rearrange("i p q x -> p i q x"), self.s_ld, free)
            for i in range(2):
                self.sp.dma(Br[i], io["s5m"][d][i], self.s_ld, free)
            self.n_ld += 64
            tl = [(self.s_ld, self.n_ld)]
            t = A_.act(dt, ld, ACT.Exp, after=tl + free)
            t1 = V_.mul(re, dt, ar, after=[t])
            t = V_.mul(th, dt, ai, after=[t])
            tm = A_.act(mag, re, ACT.Exp, after=[t1])
            t4 = A_.act(r4, re, ACT.Exp, scale=4.0, after=[t1])
            t = V_.ts(k, th, float(np.float32(1 / (2 * math.pi))), ALU.mult, after=[t])
            t = V_.ts(k, k, 12582912.0, ALU.add, after=[t])
            t = V_.ts(k, k, -12582912.0, ALU.add, after=[t])
            for part in (6.28125, 0.0019350051879882812, 3.0199159819e-07):
                t = V_.stt(th, k, -part, th, ALU.mult, ALU.add, after=[t])
            t = V_.ts(th, th, 3.1415925, ALU.min, -3.1415925, ALU.max, after=[t])
            ts = A_.act(s, th, ACT.Sin, after=[t])
            t = A_.act(x, th, ACT.Abs, after=[t])
            t = V_.ts(x, x, -1.0, ALU.mult, float(np.float32(math.pi / 2)), ALU.add, after=[t])
            tc = A_.act(c, x, ACT.Sin, after=[t])
            V_.do(lambda e: e.memset(aw[:, 0, 0, :], 1.0))
            t0 = V_.zero(aw[:, 1, 0, :])
            V_.mul(aw[:, 0, 1, :], mag, c, after=[tm, tc])
            t = V_.mul(aw[:, 1, 1, :], mag, s, after=[tm, ts])
            for j in range(2, 5):
                t = self.cmul(power(j), power(1), power(j - 1), x, y, [t])
            S["pw"] = [t, t0]
            t = V_.ts(x, aw[:, 0, 1, :], -1.0, ALU.add, after=[t])
            ta = V_.mul(fre, x, ar, after=[t])
            tb = V_.mul(y, aw[:, 1, 1, :], ai, after=[t])
            tr = V_.add(fre, fre, y, after=[ta, tb])
            ta = V_.mul(fim, aw[:, 1, 1, :], ar, after=[tr])
            tb = V_.mul(x, x, ai, after=[tr])
            ti = V_.sub(fim, fim, x, after=[ta, tb])
            ta = V_.mul(x, ar, ar, after=[ti])
            tb = V_.mul(y, ai, ai, after=[ti])
            t = V_.add(x, x, y, after=[ta, tb])
            t = V_.do(lambda e: e.reciprocal(x, x), [t])
            ta = V_.mul(fre, fre, x, after=[t])
            tb = V_.mul(fim, fim, x, after=[t])
            b1, b2 = (z[:, 0:1024].rearrange("p (q x) -> p q x", q=32) for z in (T1, T2))
            tB = self.cmul(Bb, (bc(fre), bc(fim)), Br, b1, b2, [ta, tb] + tl)
            tC = V_.ts(Cc[1], Cc[1], -1.0, ALU.mult, after=tl)
            S["B"], S["C"], S["tr"] = [tB], [tC], [tB]
            t = self.cmul((x, y), (c, s), (c, s), k, th, [tb, ts, tc, tB])
            t = self.cmul((c, s), (x, y), (x, y), k, th, [t])
            S["ph"], S["r4"] = [t], t4

        def phases(u):
            fh = u % 2
            hq = lambda z: z[:, 16 * fh:16 * fh + 16]
            P3 = (v3(P[:, 0, :]), v3(P[:, 1, :]))
            V_.do(lambda e: e.memset(P3[0][:, :, 0:1], 1.0), S["tr"])
            t = [V_.zero(P3[1][:, :, 0:1])] + S["ph"] + S["tr"]
            b1, b2 = v3(T1), v3(T2)
            cur, nxt, alt = (hq(c), hq(s)), (hq(x), hq(y)), (hq(fre), hq(fim))
            for lv in range(7):
                n = 1 << lv
                o = tuple(q[:, :, n:2 * n] for q in P3)
                a = tuple(q[:, :, 0:n] for q in P3)
                t = [self.cmul(o, (bc(cur[0], n), bc(cur[1], n)), a, b1[:, :, 0:n], b2[:, :, 0:n], t)]
                if lv < 6:
                    t = [self.cmul(nxt, cur, cur, hq(k), hq(th), t)]
                    cur, nxt = nxt, (alt if lv == 0 else cur)
            S["P"] = t

        def weights(u):
            fh = u % 2
            S["WT"] = []
            for s_ in range(4):
                pw, tp = power(3 - s_), temps[s_]
                S["WT"].append(self.cmul((f4(WT[s_][:, 0:512]), f4(WT[s_][:, 512:1024])), (a4(pw[0], fh), a4(pw[1], fh)),
                                         (c4(Bb[0], fh), c4(Bb[1], fh)), f4(tp[0]), f4(tp[1]),
                                         S["B"] + S["pw"] + S["tr"] + S["scan"] + S["temps"]))

        def inputs(u):
            d, fh = divmod(u, 2)
            for s_ in range(4):
                for i in range(2):
                    bi, ps, rd = self.bank(0, 4)
                    for f in range(4):
                        lh = WT[s_][:, 512 * i + 128 * f:512 * i + 128 * f + 128]
                        tm = self.pe.mm(ps[:, 128 * f:128 * f + 128], lh, self.c("ident"), True, True,
                                        after=[S["WT"][s_]] + rd, mark=(f == 3))
                    te = A_.copy(Wb[:, :, s_, i, :], ps[:, :].rearrange("p (f x) -> p f x", f=4), after=[tm] + S["W"])
                    self.drained[bi] = [te]
            S["tr"] = [tm]
            tv = []
            for j in range(4):
                for i in range(2):
                    bi, ps, rd = self.bank(0, 4)
                    for f in range(4):
                        for s_ in range(4):
                            v = U[32 * j:32 * j + 32, 4 * fh + f, :]
                            o = ps[:, 128 * f:128 * f + 128]
                            if d == 0:
                                v = v.rearrange("p (n s) -> p n s", s=4)[:, :, s_]
                            else:
                                v = v.rearrange("p (g n) -> p g n", g=2)[:, :, 255 - s_::-4]
                                o = o.rearrange("p (g n) -> p g n", g=2)
                            tm = self.pe.mm(o, Wb[32 * j:32 * j + 32, f, s_, i, :], v, s_ == 0, s_ == 3,
                                            after=[te] + rd, mark=(f == 3 and s_ == 3))
                    t = A_.copy(V[u % 2][:, i, 512 * j:512 * j + 512], ps[:, :], after=[tm] + S["V"][u % 2])
                    self.drained[bi] = [t]
                    tv.append(t)
            S["W"] = [tm]
            S["in", u] = tv

        def scan(u):
            fh = u % 2
            pr, pi = P[:, 0, :], P[:, 1, :]
            Vr, Vi = V[u % 2][:, 0, :], V[u % 2][:, 1, :]
            al = S["in", u] + S["P"] + S["WT"][-1:] + S["temps"]
            x1 = g.mul(T1, pr, Vr, after=al)
            x2 = h.mul(T2, pi, Vi, after=al)
            y1 = g.add(T1, T1, T2, after=[x1, x2])
            x4 = h.mul(Vr, pi, Vr, after=[x1])
            x3 = g.mul(T2, pr, Vi, after=[y1])
            y2 = g.sub(T2, T2, Vr, after=[x3, x4])
            tr_ = g.copy(v3(Vi), bc(r4[:, 16 * fh:16 * fh + 16], 128), after=[x2, x3, S["r4"]])
            tr_ = g.zero(v3(Vi)[:, :, 0:1], after=[tr_])
            z1 = g.do(lambda e: e.tensor_tensor_scan(Vr, Vi, T1, 0.0, ALU.mult, ALU.add), [tr_, y1, y2])
            z2 = g.do(lambda e: e.tensor_tensor_scan(T1, Vi, T2, 0.0, ALU.mult, ALU.add), [z1, y2])
            x1 = h.mul(T2, pi, T1, after=[z2])
            x2 = g.mul(Vi, pr, Vr, after=[z2])
            x4 = h.mul(Vr, pi, Vr, after=[x2])
            y1 = g.sub(Vi, Vi, T2, after=[x1, x2])
            x3 = g.mul(T2, pr, T1, after=[y1])
            S["x"] = g.add(Vr, Vr, T2, after=[x3, x4])
            S["scan"] = [S["x"]]

        def readouts(u):
            fh = u % 2
            for k_ in range(5):
                pw, tp = power(k_), temps[k_ % 4]
                t = self.cmul((CA[0][:, k_], CA[1][:, k_]), (a4(pw[0], fh), a4(pw[1], fh)), (c4(Cc[0], fh), c4(Cc[1], fh)),
                              f4(tp[0]), f4(tp[1]), S["C"] + S["pw"] + S["CA"] + S["scan"] + S["WT"][-1:] + S["P"] + ([tk] if k_ == 4 else []), sign=-1)
                if k_ == 0:
                    tk = t
            S["temps"], S["ca"] = [t], t

        def response(u):
            fh = u % 2
            S["l"] = []
            for f in range(4):
                bi, ps, rd = self.bank(4, 8)
                for j in range(4):
                    for i in range(2):
                        tm = self.pe.mm(ps[32 * j:32 * j + 32, 0:128].rearrange("p (t x) -> p t x", x=32),
                                        Bb[i][:, 16 * fh + 4 * j + f, :], CA[i][:, 0:4, j, f, :], i == 0, i == 1,
                                        after=[S["ca"]] + S["B"] + rd, mark=(j == 3 and i == 1))
                src = ps[:, 0:128].rearrange("p (t x) -> p t x", x=32).unsqueeze(2).broadcast_to([128, 4, 4, 32])
                mk = bd32.rearrange("p (j x) -> p j x", j=4).unsqueeze(1).broadcast_to([128, 4, 4, 32])
                S["l"].append(g.mul(LW[:, f].rearrange("p t (j x) -> p t j x", j=4), src, mk, after=[tm] + S["LW"]))
                self.drained[bi] = [S["l"][-1]]

        def outputs(u):
            d, fh = divmod(u, 2)
            XX = [v3(V[u % 2][:, 1, :]), v3(V[u % 2][:, 0, :])]
            S["o"] = []
            for f in range(4):
                F_ = 4 * fh + f
                bi, ps, rd = self.bank(4, 8)
                lat = U[:, F_, TC:T] if d == 0 else U[:, F_, T - 1:TC - 1:-1]
                lat = lat.rearrange("p (n s) -> p s n", s=4)
                o = ps[:, 0:256].rearrange("p (s n) -> p s n", s=4)
                for tau in range(4):
                    self.pe.mm(o[:, tau:4, :], LW[:, f, tau, :], lat[:, 0:4 - tau, :], tau == 0, False,
                               after=[S["l"][f]] + rd)
                for j in range(4):
                    q = 4 * j + f
                    for s_ in range(4):
                        for i in range(2):
                            tm = self.pe.mm(o[32 * j:32 * j + 32, s_, :], CA[i][:, s_ + 1, j, f, :],
                                            XX[i][:, q, 63:127], False, s_ == 3 and i == 1, after=[S["x"]],
                                            mark=(j == 3 and s_ == 3 and i == 1))
                S["o"].append((bi, o, tm))
            S["CA"] = S["LW"] = S["V"][u % 2] = [tm]

        def collect(u, outs):
            d, fh = divmod(u, 2)
            for f, (bi, o, tm) in enumerate(outs):
                yf = Y[:, 4 * fh + f, :]
                if d == 0:
                    ty = g.copy(yf.rearrange("p (n s) -> p s n", s=4), o, after=[tm] + fr)
                else:
                    yv = yf[:, 255::-1].rearrange("p (n s) -> p s n", s=4)
                    ty = g.add(yv, o, yv, after=[tm])
                self.drained[bi] = [ty]

        S["scan"], S["temps"] = [], []
        for d in range(2):
            u = 2 * d
            prepare(d)
            weights(u)
            inputs(u)
            phases(u)
            S["scan"] = S["P"]
            if d:
                collect(1, o1)
            weights(u + 1)
            readouts(u)
            inputs(u + 1)
            scan(u)
            phases(u + 1)
            response(u)
            outputs(u)
            o0 = S["o"]
            scan(u + 1)
            collect(u, o0)
            readouts(u + 1)
            response(u + 1)
            outputs(u + 1)
            o1 = S["o"]
        collect(3, o1)
        self.fence_keep()
        self.at = 0
        G = self.alloc(KT, TC)
        O = self.alloc(KT, TC)
        sgm = [self.alloc(TC), self.alloc(TC)]
        tg = []
        for f in range(8):
            t = self.dve.stt(Y[:, f, :], U[:, f, TC:T], self.v("s5d", f), Y[:, f, :], ALU.mult, ALU.add)
            tg.append(self.act.act(G[:, f, :], Y[:, f, :], ACT.Gelu_apprx_tanh, after=[t]))
        for i, _ in sl:
            self.ring.free(i, tg[-1])
        sfree = [[], []]
        ys = []
        for g_ in range(4):
            view = lambda s: s[:, :].rearrange("p (u k n) -> p u k n", u=2, k=KT)
            Wg = io["s5_w_glu_2"][0]
            s, tok = self.ring.load(*[
                (lambda s, a=a: view(s)[:, a], Wg[:, D * a + 256 * g_:D * a + 256 * g_ + 256].rearrange("(k p) n -> p k n", p=128))
                for a in range(2)])
            w = view(self.slots[s])
            for m in range(2):
                xx = 2 * g_ + m

                def zb(ps, t, xx=xx):
                    t = self.act.act(sgm[xx % 2], ps, ACT.Sigmoid, after=[t] + sfree[xx % 2])
                    sfree[xx % 2] = [t]
                    return t

                def za(ps, t, xx=xx):
                    t = self.dve.mul(O[:, xx, :], ps, sgm[xx % 2], after=[t] + sfree[xx % 2])
                    sfree[xx % 2] = [t]
                    ys.append(t)
                    return t

                rh = lambda k: G[:, k, :]
                self.fm(w[:, 1], 128 * m, 128, TC, zb, [tok, tg[-1]], 0, 6, rhs=rh)
                tm = self.fm(w[:, 0], 128 * m, 128, TC, za, [tok, tg[-1]], 0, 6, rhs=rh)
            self.ring.free(s, tm)
        if self.stop == "s5mix":
            for f in range(8):
                self.dve.copy(self.H[:, f, TC:T], O[:, f, :], after=ys)
            return
        self.resid(O, TC, 1, False, ys)


def constants():
    c = np.zeros((128, NCST), np.float32)

    def put(name, a, rows=128):
        at, n = CST[name]
        c[:rows, at:at + a.shape[1]] = a

    p = np.arange(128)
    x = np.arange(512)
    put("ident", np.eye(128, dtype=np.float32))
    put("ones", np.ones((128, 128), np.float32))
    put("bd", (p[:, None] // 64 == p[None, :] // 64).astype(np.float32))
    put("bd32", (p[:, None] // 32 == p[None, :] // 32).astype(np.float32))
    r = np.zeros((128, 128), np.float32)
    r[p[1::2], p[0::2]] = -1
    r[p[0::2], p[1::2]] = 1
    put("rotE", r)
    r = np.zeros((128, 128), np.float32)
    a = 64 + np.arange(16)
    r[a + 16, a] = -1
    r[a, a + 16] = 1
    put("rotM", r)
    r = np.zeros((128, 128), np.float32)
    a = np.concatenate([np.arange(32), 64 + np.arange(32)])
    r[a + 32, a] = -1
    r[a, a + 32] = 1
    put("rotR", r)
    m = np.ones((128, 516), np.float32)
    m[:, ::129] = 0
    put("smask", m)
    put("distF", np.maximum(x[None] - p[:, None], 0).astype(np.float32))
    put("distR", np.maximum(128 * (x[None] // 128) + p[:, None] - x[None] % 128, 0).astype(np.float32))
    put("mF", (p[None] >= p[:, None]).astype(np.float32))
    put("mR", (p[:, None] > p[None]).astype(np.float32))
    f4 = np.float32
    n = np.arange(256)
    row, col = (n // 64).astype(f4), (n % 64).astype(f4)
    inv = (f4(10000.0) ** (-np.arange(0, 32, 2, dtype=f4) / f4(32))).astype(f4)
    ang = np.concatenate([row[:, None] * inv, col[:, None] * inv], -1).astype(f4)
    fe = (p % 64) // 2
    put("cosE", np.cos(ang)[:, fe].T.astype(f4))
    put("sinE", np.sin(ang)[:, fe].T.astype(f4))
    f = (f4(10000.0) ** (-np.arange(8, dtype=f4) / f4(8))).astype(f4)
    ang = np.concatenate([row[:, None] * f, col[:, None] * f], -1).astype(f4)
    co, si = np.ones((128, 256), f4), np.zeros((128, 256), f4)
    for half in range(2):
        co[64 + 16 * half:80 + 16 * half] = np.cos(ang).T
        si[64 + 16 * half:80 + 16 * half] = np.sin(ang).T
    put("cosM", co)
    put("sinM", si)
    th = (f4(10000.0) ** (-np.arange(32, dtype=f4) / f4(32))).astype(f4)
    ang = (n.astype(f4)[:, None] * th).astype(f4)
    put("cosR", np.cos(ang)[:, p % 32].T.astype(f4))
    put("sinR", np.sin(ang)[:, p % 32].T.astype(f4))
    k = np.zeros((128, 15, 128), np.float32)
    for li, L in enumerate(LEVELS):
        same = p[:, None] // (2 * L) == p[None] // (2 * L)
        late = (p // L) % 2 == 1
        k[:, li] = same & ~late[:, None] & late[None]
        k[:, 7 + li] = same & late[:, None] & ~late[None]
    k[:, 14] = np.eye(128)
    return c, k


def layouts(a):
    f = lambda x: np.ascontiguousarray(x)
    vec = np.zeros((128, NVEC), np.float32)

    def put(name, x, rows=128):
        at, n = VEC[name]
        assert x.shape == (rows, n), (name, x.shape)
        vec[:rows, at:at + n] = x

    col = lambda x: np.asarray(x).reshape(-1, 128).T
    put("c", col(a["c"]))
    put("cc", col(a["c_ctx"]))
    put("c2", col(a["c_2"]))
    put("cc2", col(a["c_ctx_2"]))
    put("mod_b", col(a["mod_b"]))
    put("ada_b", col(a["ada_b_2"]))
    for n, m in (("pre_mix", "norm_pre_mix"), ("post_mix", "norm_post_mix"), ("pre_ffn", "norm_pre_ffn"),
                 ("post_ffn", "norm_post_ffn"), ("n1", "norm1_g_2"), ("n2", "norm2_g_2"), ("gla_b", "gla_b_gate"),
                 ("gla_n", "gla_out_norm"), ("lb", "hgrn_lower_bounds"), ("hg_n", "hgrn_out_norm"),
                 ("mq_n", "mla_q_norm_g_2"), ("mkv_n", "mla_kv_norm_g_2"), ("s5d", "s5_d_2")):
        put(n, col(a[m]))
    put("aq_n", np.tile(np.asarray(a["att_q_norm"]).reshape(64, 1), (2, 1)))
    put("ak_n", np.tile(np.asarray(a["att_k_norm"]).reshape(64, 1), (2, 1)))
    put("mqn", np.asarray(a["mla_qn_g_2"]).reshape(96, 1), 96)
    put("mkn", np.asarray(a["mla_kn_g_2"]).reshape(96, 1), 96)
    put("lgf", np.tile(np.asarray(a["ret_lg_f_2"]).reshape(1, 8), (128, 1)))
    put("lgb", np.tile(np.asarray(a["ret_lg_b_2"]).reshape(1, 8), (128, 1)))
    put("eps", np.full((128, 1), EPS, np.float32))
    put("one", np.ones((128, 1), np.float32))
    gw = np.zeros((32, 2, 256), np.float32)
    for d in range(2):
        gw[16 * d:16 * d + 16, d] = np.asarray(a["gla_w_gate"])[0, d]
    fm = lambda x: np.asarray(x).reshape(-1, 8, 128).transpose(2, 1, 0)
    xT = np.concatenate([fm(a["ctx"]), fm(a["x"])], 2)
    cst, msk = constants()
    out = {"vec": vec, "cst": cst, "msk": msk, "xT": f(xT), "x2T": f(fm(a["ctx_2"])), "gla_gw": gw.reshape(32, 512)}
    g = np.array([[8 * (4 * r + ff) + 2 * j + h for h in range(2)] for r in range(2) for j in range(4) for ff in range(4)])
    s5v = np.zeros((2, 3, 128, 32), np.float32)
    s5m = np.zeros((2, 4, 128, 32, 32), np.float32)
    for i, d in enumerate("fb"):
        for n, name in enumerate(("s5_a_re_", "s5_a_im_")):
            x = np.asarray(a[name + d + "_2"])[0]
            s5v[i, n] = x[g].transpose(1, 2, 0).reshape(128, 32)
        s5v[i, 2] = np.repeat(np.asarray(a["s5_log_dt_" + d + "_2"])[0][g].T, 64, 0)
        for n, name in enumerate(("s5_b_re_", "s5_b_im_", "s5_c_re_", "s5_c_im_")):
            x = np.asarray(a[name + d + "_2"])[0][g]
            if n >= 2:
                x = x.transpose(0, 1, 3, 2)
            for h in range(2):
                s5m[i, n, 64 * h:64 * h + 64, :, 16 * h:16 * h + 16] = x[:, h].transpose(1, 0, 2)
    out["s5v"], out["s5m"] = s5v, s5m
    for name in WEIGHTS:
        out[name] = f(np.asarray(a[name]))
    return out


WEIGHTS = ("mod_w", "even_w_in", "even_w_out", "odd_w_in", "odd_w_out", "ffn_w_gate", "ffn_w_up", "ffn_w_down",
           "ada_w_2", "mlp_w1_2", "mlp_w2_2", "w_in_2", "mla_w_uq_2", "mla_w_ukv_2", "w_out_2", "s5_w_glu_2")


def build(nc, shapes, stop=None):
    io = {}
    for name, (shape, dt) in shapes.items():
        io[name] = nc.dram_tensor(name, shape, dt, kind="ExternalInput").ap()
    n = T if stop else TC
    io["outX"] = nc.dram_tensor("outX", (128, KT, n), F32, kind="ExternalOutput").ap()
    with ExitStack() as ctx:
        p = Program(nc, ctx, io, stop)
        run_program(p, stop)


def run_program(p, stop):
    io = p.io
    first = ("pre_mix", "post_mix", "pre_ffn", "post_ffn")
    second = ("n1", None, "n2", None)
    mods = [p.mods_steps(0, io["mod_w"], "mod_b", 0, 0, *first), p.mods_steps(1, io["mod_w"], "mod_b", 0, 1, *first),
            p.mods_steps(2, io["ada_w_2"], "ada_b", 1, 0, *second), p.mods_steps(3, io["ada_w_2"], "ada_b", 1, 1, *second)]
    at = [0]

    def next_mods():
        at[0] += 1
        return mods[at[0]]

    p.next_mods = next_mods
    steps = [
        ("even", lambda: (p.begin(), p.together(mods[0]), p.use(0), p.even())),
        ("ffn0", lambda: p.ffn_swiglu(0, 0)),
        ("odd", lambda: (p.use(1), p.odd())),
        ("ffn1", lambda: p.ffn_swiglu(1, TC)),
        ("mla", lambda: (p.use(2), p.mla())),
        ("mlp0", lambda: p.ffn_sq(0, 0)),
        ("s5", lambda: (p.use(3), p.s5())),
        ("mlp1", lambda: p.ffn_sq(1, TC)),
    ]
    for name, f in steps:
        f()
        if stop and name == stop.replace("mix", ""):
            break
    p.finish()


def kernel(**inputs):
    import concourse.bacc as bacc
    from concourse.bass_utils import run_bass_kernel_spmd

    arrays = layouts(inputs)
    nc = bacc.Bacc("TRN2", target_bir_lowering=False, num_devices=1)
    build(nc, {n: (x.shape, mybir.dt.from_np(x.dtype)) for n, x in arrays.items()})
    r = run_bass_kernel_spmd(nc, [arrays], core_ids=[0])
    out = r.results[0]["outX"]
    return np.ascontiguousarray(out.transpose(2, 1, 0).reshape(1, TC, D))
```
